# Optimizing a Trainium2 kernel written in Bass

```python
import math
import jax, jax.numpy as jnp
from jax import lax
import numpy as np

D_MODEL = 1024
BATCH = 1
SEQ = 512
DEPTH = 1

PLE_DIM = 256
HEAD_DIM = 64
A_Q_HEADS = 8
A_KV_HEADS = 2
A_GROUP = A_Q_HEADS // A_KV_HEADS
A_WINDOW = 128
B_HEADS = 8
B_PATTERNS = ((128, 1), (512, 4), (2048, 16))
N_HEADS_TOTAL = A_Q_HEADS + B_HEADS
A_Q = A_Q_HEADS * HEAD_DIM
A_KV = A_KV_HEADS * HEAD_DIM
B_W = B_HEADS * HEAD_DIM
D_IN = A_Q + 2 * A_KV + 3 * B_W
D_MIX = A_Q + B_W
D_FF = 2816
NUM_BUCKETS = 32
MAX_DISTANCE = 2048
BLOCK = 128
EPS = 1e-6
NEG_INF = -1e30


def rms_norm(x, g):
    xf = x.astype(jnp.float32)
    y = xf * lax.rsqrt(jnp.mean(xf * xf, axis=-1, keepdims=True) + EPS)
    return (y * g.astype(jnp.float32)).astype(x.dtype)

def swiglu(x, w_gu, w_down):
    g, u = jnp.split(x @ w_gu, 2, axis=-1)
    return (jax.nn.silu(g) * u) @ w_down

def t5_bucket(dist):
    max_exact = NUM_BUCKETS // 2
    n = jnp.maximum(dist, 0)
    nf = jnp.maximum(n, 1).astype(jnp.float32)
    large = max_exact + (jnp.log(nf / max_exact) / math.log(MAX_DISTANCE / max_exact)
                         * (NUM_BUCKETS - max_exact)).astype(jnp.int32)
    large = jnp.minimum(large, NUM_BUCKETS - 1)
    return jnp.where(n < max_exact, n, large)

def banded_attention(q, k, v, rel_bias, max_dist, stride):
    n, L, hkv, grp, dh = q.shape
    bq = math.gcd(L, BLOCK)
    nb = L // bq
    nk = bq + max_dist
    pad = ((0, 0), (max_dist, 0), (0, 0), (0, 0))
    k_pad = jnp.pad(k, pad)
    v_pad = jnp.pad(v, pad)
    key_idx = jnp.arange(nb)[:, None] * bq + jnp.arange(nk)[None, :]
    kb = k_pad[:, key_idx]
    vb = v_pad[:, key_idx]
    qb = q.reshape(n, nb, bq, hkv, grp, dh)
    logits = jnp.einsum('nbqhgd,nbkhd->nbhgqk', qb, kb,
                        preferred_element_type=jnp.float32) * (dh ** -0.5)
    rel = jnp.arange(bq)[:, None] + max_dist - jnp.arange(nk)[None, :]
    bias = rel_bias[t5_bucket(rel * stride)].astype(jnp.float32)
    bias = bias.reshape(bq, nk, hkv, grp).transpose(2, 3, 0, 1)
    in_band = (rel >= 0) & (rel <= max_dist)
    key_pos = key_idx - max_dist
    valid = in_band[None] & (key_pos >= 0)[:, None, :]
    logits = jnp.where(valid[None, :, None, None], logits + bias, NEG_INF)
    m = jnp.max(logits, axis=-1)
    pr = jnp.exp(logits - m[..., None])
    s = jnp.sum(pr, axis=-1)
    o = jnp.einsum('nbhgqk,nbkhd->nbqhgd', pr, vb.astype(jnp.float32))
    o = o.reshape(n, L, hkv, grp, dh)
    m = m.transpose(0, 1, 4, 2, 3).reshape(n, L, hkv, grp)
    s = s.transpose(0, 1, 4, 2, 3).reshape(n, L, hkv, grp)
    return o, m, s

def to_classes(t, r):
    b, s = t.shape[:2]
    rest = t.shape[2:]
    t = jnp.moveaxis(t.reshape((b, s // r, r) + rest), 2, 1)
    return t.reshape((b * r, s // r) + rest)

def from_classes(t, b, r):
    n, L = t.shape[:2]
    rest = t.shape[2:]
    t = jnp.moveaxis(t.reshape((b, r, L) + rest), 1, 2)
    return t.reshape((b, L * r) + rest)

def sink_swa_gqa(q_a, k_a, v_a, sinks, rel_bias_a):
    b, s, _ = q_a.shape
    q = q_a.reshape(b, s, A_KV_HEADS, A_GROUP, HEAD_DIM)
    k = k_a.reshape(b, s, A_KV_HEADS, HEAD_DIM)
    v = v_a.reshape(b, s, A_KV_HEADS, HEAD_DIM)
    o, m, den = banded_attention(q, k, v, rel_bias_a, A_WINDOW - 1, 1)
    sink = sinks.reshape(A_KV_HEADS, A_GROUP).astype(jnp.float32)
    m_all = jnp.maximum(m, sink)
    scale = jnp.exp(m - m_all)
    total = den * scale + jnp.exp(sink - m_all)
    o = o * (scale / total)[..., None]
    return o.reshape(b, s, A_Q)

def dilated_mixture(q_b, k_b, v_b, rel_bias_b):
    b, s, _ = q_b.shape
    q = q_b.reshape(b, s, B_HEADS, 1, HEAD_DIM)
    k = k_b.reshape(b, s, B_HEADS, HEAD_DIM)
    v = v_b.reshape(b, s, B_HEADS, HEAD_DIM)
    outs, maxes, dens = [], [], []
    for window, dil in B_PATTERNS:
        o, m, den = banded_attention(to_classes(q, dil), to_classes(k, dil), to_classes(v, dil),
                                     rel_bias_b, window // dil, dil)
        outs.append(from_classes(o, b, dil))
        maxes.append(from_classes(m, b, dil))
        dens.append(from_classes(den, b, dil))
    m_stack = jnp.stack(maxes)
    m_all = jnp.max(m_stack, axis=0)
    w = jnp.exp(m_stack - m_all)
    num = jnp.sum(w[..., None] * jnp.stack(outs), axis=0)
    den_all = jnp.sum(w * jnp.stack(dens), axis=0)
    return (num / den_all[..., None]).reshape(b, s, B_W)

def first_inputs(seed: int = 0) -> dict:
    key = jax.random.key(seed)
    ks = jax.random.split(key, 24)
    f32 = jnp.float32

    def w(k, shape, fan_in):
        return jax.random.normal(k, shape, f32) * (fan_in ** -0.5)

    def gain(k, shape):
        return 1.0 + 0.05 * jax.random.normal(k, shape, f32)

    def small(k, shape, scale=0.02):
        return scale * jax.random.normal(k, shape, f32)

    D = D_MODEL
    return {
        "x": jax.random.normal(ks[0], (BATCH, SEQ, D), f32),
        "p": jax.random.normal(ks[1], (DEPTH, BATCH, SEQ, PLE_DIM), f32),
        "rel_bias": small(ks[2], (NUM_BUCKETS, N_HEADS_TOTAL), 0.5),
        "ffn1_pre_g": gain(ks[3], (DEPTH, D)),
        "ffn1_w_gu": w(ks[4], (DEPTH, D, 2 * D_FF), D),
        "ffn1_w_down": w(ks[5], (DEPTH, D_FF, D), D_FF),
        "ffn1_post_g": gain(ks[6], (DEPTH, D)),
        "attn_pre_g": gain(ks[7], (DEPTH, D)),
        "w_in": w(ks[8], (DEPTH, D, D_IN), D),
        "b_in": small(ks[9], (DEPTH, D_IN)),
        "sinks": small(ks[10], (DEPTH, A_Q_HEADS), 0.5),
        "w_out": w(ks[11], (DEPTH, D_MIX, D), D_MIX),
        "b_out": small(ks[12], (DEPTH, D)),
        "attn_post_g": gain(ks[13], (DEPTH, D)),
        "ffn2_pre_g": gain(ks[14], (DEPTH, D)),
        "ffn2_w_gu": w(ks[15], (DEPTH, D, 2 * D_FF), D),
        "ffn2_w_down": w(ks[16], (DEPTH, D_FF, D), D_FF),
        "ffn2_post_g": gain(ks[17], (DEPTH, D)),
        "ple_pre_g": gain(ks[18], (DEPTH, D)),
        "w_ple_gate": w(ks[19], (DEPTH, D, D), D),
        "w_ple_proj": w(ks[20], (DEPTH, PLE_DIM, D), PLE_DIM),
        "ple_post_g": gain(ks[21], (DEPTH, D)),
    }

def first_block(x, p, rel_bias, ffn1_pre_g, ffn1_w_gu, ffn1_w_down, ffn1_post_g,
              attn_pre_g, w_in, b_in, sinks, w_out, b_out, attn_post_g,
              ffn2_pre_g, ffn2_w_gu, ffn2_w_down, ffn2_post_g,
              ple_pre_g, w_ple_gate, w_ple_proj, ple_post_g):
    h = x
    splits = [A_Q, A_Q + A_KV, A_Q + 2 * A_KV, A_Q + 2 * A_KV + B_W, A_Q + 2 * A_KV + 2 * B_W]
    for i in range(DEPTH):
        f = swiglu(rms_norm(h, ffn1_pre_g[i]), ffn1_w_gu[i], ffn1_w_down[i])
        h = h + 0.5 * rms_norm(f, ffn1_post_g[i])

        z = rms_norm(h, attn_pre_g[i]) @ w_in[i] + b_in[i]
        q_a, k_a, v_a, q_b, k_b, v_b = jnp.split(z, splits, axis=-1)
        out_a = sink_swa_gqa(q_a, k_a, v_a, sinks[i], rel_bias[:, :A_Q_HEADS])
        out_b = dilated_mixture(q_b, k_b, v_b, rel_bias[:, A_Q_HEADS:])
        mix = jnp.concatenate([out_a, out_b], axis=-1).astype(x.dtype)
        att = mix @ w_out[i] + b_out[i]
        h = h + rms_norm(att, attn_post_g[i])

        f = swiglu(rms_norm(h, ffn2_pre_g[i]), ffn2_w_gu[i], ffn2_w_down[i])
        h = h + 0.5 * rms_norm(f, ffn2_post_g[i])

        gate = jax.nn.sigmoid(rms_norm(h, ple_pre_g[i]) @ w_ple_gate[i])
        e = p[i] @ w_ple_proj[i]
        h = h + rms_norm(gate * e, ple_post_g[i])
    return h


DEPTH_2 = 2

CTX_LEN = 256
GRID_W = 64

FOURIER_WIDTH = D_MODEL // 4
N_FOURIER_HEADS = 4
FOURIER_HEAD_DIM = FOURIER_WIDTH // N_FOURIER_HEADS

V_HEAD_DIM = 64
QK_NOPE_DIM = 64
QK_ROPE_DIM = 32
QK_HEAD_DIM = QK_NOPE_DIM + QK_ROPE_DIM
N_MLA_HEADS = (D_MODEL - FOURIER_WIDTH) // V_HEAD_DIM
MLA_WIDTH = N_MLA_HEADS * V_HEAD_DIM
Q_LORA_RANK = 384
KV_LORA_RANK = 128

MIX_WIDTH = FOURIER_WIDTH + MLA_WIDTH
IN_PROJ_WIDTH = FOURIER_WIDTH + Q_LORA_RANK + KV_LORA_RANK + QK_ROPE_DIM

CONV_WIDTH = 3

ROPE_THETA = 10000.0
NORM_EPS = 1e-6
Q_BLOCK = 128
SOFTMAX_SCALE = QK_HEAD_DIM ** -0.5
N_MOD = 6


def rms_norm_2(x, g):
    xf = x.astype(jnp.float32)
    y = xf * lax.rsqrt(jnp.mean(xf * xf, axis=-1, keepdims=True) + NORM_EPS)
    return (y * g.astype(jnp.float32)).astype(x.dtype)

def modulate(h, shift, scale):
    return h * (1 + scale) + shift

def axial_rope_tables(rows, dtype):
    row_ids = jnp.broadcast_to(jnp.arange(rows)[:, None], (rows, GRID_W)).reshape(-1).astype(jnp.float32)
    col_ids = jnp.broadcast_to(jnp.arange(GRID_W)[None, :], (rows, GRID_W)).reshape(-1).astype(jnp.float32)
    n_freq = QK_ROPE_DIM // 4
    inv_freq = ROPE_THETA ** (-jnp.arange(n_freq, dtype=jnp.float32) / n_freq)
    ang = jnp.concatenate([row_ids[:, None] * inv_freq, col_ids[:, None] * inv_freq], axis=-1)
    return jnp.cos(ang).astype(dtype), jnp.sin(ang).astype(dtype)

def apply_rope(x, cos, sin):
    x1, x2 = jnp.split(x, 2, axis=-1)
    return jnp.concatenate([x1 * cos - x2 * sin, x2 * cos + x1 * sin], axis=-1)

def fourier_mix(u, w_f, b_f):
    b, n, _ = u.shape
    uh = u.reshape(b, n, N_FOURIER_HEADS, FOURIER_HEAD_DIM).astype(jnp.float32)
    f = jnp.fft.fft2(uh, axes=(1, 3), norm="ortho").real
    f = f.reshape(b, n, FOURIER_WIDTH).astype(u.dtype)
    return f @ w_f + b_f

def mla_q(c_q, g_q, w_q_b, cos, sin):
    b, n, _ = c_q.shape
    q = (rms_norm_2(c_q, g_q) @ w_q_b).reshape(b, n, N_MLA_HEADS, QK_HEAD_DIM)
    q_nope, q_rope = q[..., :QK_NOPE_DIM], q[..., QK_NOPE_DIM:]
    if cos is not None:
        q_rope = apply_rope(q_rope, cos[:, None, :], sin[:, None, :])
    return q_nope, q_rope

def mla_kv(c_kv, k_rope, g_kv, w_kv_b, cos, sin):
    b, n, _ = c_kv.shape
    kv = (rms_norm_2(c_kv, g_kv) @ w_kv_b).reshape(b, n, N_MLA_HEADS, QK_NOPE_DIM + V_HEAD_DIM)
    k_nope, v = kv[..., :QK_NOPE_DIM], kv[..., QK_NOPE_DIM:]
    if cos is not None:
        k_rope = apply_rope(k_rope, cos, sin)
    return k_nope, k_rope, v

def mla_attend(q_nope, q_rope, k_nope, k_rope, v):
    s = jnp.einsum('bqhd,bkhd->bhqk', q_nope, k_nope) + jnp.einsum('bqhr,bkr->bhqk', q_rope, k_rope)
    p = jax.nn.softmax(s.astype(jnp.float32) * SOFTMAX_SCALE, axis=-1).astype(v.dtype)
    return jnp.einsum('bhqk,bkhd->bqhd', p, v)

def blocked_attention(q_nope, q_rope, k_nope, k_rope, v):
    b, n, h, _ = q_nope.shape
    nb = n // Q_BLOCK
    qn = q_nope.reshape(b, nb, Q_BLOCK, h, QK_NOPE_DIM).transpose(1, 0, 2, 3, 4)
    qr = q_rope.reshape(b, nb, Q_BLOCK, h, QK_ROPE_DIM).transpose(1, 0, 2, 3, 4)
    out = lax.map(lambda blk: mla_attend(blk[0], blk[1], k_nope, k_rope, v), (qn, qr))
    return out.transpose(1, 0, 2, 3, 4).reshape(b, n, h * V_HEAD_DIM)

def split_in_proj(p):
    f_in = p[..., :FOURIER_WIDTH]
    c_q = p[..., FOURIER_WIDTH:FOURIER_WIDTH + Q_LORA_RANK]
    c_kv = p[..., FOURIER_WIDTH + Q_LORA_RANK:FOURIER_WIDTH + Q_LORA_RANK + KV_LORA_RANK]
    k_rope = p[..., FOURIER_WIDTH + Q_LORA_RANK + KV_LORA_RANK:]
    return f_in, c_q, c_kv, k_rope

def conv_ffn(h, w_up, w_dw, b_dw, w_down):
    u = h @ w_up
    u = lax.conv_general_dilated(u, w_dw[:, None, :], window_strides=(1,),
                                 padding=((CONV_WIDTH // 2, CONV_WIDTH // 2),),
                                 dimension_numbers=('NWC', 'WIO', 'NWC'),
                                 feature_group_count=2 * D_FF) + b_dw
    gate, val = jnp.split(u, 2, axis=-1)
    return (jax.nn.silu(gate) * val) @ w_down

def second_inputs(seed: int = 0) -> dict:
    key = jax.random.key(seed)
    ks = jax.random.split(key, 24)
    f32 = jnp.float32

    def nrm(k, shape, scale):
        return jax.random.normal(k, shape, f32) * scale

    def gain(k, shape):
        return 1.0 + 0.02 * jax.random.normal(k, shape, f32)

    L, D = DEPTH_2, D_MODEL
    return {
        "x": jax.random.normal(ks[0], (BATCH, SEQ, D), f32),
        "c": jax.random.normal(ks[1], (BATCH, D), f32),
        "ctx": jax.random.normal(ks[2], (BATCH, CTX_LEN, D), f32),
        "c_ctx": jax.random.normal(ks[3], (D,), f32),
        "w_ada": nrm(ks[4], (L, D, N_MOD * D), 0.5 * D ** -0.5),
        "b_ada": nrm(ks[5], (L, N_MOD * D), 0.02),
        "g_mix": gain(ks[6], (L, D)),
        "w_in": nrm(ks[7], (L, D, IN_PROJ_WIDTH), D ** -0.5),
        "w_fourier": nrm(ks[8], (L, FOURIER_WIDTH, FOURIER_WIDTH), FOURIER_WIDTH ** -0.5),
        "b_fourier": nrm(ks[9], (L, FOURIER_WIDTH), 0.02),
        "g_q_a": gain(ks[10], (L, Q_LORA_RANK)),
        "w_q_b": nrm(ks[11], (L, Q_LORA_RANK, N_MLA_HEADS * QK_HEAD_DIM), Q_LORA_RANK ** -0.5),
        "g_kv_a": gain(ks[12], (L, KV_LORA_RANK)),
        "w_kv_b": nrm(ks[13], (L, KV_LORA_RANK, N_MLA_HEADS * (QK_NOPE_DIM + V_HEAD_DIM)), KV_LORA_RANK ** -0.5),
        "w_out": nrm(ks[14], (L, MIX_WIDTH, D), MIX_WIDTH ** -0.5),
        "g_ffn": gain(ks[15], (L, D)),
        "w_up": nrm(ks[16], (L, D, 2 * D_FF), D ** -0.5),
        "w_dw": nrm(ks[17], (L, CONV_WIDTH, 2 * D_FF), CONV_WIDTH ** -0.5),
        "b_dw": nrm(ks[18], (L, 2 * D_FF), 0.02),
        "w_down": nrm(ks[19], (L, D_FF, D), D_FF ** -0.5),
        "g_final": gain(ks[20], (D,)),
    }

def second_block(x, c, ctx, c_ctx, w_ada, b_ada, g_mix, w_in, w_fourier, b_fourier,
              g_q_a, w_q_b, g_kv_a, w_kv_b, w_out, g_ffn, w_up, w_dw, b_dw, w_down, g_final):
    b, n_lat, _ = x.shape
    ROWS = n_lat // GRID_W
    cos, sin = axial_rope_tables(ROWS, x.dtype)
    silu_c = jax.nn.silu(c)
    silu_cc = jax.nn.silu(c_ctx)

    for l in range(DEPTH_2):
        last = l == DEPTH_2 - 1
        mod_lat = (silu_c @ w_ada[l] + b_ada[l])[:, None, :]
        mod_ctx = silu_cc @ w_ada[l] + b_ada[l]
        sh1, sc1, gt1, sh2, sc2, gt2 = jnp.split(mod_lat, N_MOD, axis=-1)
        csh1, csc1, cgt1, csh2, csc2, cgt2 = jnp.split(mod_ctx, N_MOD, axis=-1)

        h = modulate(rms_norm_2(x, g_mix[l]), sh1, sc1)
        hc = modulate(rms_norm_2(ctx, g_mix[l]), csh1, csc1)
        f_in, c_q, c_kv, k_rope_raw = split_in_proj(h @ w_in[l])
        f_in_c, c_q_c, c_kv_c, k_rope_raw_c = split_in_proj(hc @ w_in[l])

        kn_c, kr_c, v_c = mla_kv(c_kv_c, k_rope_raw_c, g_kv_a[l], w_kv_b[l], None, None)
        kn_l, kr_l, v_l = mla_kv(c_kv, k_rope_raw, g_kv_a[l], w_kv_b[l], cos, sin)
        qn_l, qr_l = mla_q(c_q, g_q_a[l], w_q_b[l], cos, sin)

        k_nope_all = jnp.concatenate([kn_l, kn_c], axis=1)
        k_rope_all = jnp.concatenate([kr_l, kr_c], axis=1)
        v_all = jnp.concatenate([v_l, v_c], axis=1)
        att_l = blocked_attention(qn_l, qr_l, k_nope_all, k_rope_all, v_all)
        four_l = fourier_mix(f_in, w_fourier[l], b_fourier[l])
        mix_l = jnp.concatenate([four_l, att_l], axis=-1) @ w_out[l]
        x = x + gt1 * mix_l

        x = x + gt2 * conv_ffn(modulate(rms_norm_2(x, g_ffn[l]), sh2, sc2),
                               w_up[l], w_dw[l], b_dw[l], w_down[l])

        if not last:
            qn_c, qr_c = mla_q(c_q_c, g_q_a[l], w_q_b[l], None, None)
            att_c = mla_attend(qn_c, qr_c, kn_c, kr_c, v_c).reshape(b, -1, MLA_WIDTH)
            four_c = fourier_mix(f_in_c, w_fourier[l], b_fourier[l])
            mix_c = jnp.concatenate([four_c, att_c], axis=-1) @ w_out[l]
            ctx = ctx + cgt1 * mix_c
            ctx = ctx + cgt2 * conv_ffn(modulate(rms_norm_2(ctx, g_ffn[l]), csh2, csc2),
                                        w_up[l], w_dw[l], b_dw[l], w_down[l])

    return rms_norm_2(x, g_final)


def setup_inputs(seed=0):
    out = dict(first_inputs(seed))
    for name, value in second_inputs(seed + 1).items():
        if name != "x":
            out[name + "_2"] = value
    return out


def reference(
    x, p, rel_bias, ffn1_pre_g, ffn1_w_gu, ffn1_w_down, ffn1_post_g, attn_pre_g, w_in, b_in,
    sinks, w_out, b_out, attn_post_g, ffn2_pre_g, ffn2_w_gu, ffn2_w_down, ffn2_post_g,
    ple_pre_g, w_ple_gate, w_ple_proj, ple_post_g, c_2, ctx_2, c_ctx_2, w_ada_2, b_ada_2,
    g_mix_2, w_in_2, w_fourier_2, b_fourier_2, g_q_a_2, w_q_b_2, g_kv_a_2, w_kv_b_2, w_out_2,
    g_ffn_2, w_up_2, w_dw_2, b_dw_2, w_down_2, g_final_2,
):
    x = first_block(
        x, p, rel_bias, ffn1_pre_g, ffn1_w_gu, ffn1_w_down, ffn1_post_g, attn_pre_g, w_in, b_in,
        sinks, w_out, b_out, attn_post_g, ffn2_pre_g, ffn2_w_gu, ffn2_w_down, ffn2_post_g,
        ple_pre_g, w_ple_gate, w_ple_proj, ple_post_g,
    )
    return second_block(
        x, c_2, ctx_2, c_ctx_2, w_ada_2, b_ada_2, g_mix_2, w_in_2, w_fourier_2, b_fourier_2,
        g_q_a_2, w_q_b_2, g_kv_a_2, w_kv_b_2, w_out_2, g_ffn_2, w_up_2, w_dw_2, b_dw_2,
        w_down_2, g_final_2,
    )


_drawn_inputs = setup_inputs


def setup_inputs(seed=0):
    import zlib

    import numpy as np

    out = dict(_drawn_inputs(seed))
    spreads = {}
    factors = {'sinks': 8.0,
     'ffn2_pre_g': 2.878,
     'ffn2_post_g': 4.119,
     'ple_pre_g': 5.462,
     'ctx_2': 7.904,
     'c_ctx_2': 2.847,
     'b_ada_2': 3.662,
     'g_mix_2': 8.0,
     'b_fourier_2': 8.0,
     'g_q_a_2': 8.0,
     'w_q_b_2': 3.04,
     'g_kv_a_2': 8.0,
     'g_ffn_2': 8.0,
     'b_dw_2': 8.0,
     'g_final_2': 2.829}
    for name, (base, spread) in spreads.items():
        noise = np.random.default_rng([zlib.crc32(name.encode()), seed]).standard_normal(out[name].shape)
        drawn = base * np.exp(spread * noise) if base else spread * noise
        out[name] = __import__('jax').numpy.asarray(drawn.astype(out[name].dtype))
    for name, factor in factors.items():
        out[name] = (out[name] * factor).astype(out[name].dtype)
    return out
```

```python
from contextlib import ExitStack
import math

import numpy as np
import concourse.bass as bass
from concourse import mybir

F32 = mybir.dt.float32
F32R = mybir.dt.float32r
ALU = mybir.AluOpType
ACT = mybir.ActivationFunctionType
AX_X = mybir.AxisListType.X

P = 128
D = 1024
KD = D // P
TL, TC = 512, 256
DFF = 2816
KF = DFF // P
SLAB = 8 * P
RAW = 4
HL = 2
HD = 64
N_BUCKETS = 32
NTAB = 640
NEG = -1e30
EPS = 1e-6
MLA_H, NOPE, ROPE = 12, 64, 32
MLA_SCALE = (NOPE + ROPE) ** -0.5
NMOD = 48


def bucket_tables():
    dist = 511 - np.arange(NTAB)
    n = np.maximum(dist, 0)
    nf = np.maximum(n, 1).astype(np.float32)
    half = N_BUCKETS // 2
    large = half + (np.log(nf / np.float32(half)) / np.float32(math.log(2048 / half))
                    * np.float32(N_BUCKETS - half)).astype(np.int32)
    bucket = np.where(n < half, n, np.minimum(large, N_BUCKETS - 1))
    t = np.zeros((N_BUCKETS + 1, 2, NTAB), np.float32)
    t[bucket, :, np.arange(NTAB)] = 1.0
    count = (dist <= 128).astype(int) + (dist % 4 == 0) + (dist % 16 == 0)
    t[N_BUCKETS, 0] = np.where((dist >= 0) & (dist <= 127), 0.0, NEG)
    t[N_BUCKETS, 1] = np.where((dist >= 0) & (count > 0), np.log(np.maximum(count, 1)), NEG)
    return t


def rope_table():
    t = np.arange(TL)
    freq = (10000.0 ** (-np.arange(8, dtype=np.float32) / 8)).astype(np.float32)
    ang = np.concatenate([(t // 64)[None, :] * freq[:, None], (t % 64)[None, :] * freq[:, None]]).astype(np.float32)
    out = np.zeros((P, TL), np.float32)
    out[64:96] = np.concatenate([np.cos(ang), np.cos(ang)])
    out[96:128] = np.concatenate([-np.sin(ang), np.sin(ang)])
    return out


def dft_slabs(n):
    ang = 2 * np.pi * (np.outer(np.arange(n), np.arange(n)) % n) / n
    mats = [m.astype(np.float32).reshape(n // P, P, n).transpose(1, 0, 2).reshape(P, -1) for m in (np.cos(ang), np.sin(ang))]
    return np.concatenate(mats, axis=1).reshape(P, -1, SLAB).transpose(1, 0, 2)


def channel_dft(n):
    ang = 2 * np.pi * (np.outer(np.arange(64), np.arange(64)) % 64) / 64
    s = 1.0 / math.sqrt(n * 64)
    out = np.zeros((2, P, P), np.float32)
    for g in (0, 64):
        out[0, g:g + 64, g:g + 64] = np.cos(ang) * s
        out[1, g:g + 64, g:g + 64] = -np.sin(ang) * s
    return out


class Cols:
    def __init__(self):
        self.at, self.n = {}, 0

    def add(self, name, tiles):
        self.at[name] = self.n
        self.n += tiles


COLS = Cols()
for _n in ("ffn1_pre_g", "ffn1_post_g", "attn_pre_g", "b_out", "attn_post_g", "ffn2_pre_g", "ffn2_post_g",
           "ple_pre_g", "ple_post_g", "zero", "g_final"):
    COLS.add(_n, KD)
COLS.add("b_in", 18)
for _l in range(2):
    for _n, _k in (("b_ada", NMOD), ("g_mix", KD), ("b_f", 2), ("g_q", 3), ("g_kv", 1), ("g_ffn", KD),
                   ("w_dw0", 2 * KF), ("w_dw1", 2 * KF), ("w_dw2", 2 * KF), ("b_dw", 2 * KF)):
        COLS.add(f"{_n}{_l}", _k)


class Role:
    def __init__(self, sem, primed=0):
        self.sem, self.n, self.primed = sem, primed, primed

    def span(self, units):
        s = Span(self.sem, self.n)
        self.n += units
        return s


class Span:
    def __init__(self, sem, base):
        self.sem, self.base = sem, base

    def wait(self, e, k):
        v = self.base + k + 1
        if not isinstance(v, int) or v > 0:
            e.wait_ge(self.sem, v)


def units(e, n, body, fn):
    full = n // body if n // body >= 2 else 0
    if full:
        with e.Fori(0, full) as i:
            for j in range(body):
                fn(j, i)
    for k in range(full * body, n):
        fn(k % body, k // body)


def skewed(e, bodies, size, stages):
    def step(b, j, lo, hi):
        for lag, fn in stages:
            back = 0
            jj = j - lag
            while jj < 0:
                jj += size
                back += 1
            if lo is not None and b - back < lo:
                continue
            if hi is not None and b - back >= hi:
                continue
            fn(b - back if back else b, jj)

    assert max(lag for lag, _ in stages) <= size
    for j in range(size):
        step(0, j, 0, bodies)
    if bodies > 1:
        with e.Fori(1, bodies) as i:
            for j in range(size):
                step(i, j, None, None)
    for j in range(max(lag for lag, _ in stages)):
        step(bodies, j, 0, bodies)


def build(nc, d):
    ctx = ExitStack()
    with ctx:
        base0 = 16512
        top = 229344
        place = {"next": base0}

        def sb(name, shape, dt=F32, at=None):
            size = int(np.prod(shape[1:])) * 4
            if at is None:
                at = place["next"]
                place["next"] += (size + 31) // 32 * 32
                assert place["next"] <= top, name
            return nc.alloc_sbuf_tensor_at(name, shape, dt, offset=at)

        KB = 1024
        cols = sb("cols", [P, COLS.n])
        rope = sb("rope", [P, TL])
        ident = sb("ident", [P, P])
        flip = sb("flip", [P, P])
        ones = sb("ones", [P, P])
        mod = sb("mod", [P, 2, NMOD, 2])
        gains = sb("gains", [P, 2, 2, 2, KD])
        silu_c = sb("silu_c", [P, KD, 2])
        c_raw = sb("c_raw", [P, KD, 2])
        sinks = sb("sinks", [P, 16])
        rel = sb("rel", [N_BUCKETS + 1, 16])
        small = sb("small", [P, 64])
        rinv = sb("rinv", [P, 8])
        eps = sb("eps", [P, 2])
        qb8 = sb("qb8", [P, 8])
        x = sb("x", [P, KD, TL])
        cx = sb("cx", [P, KD, TC])
        raw = sb("raw", [P, RAW, SLAB])
        whi = sb("whi", [P, HL, SLAB], F32R)
        wlo = sb("wlo", [P, HL, SLAB], F32R)
        AR = place["next"]
        ada_raw = sb("ada_raw", [P, RAW, SLAB])
        XN = place["next"]
        xnh = sb("xnh", [P, KD, TL], F32R)
        xnl = sb("xnl", [P, KD, TL], F32R)
        HM = place["next"]
        hmh = sb("hmh", [P, KF, TL], F32R)
        hml = sb("hml", [P, KF, TL], F32R)
        SH = place["next"]
        sil = sb("sil", [P, TL])
        hbuf = sb("hbuf", [P, 2, TL])
        yg = sb("yg", [P, 2, TL], at=AR)
        yv = sb("yv", [P, 2, TL], at=AR + 4 * KB)
        nt = {k: sb("nt_" + k, s, at=HM + (60 + o) * KB) for k, s, o in
              (("sq", [P, 2, TL], 0), ("acc", [P, TL], 4), ("rstd", [P, TL], 6), ("tmp", [P, 2, TL], 8))}
        pn_ffn = {k: sb("pf_" + k, s, at=XN + o * KB) for k, s, o in
                  (("src", [P, 4, TL], 0), ("sq", [P, 2, TL], 8), ("acc", [P, TL], 12), ("rstd", [P, TL], 14),
                   ("tmp", [P, 2, TL], 16))}
        pn_hm = {k: sb("ph_" + k, s, at=HM + o * KB) for k, s, o in
                 (("src", [P, 8, TL], 72), ("sq", [P, 2, TL], 48), ("acc", [P, TL], 52), ("rstd", [P, TL], 54),
                  ("tmp", [P, 2, TL], 56))}
        nt2 = {k: sb("nt2_" + k, s, at=AR + o * KB) for k, s, o in
               (("sq", [P, 2, TL], 0), ("acc", [P, TL], 4), ("rstd", [P, TL], 6), ("tmp", [P, 2, TL], 8))}
        onehot = sb("onehot", [N_BUCKETS + 1, 2, NTAB], at=HM)
        tab = sb("tab", [8, 4, NTAB // 2], at=HM + 8 * KB)
        q1 = sb("q1", [HD, 16, TL], at=HM)
        k1 = sb("k1", [HD, 12, TL], at=HM + 32 * KB)
        v1 = sb("v1", [P, 4, 12 * HD], at=HM + 56 * KB)
        qst1 = sb("qst1", [HD, 2, TL], at=HM + 68 * KB)
        strip = sb("strip", [P, 2, TL], at=HM + 72 * KB)
        p1 = sb("p1", [P, 2, TL], at=HM + 76 * KB)
        pt1 = sb("pt1", [P, 2, TL], at=HM + 80 * KB)
        v_bias = sb("v_bias", [P, 640], at=HM + 84 * KB)
        mix1 = sb("mix1", [P, 4, 2 * TL], at=XN)
        m1h = sb("m1h", [P, KD, TL], F32R, at=HM)
        m1l = sb("m1l", [P, KD, TL], F32R, at=HM + 16 * KB)
        e_sb = sb("e_sb", [P, KD, TL], at=HM)
        sg = sb("sg", [P, 2, TL], at=HM + 32 * KB)
        p_raw = sb("p_raw", [P, 2, TL], at=HM + 36 * KB)
        ph = sb("ph", [P, 2, TL], F32R, at=HM + 40 * KB)
        pl = sb("pl", [P, 2, TL], F32R, at=HM + 44 * KB)
        q2 = sb("q2", [96, MLA_H, TL], at=HM)
        k2 = sb("k2", [96, MLA_H, TL + TC], at=HM + 24 * KB)
        v2 = sb("v2", [P, 6, MLA_H * HD], at=HM + 60 * KB)
        qst2 = sb("qst2", [96, 2, TL], at=HM + 78 * KB)
        p2 = sb("p2", [P, 2, TL + TC], at=HM + 82 * KB)
        pt2 = sb("pt2", [P, 2, TL + TC], at=SH)
        mix2 = sb("mix2", [P, 4, MLA_H * HD], at=AR)
        rt2 = sb("rt2", [96, 2, TL], at=AR + 12 * KB)
        finh = sb("finh", [P, 4, 256], F32R, at=HM)
        finl = sb("finl", [P, 4, 256], F32R, at=HM + 4 * KB)
        fh = sb("fh", [P, 2, TL], F32R, at=HM)
        fl = sb("fl", [P, 2, TL], F32R, at=HM + 4 * KB)
        pqh = sb("pqh", [P, 4, TL], F32R, at=HM + 8 * KB)
        pql = sb("pql", [P, 4, TL], F32R, at=HM + 16 * KB)
        cq = sb("cq", [P, 4, TL], at=HM + 78 * KB)
        cnh = sb("cnh", [P, 4, TL], F32R, at=XN + 4 * KB)
        cnl = sb("cnl", [P, 4, TL], F32R, at=XN + 20 * KB)
        yout = sb("yout", [P, KD, TL], at=XN)

        ps = ctx.enter_context(nc.psum_tensor("ps", [P, 8, TL], F32))

        def sem(name):
            return ctx.enter_context(nc.semaphore(name))

        def role(name, primed=0):
            return Role(sem(name), primed)

        s_setup = sem("setup_loads")
        s_out = sem("output_stores")
        s_tab = sem("bias_table_stored")
        s_vbias = sem("v_bias_loaded")
        s_pload = sem("p_loaded")
        s_krope = sem("krope_spread")
        raw_full = [sem(f"raw_full{i}") for i in range(RAW)]
        ada_full = [sem(f"ada_full{i}") for i in range(RAW)]
        strip_full = [sem(f"strip_full{i}") for i in range(2)]
        count = {"slabs": 0, "ada": 0, "strips": 0, "krope": 0}
        r = {}
        for name, primed in (
                ("slab_hi", 0), ("slab_lo", 0), ("slab_used", 0), ("ada_used", 0), ("mod", 0), ("gain", 0),
                ("const", 0), ("silu_c", 0), ("tab_mm", 0), ("tab_sb", 0),
                ("sil", 0), ("h", 2), ("h_hi", 0), ("h_lo", 2), ("yg", 0), ("yv", 0), ("cg", 0), ("cv", 0),
                ("x", 0), ("cx", 4), ("fsb", 0), ("sq", 0), ("acc", 0), ("ss", 0), ("std", 0), ("rstd", 0),
                ("tmp", 0), ("xn_hi", 0), ("xn", 0), ("upd", 0), ("ev_a", 4), ("ev_d", 4),
                ("qst", 0), ("S", 0), ("mx", 0), ("negm", 0), ("exp", 0), ("es", 0), ("tot", 0), ("rinv", 0),
                ("PT", 0), ("cp_a", 0), ("cp_d", 0), ("pv", 0), ("o", 0),
                ("mt_mm", 0), ("mt_hi", 0), ("mt", 0), ("fin_hi", 0), ("fin", 0), ("pq_hi", 0), ("pq", 0),
                ("f_mm", 0), ("f_hi", 0), ("f", 0), ("four_hi", 0), ("four", 0), ("cq", 0), ("kr", 0),
                ("rot", 0), ("vt", 0), ("p_hi", 0), ("p_lo", 0), ("e", 0), ("sg", 0), ("y", 4), ("qb", 0), ("yout", 0)):
            r[name] = Role(sem(name), primed)

        def take(kind, n):
            b = count[kind]
            count[kind] += n
            return b

        def col(name, n=0):
            return cols[:, bass.ds(COLS.at[name] + n, 1)]

        hi_done, lo_done, used = r["slab_hi"].span(0), r["slab_lo"].span(0), r["slab_used"].span(0)

        def load(e, s0, i):
            lo_done.wait(e, s0 + RAW * i - RAW)
            e.dma_start(raw[:, s0 % RAW, :], d["ws"][bass.ds(s0 + RAW * i, 1)].rearrange("a p n -> (a p) n")) \
                .then_inc(raw_full[s0 % RAW], 16)

        def split_hi(e, s0, i=0):
            if isinstance(i, int) and s0 + RAW * i >= count["slabs"]:
                return
            e.wait_ge(raw_full[s0 % RAW], 16 * (s0 // RAW + 1 + i))
            used.wait(e, s0 + RAW * i - HL)
            e.activation(whi[:, s0 % HL, :], raw[:, s0 % RAW, :], ACT.Copy).then_inc(hi_done.sem, 1)

        def split_lo(e, s0, i=0):
            if isinstance(i, int) and s0 + RAW * i >= count["slabs"]:
                return
            hi_done.wait(e, s0 + RAW * i)
            e.tensor_tensor(wlo[:, s0 % HL, :], raw[:, s0 % RAW, :], whi[:, s0 % HL, :].bitcast(F32),
                            ALU.subtract).then_inc(lo_done.sem, 1)

        def slab(s0):
            return whi[:, s0 % HL, :], wlo[:, s0 % HL, :]

        def ring_act(e, base, n, evac=lambda j, i: None):
            def step(j, i):
                used.wait(e, base + RAW * i + j)
                evac(j, i)
                split_hi(e, base + j + HL, i)
            units(e, n, RAW, step)

        def ring_dve(e, base, n, evac=lambda j, i: None):
            def step(j, i):
                used.wait(e, base + RAW * i + j)
                evac(j, i)
                split_lo(e, base + j + HL, i)
            units(e, n, RAW, step)

        def ring_pe(e, base, n, mms):
            def step(j, i):
                lo_done.wait(e, base + RAW * i + j)
                mms(j, i, *slab(base + j)).then_inc(used.sem, 1)
            units(e, n, RAW, step)

        def mm3(e, out, a, b, start, stop):
            e.matmul(out, a[0], b[0], start=start, stop=False, skip_group_check=True)
            e.matmul(out, a[0], b[1], start=False, stop=False, skip_group_check=True)
            return e.matmul(out, a[1], b[0], start=False, stop=stop, skip_group_check=True)

        def blk(pair, b, n=P):
            return tuple(w[:, b * n:(b + 1) * n] for w in pair)

        def dense(e, out, w, acts, T, kb=KD, wait_k=None):
            for k in range(kb):
                if wait_k is not None:
                    wait_k(k)
                mm = mm3(e, out, blk(w, k), tuple(a[:, k, 0:T] for a in acts), k == 0, k == kb - 1)
            return mm

        phases = []

        class Phase:
            def __init__(self):
                phases.append(self)

            def pe(self, e): pass
            def act(self, e): pass
            def dve(self, e): pass
            def pool(self, e): pass

        class Setup(Phase):
            LOADS = 11

            def __init__(self):
                super().__init__()
                self.const = r["const"].span(4)
                self.qb = r["qb"].span(1)
                self.silu = r["silu_c"].span(1)
                self.mm = r["tab_mm"].span(1)
                self.tsb = r["tab_sb"].span(1)

            def wait(self, e):
                e.wait_ge(s_setup, 16 * self.LOADS)

            def pool(self, e):
                for n, (dst, v) in enumerate(((ones[:], 1.0), (rel[N_BUCKETS:N_BUCKETS + 1, :], 1.0), (eps[:, 0:1], EPS),
                                              (eps[:, 1:2], 4 * EPS))):
                    self.const.wait(e, n - 1)
                    e.memset(dst, v).then_inc(self.const.sem, 1)
                self.const.wait(e, 3)
                for ro in r.values():
                    if ro.primed:
                        e.sem_inc(ro.sem, ro.primed)
                self.wait(e)

            def act(self, e):
                for dst, src in ((cols[:], d["cols"]), (x[:], d["xT"]), (c_raw[:], d["cT"]),
                                 (onehot[:], d["onehot"]), (rel[0:N_BUCKETS, :], d["rel_bias"]),
                                 (ident[:], d["ident"]), (flip[:], d["flip"]), (cx[:], d["ctxT"]),
                                 (rope[:], d["rope"]), (sinks[:, 0:8], d["sinks"].partition_broadcast(P)),
                                 (sinks[:, 8:16], d["no_sinks"].partition_broadcast(P))):
                    e.dma_start(dst, src).then_inc(s_setup, 16)
                self.wait(e)
                self.const.wait(e, 3)
                e.activation(silu_c[:], c_raw[:], ACT.Silu).then_inc(self.silu.sem, 1)
                self.mm.wait(e, 0)
                e.activation(tab[:], ps[0:8, 0:4, 0:NTAB // 2], ACT.Copy).then_inc(self.tsb.sem, 1)
                self.tsb.wait(e, 0)
                for m in range(2):
                    e.dma_start(d["tables"][m].rearrange("h (c x) -> h c x", c=2),
                                tab[:, 2 * m:2 * m + 2, :]).then_inc(s_tab, 16)
                split_hi(e, 0)
                split_hi(e, 1)
                e.wait_ge(s_tab, 32)

            def pe(self, e):
                self.wait(e)
                self.const.wait(e, 1)
                for m in range(2):
                    for c in range(2):
                        mm = e.matmul(ps[0:8, 2 * m + c, 0:320], rel[:, 8 * m:8 * m + 8],
                                      onehot[:, m, c * 320:(c + 1) * 320], start=True, stop=True)
                mm.then_inc(self.mm.sem, 1)
                self.tsb.wait(e, 0)
                self.silu.wait(e, 0)

            def dve(self, e):
                self.wait(e)
                b0 = COLS.at["b_in"]
                e.tensor_scalar(qb8[:], cols[:, b0:b0 + 8], 0.125, None, ALU.mult).then_inc(self.qb.sem, 1)
                split_lo(e, 0)
                split_lo(e, 1)

        class Norm:
            def __init__(self, srcs, ready, T, dim, t, gain=None, shift=None, outs=None, plain=None, bank=4):
                self.bank = bank
                self.srcs, self.ready, self.T, self.dim, self.t = srcs, ready, T, dim, t
                self.gain, self.shift, self.outs, self.plain = gain, shift, outs, plain
                n = self.n = len(srcs)
                self.sq, self.acc = r["sq"].span(n), r["acc"].span(n - 1)
                self.ss, self.std, self.rs = r["ss"].span(1), r["std"].span(1), r["rstd"].span(1)
                if outs is not None:
                    self.tmp, self.hi, self.out = r["tmp"].span(n), r["xn_hi"].span(n), r["xn"].span(n)
                if plain is not None:
                    self.out = r["yout"].span(n)

            def act_squares(self, e, first=0, last=None):
                for n in range(first, self.n if last is None else last):
                    self.ready(e, n)
                    if n >= 2:
                        self.acc.wait(e, n - 3 if n > 3 else 0)
                    e.activation(self.t["sq"][:, n % 2, 0:self.T], self.srcs[n], ACT.Square).then_inc(self.sq.sem, 1)

            def pool_adds(self, e):
                acc = self.t["acc"][:, 0:self.T]
                for n in range(1, self.n):
                    self.sq.wait(e, n)
                    if n >= 2:
                        self.acc.wait(e, n - 2)
                    first = self.t["sq"][:, 0, 0:self.T] if n == 1 else acc
                    e.tensor_tensor(acc, first, self.t["sq"][:, n % 2, 0:self.T], ALU.add).then_inc(self.acc.sem, 1)

            def pe_stats(self, e):
                if self.n > 1:
                    self.acc.wait(e, self.n - 2)
                    src = self.t["acc"][:, 0:self.T]
                else:
                    self.sq.wait(e, 0)
                    src = self.t["sq"][:, 0, 0:self.T]
                e.matmul(ps[:, self.bank, 0:self.T], ones[:], src, start=True, stop=True,
                         skip_group_check=True).then_inc(self.ss.sem, 1)

            def act_std(self, e, half=False):
                self.ss.wait(e, 0)
                f = 4.0 if half else 1.0
                e.activation(self.t["rstd"][:, 0:self.T], ps[:, self.bank, 0:self.T], ACT.Sqrt,
                             scale=f / self.dim, bias=eps[:, int(half):int(half) + 1]).then_inc(self.std.sem, 1)

            def dve_rstd(self, e):
                self.std.wait(e, 0)
                e.reciprocal(self.t["rstd"][:, 0:self.T], self.t["rstd"][:, 0:self.T]).then_inc(self.rs.sem, 1)

            def act_hi(self, e):
                for n in range(self.n):
                    self.tmp.wait(e, n)
                    e.activation(self.outs[0][:, n, 0:self.T], self.t["tmp"][:, n % 2, 0:self.T], ACT.Identity,
                                 bias=self.shift(n)).then_inc(self.hi.sem, 1)

            def dve_tiles(self, e):
                self.rs.wait(e, 0)
                def lo(n):
                    self.hi.wait(e, n)
                    e.scalar_tensor_tensor(out=self.outs[1][:, n, 0:self.T], in0=self.t["tmp"][:, n % 2, 0:self.T],
                                           scalar=self.shift(n), in1=self.outs[0][:, n, 0:self.T].bitcast(F32),
                                           op0=ALU.add, op1=ALU.subtract).then_inc(self.out.sem, 1)
                for n in range(self.n):
                    if n >= 2:
                        self.out.wait(e, n - 2)
                    e.scalar_tensor_tensor(out=self.t["tmp"][:, n % 2, 0:self.T], in0=self.srcs[n],
                                           scalar=self.gain(n), in1=self.t["rstd"][:, 0:self.T],
                                           op0=ALU.mult, op1=ALU.mult).then_inc(self.tmp.sem, 1)
                    if n >= 1:
                        lo(n - 1)
                lo(self.n - 1)

            def dve_plain(self, e):
                self.rs.wait(e, 0)
                for n in range(self.n):
                    e.scalar_tensor_tensor(out=self.plain[:, n, 0:self.T], in0=self.srcs[n], scalar=self.gain(n),
                                           in1=self.t["rstd"][:, 0:self.T], op0=ALU.mult,
                                           op1=ALU.mult).then_inc(self.out.sem, 1)

        class PreNorm(Phase):
            def __init__(self, stream, ready, gain, shift):
                super().__init__()
                xs, T = stream
                self.norm = Norm([xs[:, n, 0:T] for n in range(KD)], ready, T, D, nt, gain, shift, (xnh, xnl))
                self.out = self.norm.out

            def act(self, e):
                self.norm.act_squares(e)
                self.norm.act_std(e)
                self.norm.act_hi(e)

            def pool(self, e):
                self.norm.pool_adds(e)

            def pe(self, e):
                self.norm.pe_stats(e)

            def dve(self, e):
                self.norm.dve_rstd(e)
                self.norm.dve_tiles(e)

        class PostNorm(Phase):
            def __init__(self, srcs, ready, t, gain, half, early=0):
                super().__init__()
                self.norm = Norm(srcs, ready, TL, D, t, gain)
                self.half, self.early, self.gain = half, early, gain
                self.upd = r["upd"].span(KD)
                self.out = r["x"].span(KD)

            def act(self, e):
                self.norm.act_squares(e, self.early)
                self.norm.act_std(e, self.half)

            def pool(self, e):
                self.norm.pool_adds(e)

            def pe(self, e):
                self.norm.pe_stats(e)

            def dve(self, e):
                m = self.norm
                m.dve_rstd(e)
                m.rs.wait(e, 0)
                def add_x(n):
                    self.upd.wait(e, n)
                    e.tensor_tensor(x[:, n, :], x[:, n, :], m.t["tmp"][:, n % 2, :], ALU.add).then_inc(self.out.sem, 1)
                for n in range(KD):
                    if n >= 2:
                        self.out.wait(e, n - 2)
                    e.scalar_tensor_tensor(out=m.t["tmp"][:, n % 2, :], in0=m.srcs[n], scalar=self.gain(n),
                                           in1=m.t["rstd"][:], op0=ALU.mult, op1=ALU.mult).then_inc(self.upd.sem, 1)
                    if n >= 1:
                        add_x(n - 1)
                add_x(KD - 1)

        class GateUp(Phase):
            def __init__(self, T, xn, conv=None, ada=None):
                super().__init__()
                self.T, self.xn, self.conv, self.ada = T, xn, conv, ada
                self.base = take("slabs", 2 * KF)
                if ada is not None:
                    self.abase = take("ada", NMOD)
                    self.mod = r["mod"].span(1)
                    self.gain = r["gain"].span(4)
                self.sil, self.h = r["sil"].span(KF), r["h"].span(KF)
                self.h_hi, self.h_lo = r["h_hi"].span(KF), r["h_lo"].span(KF)
                if conv is not None:
                    self.yg, self.yv = r["yg"].span(KF), r["yv"].span(KF)
                    self.cg, self.cv = r["cg"].span(2 * KF), r["cv"].span(2 * KF)

            def ada_tile(self, e, j, i, shift=0):
                a0 = self.abase + j
                e.wait_ge(ada_full[a0 % RAW], 16 * (a0 // RAW + 1 + i))
                for k in range(KD):
                    mm = e.matmul(ps[:, 7, bass.ds(8 * i + 2 * j, 2)], ada_raw[:, a0 % RAW, k * P:(k + 1) * P],
                                  silu_c[:, k, :], start=(k == 0), stop=(k == KD - 1), skip_group_check=True)
                mm.then_inc(r["ada_used"].sem, 1)

            def pe(self, e):
                T, acts = self.T, (xnh, xnl)

                def mms(j, i, hi, lo):
                    if j % 2 == 0:
                        self.h.wait(e, 2 * i + j // 2 - 2)
                    mm = dense(e, ps[:, j, 0:T], (hi, lo), acts, T,
                               wait_k=(lambda k: self.xn.wait(e, k)) if j == 0 else None)
                    return mm

                def step(j, i):
                    lo_done.wait(e, self.base + RAW * i + j)
                    mms(j, i, *slab(self.base + j)).then_inc(used.sem, 1)
                    if self.ada is not None:
                        self.ada_tile(e, j, i)
                units(e, 2 * KF, RAW, step)
                if self.ada is not None:
                    for a in range(2 * KF, NMOD):
                        self.ada_tile(e, a % RAW, a // RAW)

            def act(self, e):
                T = self.T

                def hid(b, m, q):
                    self.h.wait(e, m)
                    e.activation(hmh[:, bass.ds(m, 1), 0:T].rearrange("p a t -> p (a t)"), hbuf[:, q, 0:T],
                                 ACT.Copy).then_inc(self.h_hi.sem, 1)

                def evac(j, i):
                    q, m = j // 2, 2 * i + j // 2
                    if self.conv is None:
                        if j % 2 == 0:
                            self.h.wait(e, m - 1)
                            e.activation(sil[:, 0:T], ps[:, j, 0:T], ACT.Silu).then_inc(self.sil.sem, 1)
                        else:
                            split_hi(e, self.base + j + HL, i)
                            hid(None, m, q)
                        return
                    l = self.conv
                    y, ro, off = (yg, self.yg, 0) if j % 2 == 0 else (yv, self.yv, KF)
                    self.h.wait(e, m - 2)
                    e.activation(y[:, q, 0:T], ps[:, j, 0:T], ACT.Identity, bias=col(f"b_dw{l}", m + off),
                                 scale=col(f"w_dw1{l}", m + off)).then_inc(ro.sem, 1)
                    if j % 2 == 1:
                        split_hi(e, self.base + j + HL, i)
                        self.cg.wait(e, 2 * m + 1)
                        self.h.wait(e, m - 1)
                        e.activation(sil[:, 0:T], yg[:, q, 0:T], ACT.Silu).then_inc(self.sil.sem, 1)
                        hid(None, m, q)

                def step(j, i):
                    used.wait(e, self.base + RAW * i + j)
                    evac(j, i)
                    if j % 2 == 0:
                        split_hi(e, self.base + j + HL, i)
                units(e, 2 * KF, RAW, step)

            def dve(self, e):
                T = self.T

                def make_h(m, q, up):
                    self.sil.wait(e, m)
                    self.h_lo.wait(e, m - 2)
                    e.tensor_tensor(hbuf[:, q, 0:T], sil[:, 0:T], up, ALU.mult).then_inc(self.h.sem, 1)

                def lo(m, q):
                    self.h_hi.wait(e, m)
                    dst = (slice(None), bass.ds(m, 1), slice(0, T))
                    e.tensor_tensor(hml[dst].rearrange("p a t -> p (a t)"), hbuf[:, q, 0:T],
                                    hmh[dst].rearrange("p a t -> p (a t)").bitcast(F32),
                                    ALU.subtract).then_inc(self.h_lo.sem, 1)

                def conv(j, m, q):
                    l = self.conv
                    y, ro, dn, off = (yg, self.yg, self.cg, 0) if j % 2 == 0 else (yv, self.yv, self.cv, KF)
                    ro.wait(e, m)
                    for k, (o, s, w) in enumerate(((slice(1, T), slice(0, T - 1), f"w_dw0{l}"),
                                                   (slice(0, T - 1), slice(1, T), f"w_dw2{l}"))):
                        if k:
                            dn.wait(e, 2 * m)
                        e.scalar_tensor_tensor(out=y[:, q, o], in0=ps[:, j, s], scalar=col(w, m + off), in1=y[:, q, o],
                                               op0=ALU.mult, op1=ALU.add).then_inc(dn.sem, 1)

                def step(j, i):
                    q, m = j // 2, 2 * i + j // 2
                    used.wait(e, self.base + RAW * i + j)
                    if self.conv is not None:
                        conv(j, m, q)
                    if j % 2 == 1:
                        if self.conv is None:
                            make_h(m, q, ps[:, j, 0:T])
                            split_lo(e, self.base + j + HL, i)
                        else:
                            split_lo(e, self.base + j + HL, i)
                            self.cv.wait(e, 2 * m + 1)
                            make_h(m, q, yv[:, q, 0:T])
                        lo(m, q)
                    else:
                        split_lo(e, self.base + j + HL, i)
                units(e, 2 * KF, RAW, step)
                if self.ada is not None:
                    l = self.ada
                    e.wait_ge(r["ada_used"].sem, self.abase + NMOD)
                    b_ada = cols[:, COLS.at[f"b_ada{l}"]:COLS.at[f"b_ada{l}"] + NMOD]
                    e.tensor_tensor(mod[:, l], ps[:, 7, 0:2 * NMOD].rearrange("p (n c) -> p n c", c=2),
                                    b_ada.unsqueeze(2).broadcast_to([P, NMOD, 2]), ALU.add).then_inc(self.mod.sem, 1)
                    self.mod.wait(e, 0)
                    for st in range(2):
                        for w, (at, g) in enumerate(((8, "g_mix"), (32, "g_ffn"))):
                            c = COLS.at[f"{g}{l}"]
                            e.scalar_tensor_tensor(out=gains[:, l, st, w, :], in0=mod[:, l, at:at + KD, st], scalar=1.0,
                                                   in1=cols[:, c:c + KD], op0=ALU.add,
                                                   op1=ALU.mult).then_inc(self.gain.sem, 1)

        class Down(Phase):
            SH = KF // 2

            def __init__(self, T, gu, stream=None, gate=None, x_role=None):
                super().__init__()
                self.T, self.gu, self.gate = T, gu, gate
                self.stream = stream
                self.base = take("slabs", 2 * self.SH)
                if gate is None:
                    self.fsb = r["fsb"].span(4)
                else:
                    self.out = r[x_role].span(KD)

            def halves(self, e, step):
                for hf in range(2):
                    b = self.base + hf * self.SH
                    for j in range(3):
                        step(hf, b, j, 0, j)
                    with e.Fori(0, 2) as i:
                        for j in range(RAW):
                            step(hf, b + 3, j, i, 3 + j + RAW * i)

            def bank(self, n):
                return n + 4 if n < 4 else n - 4

            def pe(self, e):
                T = self.T

                def step(hf, b, j, i, k):
                    lo_done.wait(e, b + RAW * i + j)
                    if hf == 0:
                        self.gu.h_lo.wait(e, 2 * k + 1)
                    w = slab(b + j)
                    for kk in range(2):
                        act = tuple(h[:, bass.ds(2 * k + kk, 1), 0:T].rearrange("p a t -> p (a t)") for h in (hmh, hml))
                        for n in range(4):
                            if self.gu.ada is not None and hf == 0 and isinstance(k, int) and k == 0 and n == 3:
                                self.gu.mod.wait(e, 0)
                            mm = mm3(e, ps[:, self.bank(4 * hf + n), 0:T], blk(w, kk * 4 + n), act,
                                     isinstance(k, int) and k == 0 and kk == 0, True)
                    mm.then_inc(used.sem, 1)
                self.halves(e, step)

            def act(self, e):
                done = {"half0": False}

                def step(hf, b, j, i, k):
                    used.wait(e, b + RAW * i + j)
                    split_hi(e, b + j + HL, i)
                    if self.gate is None and hf == 1 and isinstance(k, int) and k == 0:
                        for n in range(4):
                            e.activation(pn_ffn["src"][:, n, :], ps[:, self.bank(n), :], ACT.Copy).then_inc(self.fsb.sem, 1)
                        self.post.norm.act_squares(e, 0, 4)
                self.halves(e, step)

            def update(self, e, hf):
                xs, T = self.stream
                for n in range(4 * hf, 4 * hf + 4):
                    e.scalar_tensor_tensor(out=xs[:, n, 0:T], in0=ps[:, self.bank(n), 0:T], scalar=self.gate(n),
                                           in1=xs[:, n, 0:T], op0=ALU.mult, op1=ALU.add).then_inc(self.out.sem, 1)

            def dve(self, e):
                def step(hf, b, j, i, k):
                    used.wait(e, b + RAW * i + j)
                    split_lo(e, b + j + HL, i)
                    if self.gate is not None and hf == 1 and isinstance(k, int) and k == 0:
                        self.update(e, 0)
                self.halves(e, step)
                if self.gate is not None:
                    self.update(e, 1)

        def ffn_block1(xn, pre_gain, post_gain, ada, ready):
            pre = PreNorm((x, TL), ready, lambda n: col(pre_gain, n), lambda n: col("zero", n))
            gu = GateUp(TL, pre.out, ada=ada)
            down = Down(TL, gu)

            def f_ready(e, n):
                if n < 4:
                    down.fsb.wait(e, n)
                else:
                    used.wait(e, down.base + 2 * Down.SH - 1)
            srcs = [pn_ffn["src"][:, n, :] if n < 4 else ps[:, n - 4, :] for n in range(KD)]
            down.post = PostNorm(srcs, f_ready, pn_ffn, lambda n: col(post_gain, n), True, early=4)
            return down.post.out, gu

        class Attention(Phase):
            def __init__(self, heads, tt, tiles, q, k, v, qst, p, pt, mix, dk, scale, ready, q0=0, kslot=None,
                         key0=0, vt0=0, mix0=0, bias=False, head0=0, dsplit=0, free=None):
                super().__init__()
                self.heads, self.tt, self.tiles, self.q, self.k, self.v, self.qst_buf, self.p, self.pt, self.mix = heads, tt, tiles, q, k, v, qst, p, pt, mix
                self.dk, self.scale, self.ready, self.q0, self.kslot, self.key0, self.vt0, self.mix0, self.bias, self.head0, self.dsplit = dk, scale, ready, q0, kslot, key0, vt0, mix0, bias, head0, dsplit
                self.U = 2 * tt
                n = heads * tt
                self.S, self.mx, self.negm, self.exp, self.rinv, self.PT, self.pv = (
                    r[name].span(n) for name in ("S", "mx", "negm", "exp", "rinv", "PT", "pv"))
                self.cp_a, self.cp_d = r["cp_a"].span(n), r["cp_d"].span(n if dsplit else 0)
                self.qst, self.o = r["qst"].span(heads), r["o"].span(heads)
                if bias:
                    self.es, self.tot = r["es"].span(n), r["tot"].span(n)
                    self.strips0 = take("strips", heads // 2)

            def unit(self, b, j):
                return self.U * b + j, 2 * b + j // self.tt, j // self.tt, j % self.tt

            def cols_of(self, qt):
                t = self.tiles(qt)
                return t[0] * P, len(t) * P

            def s_ap(self, j, lo, n):
                return ps[:, 2 * (j % 2):2 * (j % 2) + 2, :].rearrange("p a t -> p (a t)")[:, lo:lo + n]

            def pool(self, e):
                self.ready(e)
                T = self.tt * P

                def stage(b, j):
                    h = 2 * b + j
                    self.S.wait(e, self.tt * (h - 1) - 1)
                    self.qst.wait(e, h - 1)
                    src = self.q[0:self.dk, bass.ds(h + self.q0, 1), 0:T].rearrange("p a t -> p (a t)")
                    e.tensor_copy(self.qst_buf[0:self.dk, j, 0:T], src).then_inc(self.qst.sem, 1)
                    if self.bias:
                        e.dma_start(strip[:, j, :], strips_view[bass.ds(h + self.head0, 1)]
                                    .rearrange("a p n -> (a p) n")).then_inc(strip_full[j], 16)
                if self.bias:
                    e.wait_ge(s_tab, 32)
                skewed(e, self.heads // 2, 2, [(0, stage)])

            def pe(self, e):
                self.ready(e)

                def scores(b, j):
                    u, h, par, qt = self.unit(b, j)
                    self.exp.wait(e, u - 2)
                    if qt == 0:
                        self.qst.wait(e, h)
                        if self.bias:
                            e.wait_ge(strip_full[par], 16 * (self.strips0 + b + 1))
                    c0, n = self.cols_of(qt)
                    if self.bias:
                        g0 = (3 - qt) * P + c0
                        e.matmul(self.s_ap(j, 0, n), flip[:], strip[:, par, g0:g0 + n], start=True, stop=False,
                                 skip_group_check=True)
                    for lo in range(0, n, 512):
                        m = min(512, n - lo)
                        kk = self.k[0:self.dk, bass.ds(self.kslot(b, par), 1), self.key0 + c0 + lo:self.key0 + c0 + lo + m]
                        mm = e.matmul(self.s_ap(j, lo, m), self.qst_buf[0:self.dk, par, qt * P:(qt + 1) * P],
                                      kk.rearrange("p a t -> p (a t)"), start=not self.bias, stop=True,
                                      skip_group_check=True)
                    mm.then_inc(self.S.sem, 1)

                def turn(b, j):
                    u, h, par, qt = self.unit(b, j)
                    self.exp.wait(e, u)
                    self.cp_a.wait(e, u - 1)
                    if self.dsplit:
                        self.cp_d.wait(e, u - 1)
                    _, n = self.cols_of(qt)
                    for t in range(n // P):
                        mm = e.transpose(ps[:, 4 + t // 4, (t % 4) * P:(t % 4 + 1) * P],
                                         self.p[:, j % 2, t * P:(t + 1) * P], ident[:])
                    mm.then_inc(self.PT.sem, 1)

                def pv(b, j):
                    u, h, par, qt = self.unit(b, j)
                    self.cp_a.wait(e, u)
                    if self.dsplit:
                        self.cp_d.wait(e, u)
                    if qt == 0:
                        self.o.wait(e, h - 2)
                    ts = self.tiles(qt)
                    for i_, t in enumerate(ts):
                        vv = self.v[:, self.vt0 + t, bass.ds(self.kslot(b, par) * HD, HD)]
                        mm = e.matmul(ps[:, 6 + par, qt * HD:(qt + 1) * HD], self.pt[:, j % 2, i_ * P:(i_ + 1) * P], vv,
                                      start=(i_ == 0), stop=(i_ == len(ts) - 1), skip_group_check=True)
                    mm.then_inc(self.pv.sem, 1)
                skewed(e, self.heads // 2, self.U, [(0, scores), (2, turn), (3, pv)])

            def sm(self, what, j):
                return small[:, 24 + 8 * what + j:25 + 8 * what + j]

            def dve(self, e):
                def rowmax(b, j):
                    u, h, par, qt = self.unit(b, j)
                    self.S.wait(e, u)
                    _, n = self.cols_of(qt)
                    e.tensor_reduce(self.sm(0, j), self.s_ap(j, 0, n), AX_X, ALU.max).then_inc(self.mx.sem, 1)
                    self.mx.wait(e, u)
                    if self.bias:
                        e.tensor_scalar(self.sm(1, j), self.sm(0, j), sinks[:, bass.ds(h + self.head0, 1)], -1.0, ALU.max,
                                        ALU.mult).then_inc(self.negm.sem, 1)
                    else:
                        e.tensor_scalar(self.sm(1, j), self.sm(0, j), -self.scale, None, ALU.mult) \
                            .then_inc(self.negm.sem, 1)

                def copy_t(b, j):
                    u, h, par, qt = self.unit(b, j)
                    self.PT.wait(e, u)
                    e.tensor_copy(self.pt[:, j % 2, 0:self.dsplit], ps[:, 4, 0:self.dsplit]).then_inc(self.cp_d.sem, 1)

                def inverse(b, j):
                    u, h, par, qt = self.unit(b, j)
                    src = self.sm(2, j)
                    if qt == 0:
                        self.o.wait(e, h - 2)
                    if self.bias:
                        self.es.wait(e, u)
                        e.tensor_tensor(self.sm(4, j), self.sm(2, j), self.sm(3, j), ALU.add).then_inc(self.tot.sem, 1)
                        self.tot.wait(e, u)
                        src = self.sm(4, j)
                    else:
                        self.exp.wait(e, u)
                    e.reciprocal(rinv[:, j:j + 1], src).then_inc(self.rinv.sem, 1)

                def finish(b, j):
                    u, h, par, qt = self.unit(b, j)
                    if qt < self.tt - 1:
                        return
                    self.pv.wait(e, u)
                    self.rinv.wait(e, u)
                    j0 = j - self.tt + 1
                    e.tensor_tensor(self.mix[:, 0:self.tt, bass.ds(h * HD + self.mix0, HD)],
                                    ps[:, 6 + par, 0:self.tt * HD].rearrange("p (t c) -> p t c", c=HD),
                                    rinv[:, j0:j0 + self.tt].unsqueeze(2).broadcast_to([P, self.tt, HD]),
                                    ALU.mult).then_inc(self.o.sem, 1)
                st = [(0, rowmax)] + ([(2, copy_t)] if self.dsplit else []) + [(2, inverse), (4, finish)]
                skewed(e, self.heads // 2, self.U, st)

            def act(self, e):
                def copy_t(b, j):
                    u, h, par, qt = self.unit(b, j)
                    self.PT.wait(e, u)
                    _, n = self.cols_of(qt)
                    n -= self.dsplit
                    bank = 5 if self.dsplit else 4
                    if n == 0:
                        raise AssertionError
                    e.activation(self.pt[:, j % 2, self.dsplit:self.dsplit + n], ps[:, bank, 0:n],
                                 ACT.Copy).then_inc(self.cp_a.sem, 1)

                def exps(b, j):
                    u, h, par, qt = self.unit(b, j)
                    self.negm.wait(e, u)
                    self.PT.wait(e, u - 2)
                    _, n = self.cols_of(qt)
                    e.activation(self.p[:, j % 2, 0:n], self.s_ap(j, 0, n), ACT.Exp, bias=self.sm(1, j),
                                 scale=self.scale, accum_out=self.sm(2, j)).then_inc(self.exp.sem, 1)
                    if self.bias:
                        e.activation(self.sm(3, j), sinks[:, bass.ds(h + self.head0, 1)], ACT.Exp,
                                     bias=self.sm(1, j)).then_inc(self.es.sem, 1)
                skewed(e, self.heads // 2, self.U, [(2, copy_t), (0, exps)])

        class MixTurn(Phase):
            def __init__(self, mix, n, tt, outs, first, ready, after):
                super().__init__()
                self.mix, self.n, self.tt = mix, n, tt
                self.outs, self.first, self.ready, self.after = outs, first, ready, after
                self.mm, self.hi, self.out = r["mt_mm"].span(n), r["mt_hi"].span(n), r["mt"].span(n)

            def pe(self, e):
                self.ready(e)
                for c in range(self.n):
                    if c >= 4:
                        self.out.wait(e, c - 4)
                    for t in range(self.tt):
                        mm = e.transpose(ps[:, c % 4, t * P:(t + 1) * P], self.mix[:, t, c * P:(c + 1) * P], ident[:])
                    mm.then_inc(self.mm.sem, 1)

            def act(self, e):
                T = self.tt * P
                for c in range(self.n):
                    self.mm.wait(e, c)
                    e.activation(self.outs[0][:, self.first + c, 0:T], ps[:, c % 4, 0:T], ACT.Copy).then_inc(self.hi.sem, 1)

            def dve(self, e):
                T = self.tt * P
                for c in range(self.n):
                    self.hi.wait(e, c)
                    e.tensor_tensor(self.outs[1][:, self.first + c, 0:T], ps[:, c % 4, 0:T],
                                    self.outs[0][:, self.first + c, 0:T].bitcast(F32), ALU.subtract).then_inc(self.out.sem, 1)

        class InProj1(Phase):
            def __init__(self, xn):
                super().__init__()
                self.xn, self.qb = xn, setup.qb
                self.base = take("slabs", 18)
                self.a, self.v = r["ev_a"].span(18), r["ev_d"].span(18)

            def pe(self, e):
                acts = (xnh, xnl)

                def free(k):
                    self.a.wait(e, k - 4)
                    self.v.wait(e, k - 4)

                def q(j, i, hi, lo):
                    free(RAW * i + j)
                    return dense(e, ps[:, j, :], (hi, lo), acts, TL,
                                 wait_k=(lambda k: self.xn.wait(e, k)) if j == 0 else None)

                def kv(j, i, hi, lo):
                    k = 8 + RAW * i + j
                    free(k)
                    if k < 13:
                        return dense(e, ps[:, k % 4, :], (hi, lo), acts, TL)
                    for t in range(4):
                        for kb in range(KD):
                            mm = mm3(e, ps[:, k % 4, t * P:(t + 1) * P], tuple(a[:, kb, t * P:(t + 1) * P] for a in acts),
                                     blk((hi, lo), kb), kb == 0, kb == KD - 1)
                    return mm
                ring_pe(e, self.base, 8, q)
                for k in range(10):
                    lo_done.wait(e, self.base + 8 + k)
                    kv(k % 4, k // 4, *slab(self.base + 8 + k)).then_inc(used.sem, 1)

            def pool(self, e):
                for lo, hi, at in ((640, 768, 0), (1792, 2304, P)):
                    e.dma_start(v_bias[:, at:at + hi - lo], d["b_in"][lo:hi].partition_broadcast(P)).then_inc(s_vbias, 16)

            def act(self, e):
                self.qb.wait(e, 0)
                def q(j, i):
                    c = RAW * i + j
                    e.activation(q1[:, bass.ds(2 * c, 1), :].rearrange("p a t -> p (a t)"), ps[0:HD, j, :], ACT.Identity,
                                 scale=0.125, bias=qb8[0:HD, bass.ds(c, 1)]).then_inc(self.a.sem, 1)
                ring_act(e, self.base, 8, q)
                for k in range(8, 18):
                    used.wait(e, self.base + k)
                    b = lambda c: cols[0:HD, COLS.at["b_in"] + c:COLS.at["b_in"] + c + 1]
                    if k == 8:
                        e.activation(k1[:, 0, :], ps[0:HD, k % 4, :], ACT.Identity, bias=b(k))
                        e.activation(k1[:, 1, :], ps[0:HD, k % 4, :], ACT.Identity, bias=b(k)).then_inc(self.a.sem, 1)
                    elif k < 13:
                        e.activation(k1[:, 4 + 2 * (k - 9), :], ps[0:HD, k % 4, :], ACT.Identity, bias=b(k)) \
                            .then_inc(self.a.sem, 1)
                    elif k == 13:
                        e.sem_inc(self.a.sem, 5)
                    split_hi(e, self.base + k + HL)

            def dve(self, e):
                self.qb.wait(e, 0)
                def q(j, i):
                    c = RAW * i + j
                    e.tensor_scalar(q1[:, bass.ds(2 * c + 1, 1), :].rearrange("p a t -> p (a t)"), ps[HD:P, j, :], 0.125,
                                    qb8[HD:P, bass.ds(c, 1)], ALU.mult, ALU.add).then_inc(self.v.sem, 1)
                ring_dve(e, self.base, 8, q)
                for k in range(8, 18):
                    used.wait(e, self.base + k)
                    b = cols[HD:P, COLS.at["b_in"] + k:COLS.at["b_in"] + k + 1]
                    if k < 13:
                        slots = (2, 3) if k == 8 else (5 + 2 * (k - 9),)
                        for s in slots:
                            op = e.tensor_scalar(k1[:, s, :], ps[HD:P, k % 4, :], b, None, ALU.add)
                    else:
                        if k == 13:
                            e.wait_ge(s_vbias, 32)
                        c = k - 13
                        src = ps[:, k % 4, :].rearrange("p (t c) -> p t c", c=P)
                        bias = v_bias[:, c * P:(c + 1) * P].unsqueeze(1).broadcast_to([P, 4, P])
                        if c == 0:
                            for kv in range(2):
                                for dup in range(2):
                                    at = (2 * kv + dup) * HD
                                    op = e.tensor_tensor(v1[:, :, at:at + HD], src[:, :, kv * HD:(kv + 1) * HD],
                                                         bias[:, :, kv * HD:(kv + 1) * HD], ALU.add)
                        else:
                            at = 4 * HD + (c - 1) * P
                            op = e.tensor_tensor(v1[:, :, at:at + P], src, bias, ALU.add)
                    op.then_inc(self.v.sem, 1)
                    split_lo(e, self.base + k + HL)

        class OutProj(Phase):
            def __init__(self, T, acts, ready, stream=None, gate=None, x_role=None, mats=None):
                super().__init__()
                self.T, self.acts, self.ready, self.stream, self.gate = T, acts, ready, stream, gate
                self.base = take("slabs", KD)
                self.out = r["ev_a"].span(KD) if gate is None else r[x_role].span(KD)

            def pe(self, e):
                self.ready(e)

                def mms(j, i, hi, lo):
                    k = RAW * i + j
                    if isinstance(k, int):
                        if k >= 4:
                            self.out.wait(e, k - 4)
                    else:
                        self.out.wait(e, k - 4)
                    return dense(e, ps[:, j, 0:self.T], (hi, lo), self.acts, self.T)
                ring_pe(e, self.base, KD, mms)

            def act(self, e):
                if self.gate is not None:
                    return ring_act(e, self.base, KD)
                def evac(j, i):
                    n = RAW * i + j
                    e.activation(pn_hm["src"][:, bass.ds(n, 1), :].rearrange("p a t -> p (a t)"), ps[:, j, :],
                                 ACT.Identity, bias=col("b_out", n)).then_inc(self.out.sem, 1)
                ring_act(e, self.base, KD, evac)

            def dve(self, e):
                if self.gate is None:
                    return ring_dve(e, self.base, KD)
                xs, T = self.stream

                def evac(j, i):
                    n = RAW * i + j
                    xa = xs[:, bass.ds(n, 1), 0:T].rearrange("p a t -> p (a t)")
                    e.scalar_tensor_tensor(out=xa, in0=ps[:, j, 0:T], scalar=self.gate(n), in1=xa, op0=ALU.mult,
                                           op1=ALU.add).then_inc(self.out.sem, 1)
                ring_dve(e, self.base, KD, evac)

        class Embed(Phase):
            def __init__(self, xn):
                super().__init__()
                self.xn = xn
                self.base = take("slabs", 10)
                self.e = r["e"].span(KD)
                self.sg, self.y = r["sg"].span(KD), r["y"].span(KD)
                self.p_hi, self.p_lo = r["p_hi"].span(1), r["p_lo"].span(1)

            def pe(self, e):
                self.p_lo.wait(e, 0)
                for s in range(2):
                    lo_done.wait(e, self.base + s)
                    for n in range(4):
                        if s == 1:
                            self.e.wait(e, n)
                        for k in range(2):
                            mm = mm3(e, ps[:, n, :], blk(slab(self.base + s), 2 * n + k), (ph[:, k, :], pl[:, k, :]),
                                     k == 0, k == 1)
                    mm.then_inc(used.sem, 1)

                self.xn.wait(e, KD - 1)

                def mms(j, i, hi, lo):
                    self.y.wait(e, RAW * i + j - 4)
                    self.e.wait(e, KD - 1)
                    return dense(e, ps[:, j, :], (hi, lo), (xnh, xnl), TL)
                ring_pe(e, self.base + 2, KD, mms)

            def pool(self, e):
                e.dma_start(p_raw[:], d["pT"]).then_inc(s_pload, 16)

            def act(self, e):
                e.wait_ge(s_pload, 16)
                e.activation(ph[:], p_raw[:], ACT.Copy).then_inc(self.p_hi.sem, 1)
                for s in range(2):
                    used.wait(e, self.base + s)
                    for n in range(4):
                        e.activation(e_sb[:, 4 * s + n, :], ps[:, n, :], ACT.Copy).then_inc(self.e.sem, 1)
                    split_hi(e, self.base + s + HL)

                def evac(j, i):
                    n = RAW * i + j
                    self.y.wait(e, n - 2)
                    e.activation(sg[:, j % 2, :], ps[:, j, :], ACT.Sigmoid).then_inc(self.sg.sem, 1)
                ring_act(e, self.base + 2, KD, evac)

            def dve(self, e):
                self.p_hi.wait(e, 0)
                e.tensor_tensor(pl[:], p_raw[:], ph[:].bitcast(F32), ALU.subtract).then_inc(self.p_lo.sem, 1)
                for s in range(2):
                    used.wait(e, self.base + s)
                    split_lo(e, self.base + s + HL)
                self.e.wait(e, KD - 1)

                def evac(j, i):
                    n = RAW * i + j
                    self.sg.wait(e, n)
                    e.tensor_tensor(pn_hm["src"][:, bass.ds(n, 1), :].rearrange("p a t -> p (a t)"), sg[:, j % 2, :],
                                    e_sb[:, bass.ds(n, 1), :].rearrange("p a t -> p (a t)"), ALU.mult) \
                        .then_inc(self.y.sem, 1)
                ring_dve(e, self.base + 2, KD, evac)

        class LatentIn(Phase):
            def __init__(self, T, xn, key0, rotate, full):
                super().__init__()
                self.T, self.tt, self.xn, self.key0, self.rotate, self.full = T, T // P, xn, key0, rotate, full
                self.base = take("slabs", 7 if full else 2)
                self.first = 0 if full else 5
                self.fin_hi, self.fin = r["fin_hi"].span(self.tt if full else 0), r["fin"].span(self.tt if full else 0)
                self.cq = r["cq"].span(4 if full else 1)
                self.rot, self.kr = r["rot"].span(2 if rotate else 0), r["kr"].span(1)
                self.spread = take("krope", 1)

            def cq_ready(self, e, c):
                self.cq.wait(e, c if self.full else 0)

            def pe(self, e):
                T, acts = self.T, (xnh, xnl)
                self.xn.wait(e, KD - 1)
                for k in range(self.first, 7):
                    s = self.base + k - self.first
                    lo_done.wait(e, s)
                    w = slab(s)
                    if k < 2:
                        for t in range(self.tt):
                            for kb in range(4):
                                mm = mm3(e, ps[:, t, 0:256], tuple(a[:, 4 * k + kb, t * P:(t + 1) * P] for a in acts),
                                         blk(w, kb, 256), k == 0 and kb == 0, k == 1 and kb == 3)
                    elif k < 6:
                        mm = dense(e, ps[:, (5, 6, 7, 4)[k - 2], 0:T], w, acts, T)
                    else:
                        if self.full:
                            self.fin.wait(e, 0)
                        mm = dense(e, ps[:, 0, 0:T], w, acts, T)
                    mm.then_inc(used.sem, 1)

            def act(self, e):
                T = self.T
                for k in range(self.first, 7):
                    s = self.base + k - self.first
                    used.wait(e, s)
                    if k == 1:
                        for t in range(self.tt):
                            e.activation(finh[:, t, :], ps[:, t, 0:256], ACT.Copy).then_inc(self.fin_hi.sem, 1)
                    if 2 <= k < 6:
                        e.activation(cq[:, k - 2, 0:T], ps[:, (5, 6, 7, 4)[k - 2], 0:T], ACT.Copy).then_inc(self.cq.sem, 1)
                    split_hi(e, s + HL)

            def dve(self, e):
                T = self.T
                for k in range(self.first, 7):
                    s = self.base + k - self.first
                    used.wait(e, s)
                    if k == 1:
                        for t in range(self.tt):
                            self.fin_hi.wait(e, t)
                            e.tensor_tensor(finl[:, t, :], ps[:, t, 0:256], finh[:, t, :].bitcast(F32),
                                            ALU.subtract).then_inc(self.fin.sem, 1)
                    split_lo(e, s + HL)
                out = k2[64:96, 0, self.key0:self.key0 + T]
                if self.rotate:
                    rotary(e, out, 0, 0, T, self.rot, 0, self.kr)
                else:
                    e.tensor_copy(out, ps[64:96, 0, 0:T]).then_inc(self.kr.sem, 1)

            def pool(self, e):
                self.kr.wait(e, 0)
                src = k2[64:96, 0:1, self.key0:self.key0 + self.T].broadcast_to([32, MLA_H - 1, self.T])
                e.dma_start(k2[64:96, 1:MLA_H, self.key0:self.key0 + self.T], src).then_inc(s_krope, 16)

        def rotary(e, out, bank, slot, T, rot, n, done):
            e.tensor_tensor(rt2[64:96, slot, 0:T], ps[96:128, bank, 0:T], rope[96:128, 0:T], ALU.mult).then_inc(rot.sem, 1)
            e.tensor_tensor(out, ps[64:96, bank, 0:T], rope[64:96, 0:T], ALU.mult).then_inc(rot.sem, 1)
            rot.wait(e, n + 1)
            e.tensor_tensor(out, out, rt2[64:96, slot, 0:T], ALU.add).then_inc(done.sem, 1)

        class Fourier(Phase):
            def __init__(self, l, T, inp, nq, nkv):
                super().__init__()
                self.l, self.T, self.tt, self.inp, self.nq, self.nkv = l, T, T // P, inp, nq, nkv
                self.nd = 2 * self.tt * T // SLAB
                self.base = take("slabs", self.nd + 1)
                self.pq_hi, self.pq = r["pq_hi"].span(4), r["pq"].span(4)
                self.f_mm, self.f_hi, self.f = r["f_mm"].span(1), r["f_hi"].span(2), r["f"].span(2)
                self.four_hi, self.four = r["four_hi"].span(2), r["four"].span(2)

            def pe(self, e):
                T, tt = self.T, self.tt
                self.inp.fin.wait(e, tt - 1)
                self.inp.kr.wait(e, 0)
                for s in range(self.nd):
                    lo_done.wait(e, self.base + s)
                    w = slab(self.base + s)
                    for g in range(SLAB // T):
                        m, tb = divmod(s * (SLAB // T) + g, tt)
                        for c in range(2):
                            mm = mm3(e, ps[:, 2 * m + c, 0:T], tuple(f[:, tb, c * P:(c + 1) * P] for f in (finh, finl)),
                                     blk(w, g, T), tb == 0, tb == tt - 1)
                    mm.then_inc(used.sem, 1)
                self.inp.cq_ready(e, 3)
                self.nq.pe_stats(e)
                self.nkv.pe_stats(e)
                s = self.base + self.nd
                lo_done.wait(e, s)
                w = slab(s)
                self.pq.wait(e, 3)
                for c in range(2):
                    for m in range(2):
                        mm = mm3(e, ps[:, 5 + c, 0:T], blk(w, m), tuple(a[:, 2 * m + c, 0:T] for a in (pqh, pql)),
                                 m == 0, m == 1)
                mm.then_inc(self.f_mm.sem, 1)
                self.f.wait(e, 1)
                for n in range(2):
                    for k in range(2):
                        mm = mm3(e, ps[:, n, 0:T], blk(w, 2 + 2 * k + n), tuple(a[:, k, 0:T] for a in (fh, fl)),
                                 k == 0, k == 1)
                mm.then_inc(used.sem, 1)

            def act(self, e):
                T = self.T
                self.nq.act_squares(e)
                self.nkv.act_squares(e)
                for s in range(self.nd):
                    used.wait(e, self.base + s)
                    split_hi(e, self.base + s + HL)
                for c in range(4):
                    e.activation(pqh[:, c, 0:T], ps[:, c, 0:T], ACT.Copy).then_inc(self.pq_hi.sem, 1)
                self.nq.act_std(e)
                self.nkv.act_std(e)
                self.f_mm.wait(e, 0)
                for c in range(2):
                    e.activation(fh[:, c, 0:T], ps[:, 5 + c, 0:T], ACT.Copy).then_inc(self.f_hi.sem, 1)
                self.nq.act_hi(e)
                self.nkv.act_hi(e)
                used.wait(e, self.base + self.nd)
                for n in range(2):
                    e.activation(xnh[:, n, 0:T], ps[:, n, 0:T], ACT.Identity, bias=col(f"b_f{self.l}", n)) \
                        .then_inc(self.four_hi.sem, 1)
                split_hi(e, self.base + self.nd + HL)

            def pool(self, e):
                self.nq.pool_adds(e)
                self.nkv.pool_adds(e)

            def dve(self, e):
                T = self.T
                for s in range(self.nd):
                    used.wait(e, self.base + s)
                    split_lo(e, self.base + s + HL)
                for c in range(4):
                    self.pq_hi.wait(e, c)
                    e.tensor_tensor(pql[:, c, 0:T], ps[:, c, 0:T], pqh[:, c, 0:T].bitcast(F32),
                                    ALU.subtract).then_inc(self.pq.sem, 1)
                self.nq.dve_rstd(e)
                self.nkv.dve_rstd(e)
                for c in range(2):
                    self.f_hi.wait(e, c)
                    e.tensor_tensor(fl[:, c, 0:T], ps[:, 5 + c, 0:T], fh[:, c, 0:T].bitcast(F32),
                                    ALU.subtract).then_inc(self.f.sem, 1)
                self.nq.dve_tiles(e)
                self.nkv.dve_tiles(e)
                for n in range(2):
                    self.four_hi.wait(e, n)
                    e.scalar_tensor_tensor(out=xnl[:, n, 0:T], in0=ps[:, n, 0:T], scalar=col(f"b_f{self.l}", n),
                                           in1=xnh[:, n, 0:T].bitcast(F32), op0=ALU.add,
                                           op1=ALU.subtract).then_inc(self.four.sem, 1)
                split_lo(e, self.base + self.nd + HL)

        class NormOnly(Phase):
            def __init__(self, norm, ready):
                super().__init__()
                self.norm, self.ready = norm, ready

            def act(self, e):
                self.norm.act_squares(e)
                self.norm.act_std(e)
                self.norm.act_hi(e)

            def pe(self, e):
                self.norm.pe_stats(e)

            def dve(self, e):
                self.norm.dve_rstd(e)
                self.norm.dve_tiles(e)

        class QProj(Phase):
            def __init__(self, T, norm, rotate, four):
                super().__init__()
                self.T, self.norm, self.rotate, self.four = T, norm, rotate, four
                self.base = take("slabs", MLA_H // 2)
                self.a = r["ev_a"].span(MLA_H)
                self.v = r["ev_d"].span(MLA_H if rotate else 0)
                self.rot = r["rot"].span(2 * MLA_H if rotate else 0)

            def pe(self, e):
                T = self.T
                self.norm.out.wait(e, 2)
                self.four.four.wait(e, 1)
                for s in range(MLA_H // 2):
                    lo_done.wait(e, self.base + s)
                    for hh in range(2):
                        h = 2 * s + hh
                        if h >= 4:
                            self.a.wait(e, h - 4)
                            if self.rotate:
                                self.v.wait(e, h - 4)
                        for k in range(3):
                            mm = mm3(e, ps[:, h % 4, 0:T], blk(slab(self.base + s), 3 * hh + k),
                                     (cnh[:, k, 0:T], cnl[:, k, 0:T]), k == 0, k == 2)
                    mm.then_inc(used.sem, 1)

            def act(self, e):
                T = self.T
                n = NOPE if self.rotate else NOPE + ROPE
                for s in range(MLA_H // 2):
                    used.wait(e, self.base + s)
                    for h in (2 * s, 2 * s + 1):
                        e.activation(q2[0:n, h, 0:T], ps[0:n, h % 4, 0:T], ACT.Copy).then_inc(self.a.sem, 1)
                    split_hi(e, self.base + s + HL)

            def dve(self, e):
                T = self.T
                for s in range(MLA_H // 2):
                    used.wait(e, self.base + s)
                    if self.rotate:
                        for h in (2 * s, 2 * s + 1):
                            if h >= 2:
                                self.v.wait(e, h - 2)
                            rotary(e, q2[64:96, h, 0:T], h % 4, h % 2, T, self.rot, 2 * h, self.v)
                    split_lo(e, self.base + s + HL)

        class KVProj(Phase):
            def __init__(self, T, norm, key0, after=None):
                super().__init__()
                self.T, self.tt, self.norm, self.key0, self.after = T, T // P, norm, key0, after
                self.base = take("slabs", 2)
                n = MLA_H // 2 + self.tt
                self.vt = r["vt"].span(self.tt)
                self.a, self.v = r["ev_a"].span(n), r["ev_d"].span(n)

            def pe(self, e):
                T = self.T
                self.norm.out.wait(e, 0)
                if self.after is not None:
                    self.after.a.wait(e, MLA_H - 1)
                    if self.after.rotate:
                        self.after.v.wait(e, MLA_H - 1)
                lo_done.wait(e, self.base)
                for p_ in range(MLA_H // 2):
                    if p_ >= 4:
                        self.a.wait(e, p_ - 4)
                        self.v.wait(e, p_ - 4)
                    mm = mm3(e, ps[:, p_ % 4, 0:T], blk(slab(self.base), p_), (cnh[:, 3, 0:T], cnl[:, 3, 0:T]), True, True)
                    if p_ == 3:
                        mm.then_inc(self.vt.sem, 1)
                mm.then_inc(used.sem, 1)
                lo_done.wait(e, self.base + 1)
                w = slab(self.base + 1)
                for t in range(self.tt):
                    last = MLA_H // 2 + t - 2 if t >= 2 else (5 if t == 0 else 3)
                    self.a.wait(e, last)
                    self.v.wait(e, last)
                    act = tuple(c[:, 3, t * P:(t + 1) * P] for c in (cnh, cnl))
                    mm3(e, ps[:, 2 * (t % 2), :], act, tuple(a[:, 0:512] for a in w), True, True)
                    mm = mm3(e, ps[:, 2 * (t % 2) + 1, 0:256], act, tuple(a[:, 512:768] for a in w), True, True)
                    mm.then_inc(self.vt.sem if t < self.tt - 1 else used.sem, 1)

            def act(self, e):
                T, k0 = self.T, self.key0
                for p_ in range(MLA_H // 2):
                    if p_ == 0:
                        self.vt.wait(e, 0)
                    if p_ == 4:
                        used.wait(e, self.base)
                    e.activation(k2[0:HD, 2 * p_, k0:k0 + T], ps[0:HD, p_ % 4, 0:T], ACT.Copy).then_inc(self.a.sem, 1)
                split_hi(e, self.base + HL)
                for t in range(self.tt):
                    self.tile_ready(e, t)
                    e.activation(v2[:, k0 // P + t, 0:512], ps[:, 2 * (t % 2), :], ACT.Copy).then_inc(self.a.sem, 1)
                split_hi(e, self.base + 1 + HL)

            def tile_ready(self, e, t):
                if t < self.tt - 1:
                    self.vt.wait(e, t + 1)
                else:
                    used.wait(e, self.base + 1)

            def dve(self, e):
                T, k0 = self.T, self.key0
                for p_ in range(MLA_H // 2):
                    if p_ == 0:
                        self.vt.wait(e, 0)
                    if p_ == 4:
                        used.wait(e, self.base)
                    e.tensor_copy(k2[0:HD, 2 * p_ + 1, k0:k0 + T], ps[HD:P, p_ % 4, 0:T]).then_inc(self.v.sem, 1)
                split_lo(e, self.base + HL)
                for t in range(self.tt):
                    self.tile_ready(e, t)
                    e.tensor_copy(v2[:, k0 // P + t, 512:768], ps[:, 2 * (t % 2) + 1, 0:256]).then_inc(self.v.sem, 1)
                split_lo(e, self.base + 1 + HL)

        class Final(Phase):
            def __init__(self, ready):
                super().__init__()
                self.norm = Norm([x[:, n, :] for n in range(KD)], ready, TL, D, nt, lambda n: col("g_final", n),
                                 plain=yout)

            def act(self, e):
                self.norm.act_squares(e)
                self.norm.act_std(e)
                for n in range(KD):
                    self.norm.out.wait(e, n)
                    e.dma_start(d["out"][:, n, :], yout[:, n, :]).then_inc(s_out, 16)
                e.wait_ge(s_out, 16 * KD)

            def pool(self, e):
                self.norm.pool_adds(e)

            def pe(self, e):
                self.norm.pe_stats(e)

            def dve(self, e):
                self.norm.dve_rstd(e)
                self.norm.dve_plain(e)

        def latent_mixer(l, st, x_ready):
            T, xs, key0 = ((TL, x, 0), (TC, cx, TL))[st]
            full = st == 0 or l == 0
            pre = PreNorm((xs, T), x_ready, lambda n: gains[:, l, st, 0, n:n + 1], lambda n: mod[:, l, n, st:st + 1])
            inp = LatentIn(T, pre.out, key0, st == 0, full)
            zero = lambda n: col("zero", n)
            nkv = lambda: Norm([cq[:, 3, 0:T]], lambda e, n: inp.cq_ready(e, 3), T, P, nt2, lambda n: col(f"g_kv{l}", n),
                               zero, (cnh[:, 3:4, :], cnl[:, 3:4, :]), bank=7)
            if full:
                nq = Norm([cq[:, c, 0:T] for c in range(3)], lambda e, n: inp.cq_ready(e, n), T, 3 * P, nt,
                          lambda n: col(f"g_q{l}", n), zero, (cnh, cnl))
                nk = nkv()
                four = Fourier(l, T, inp, nq, nk)
                qp = QProj(T, nq, st == 0, four)
            else:
                nk = nkv()
                NormOnly(nk, None)
                qp = None
            kv = KVProj(T, nk, key0, qp)
            count["krope_done"] = inp.spread + 1
            if not full:
                return None
            spread = inp.spread + 1

            def ready(e):
                kv.a.wait(e, MLA_H // 2 + kv.tt - 1)
                kv.v.wait(e, MLA_H // 2 + kv.tt - 1)
                e.wait_ge(s_krope, 16 * spread)
            keys = (lambda qt: list(range(6))) if st == 0 else (lambda qt: [0, 1])
            att = Attention(MLA_H, T // P, keys, q2, k2, v2, qst2, p2, pt2, mix2, 96, MLA_SCALE, ready,
                            kslot=lambda b, par: 2 * b + par, key0=0 if st == 0 else TL, vt0=0 if st == 0 else 4,
                            dsplit=512 if st == 0 else 0)
            turn = MixTurn(mix2, 6, T // P, (xnh, xnl), 2, lambda e: att.o.wait(e, MLA_H - 1), None)

            def mixed(e):
                four.four.wait(e, 1)
                turn.out.wait(e, 5)
            role_x = ("x", "cx")[st]
            out = OutProj(T, (xnh, xnl), mixed, (xs, T), lambda n: mod[:, l, bass.ds(16 + n, 1), st],
                          role_x)
            return out.out

        def latent_ffn(l, st, x_done):
            T, xs = ((TL, x), (TC, cx))[st]
            pre = PreNorm((xs, T), lambda e, n: x_done.wait(e, n), lambda n: gains[:, l, st, 1, n:n + 1],
                          lambda n: mod[:, l, 24 + n, st:st + 1])
            gu = GateUp(T, pre.out, conv=l)
            down = Down(T, gu, (xs, T), lambda n: mod[:, l, 40 + n, st:st + 1], ("x", "cx")[st])
            return down.out

        setup = Setup()
        tables_view = d["tables"]
        strips_view = bass.AP(tables_view.tensor, 0, [[NTAB, 16], [1, P], [1, TL]])
        after = lambda sp: (lambda e, n: sp.wait(e, n))

        x1, _ = ffn_block1(None, "ffn1_pre_g", "ffn1_post_g", 0, lambda e, n: e.wait_ge(s_setup, 16 * Setup.LOADS))

        pre = PreNorm((x, TL), after(x1), lambda n: col("attn_pre_g", n), lambda n: col("zero", n))
        proj = InProj1(pre.out)

        def qkv_ready(e):
            proj.a.wait(e, 12)
            proj.v.wait(e, 17)
        att_a = Attention(8, 4, lambda qt: [qt - 1, qt] if qt else [0], q1, k1, v1, qst1, p1, pt1, mix1, HD, 1.0,
                          qkv_ready, kslot=lambda b, par: b, bias=True)
        att_b = Attention(8, 4, lambda qt: list(range(qt + 1)), q1, k1, v1, qst1, p1, pt1, mix1, HD, 1.0,
                          qkv_ready, q0=8, kslot=lambda b, par: 4 + 2 * b + par, mix0=512, bias=True, head0=8)
        turn1 = MixTurn(mix1, 8, 4, (m1h, m1l), 0, lambda e: att_b.o.wait(e, 7), None)
        outp = OutProj(TL, (m1h, m1l), lambda e: turn1.out.wait(e, 7))
        post = PostNorm([pn_hm["src"][:, n, :] for n in range(KD)], after(outp.out), pn_hm,
                        lambda n: col("attn_post_g", n), False)

        x2, _ = ffn_block1(None, "ffn2_pre_g", "ffn2_post_g", 1, after(post.out))

        pre = PreNorm((x, TL), after(x2), lambda n: col("ple_pre_g", n), lambda n: col("zero", n))
        emb = Embed(pre.out)
        post = PostNorm([pn_hm["src"][:, n, :] for n in range(KD)], after(emb.y), pn_hm,
                        lambda n: col("ple_post_g", n), False)

        x_now = post.out
        c1 = latent_mixer(0, 1, lambda e, n: None)
        x_mix = latent_mixer(0, 0, after(x_now))
        x_now = latent_ffn(0, 0, x_mix)
        c2 = latent_ffn(0, 1, c1)
        latent_mixer(1, 1, after(c2))
        x_mix = latent_mixer(1, 0, after(x_now))
        x_now = latent_ffn(1, 0, x_mix)
        Final(after(x_now))
        take("slabs", HL)
        assert count["slabs"] == d["n_slabs"], count

        block = ctx.enter_context(nc.Block())

        @block.sync
        def _(e):
            at = 0

            def main(n):
                nonlocal at
                b = at
                units(e, n, RAW, lambda j, i: load(e, b + j, i))
                at += n

            def ada_load(a0, i):
                v = a0 + RAW * i - RAW + 1
                if not isinstance(v, int) or v > 0:
                    e.wait_ge(r["ada_used"].sem, v)
                e.dma_start(ada_raw[:, a0 % RAW, :], d["wa"][bass.ds(a0 + RAW * i, 1)].rearrange("a p n -> (a p) n")) \
                    .then_inc(ada_full[a0 % RAW], 16)

            for g in [ph_ for ph_ in phases if isinstance(ph_, GateUp) and ph_.ada is not None]:
                main(g.base - at)
                main(RAW)
                for a in range(RAW):
                    ada_load(g.abase + a, 0)

                def both(j, i):
                    load(e, g.base + RAW + j, i)
                    ada_load(g.abase + RAW + j, i)
                units(e, 2 * KF - RAW, RAW, both)
                at += 2 * KF - RAW
                for a in range(2 * KF, NMOD):
                    ada_load(g.abase + a, 0)
            main(count["slabs"] - at)

        @block.tensor
        def _(e):
            for ph_ in phases:
                ph_.pe(e)

        @block.scalar
        def _(e):
            for ph_ in phases:
                ph_.act(e)

        @block.vector
        def _(e):
            for ph_ in phases:
                ph_.dve(e)

        @block.gpsimd
        def _(e):
            for ph_ in phases:
                ph_.pool(e)


def slabs_by_column(w):
    k, n = w.shape
    return w.reshape(k // P, P, n // P, P).transpose(2, 1, 0, 3).reshape(n // P, P, -1)


def gate_up_slabs(w):
    s = slabs_by_column(w)
    return np.stack([s[:KF], s[KF:]], axis=1).reshape(2 * KF, P, SLAB)


def down_slabs(w):
    a = w.reshape(KF // 2, 2, P, 2, 4 * P)
    return a.transpose(3, 0, 2, 1, 4).reshape(KF, P, SLAB)


def pad(a):
    return np.concatenate([a, np.zeros((P, SLAB - a.shape[1]), a.dtype)], axis=1)[None]


def latent_slabs(i, l, st, full):
    T = (TL, TC)[st]
    w = i["w_in_2"][l]
    out = []
    kr = w[:, 768:800]
    swapped = np.concatenate([kr[:, 16:], kr[:, :16]], axis=1)
    kr = slabs_by_column(np.concatenate([kr, swapped, kr, swapped], axis=1))
    if full:
        out.append(w[:, :256].reshape(2, 4, P, 256).transpose(0, 2, 1, 3).reshape(2, P, SLAB))
        out.append(slabs_by_column(w[:, 256:640]))
    out += [slabs_by_column(w[:, 640:768]), kr]
    if full:
        out.append(dft_slabs(T))
        wf = i["w_fourier_2"][l].reshape(2, P, 2, P).transpose(1, 0, 2, 3).reshape(P, 512)
        out.append(pad(np.concatenate([*channel_dft(T), wf], axis=1)))
        q = i["w_q_b_2"][l].reshape(3, P, MLA_H, 96)
        q = np.concatenate([q, q[..., 80:], q[..., 64:80]], axis=3)
        for s in range(MLA_H // 2):
            out.append(pad(q[:, :, 2 * s:2 * s + 2].transpose(1, 2, 0, 3).reshape(P, 768)))
    kv = i["w_kv_b_2"][l].reshape(P, MLA_H, 2, HD)
    out += [pad(kv[:, :, 0].reshape(P, 768)), pad(kv[:, :, 1].reshape(P, 768))]
    if full:
        out.append(slabs_by_column(i["w_out_2"][l]))
    return out


def weight_stream(i):
    a_kv, b0 = 512, 768
    w = i["w_in"][0]
    out = [gate_up_slabs(i["ffn1_w_gu"][0]), down_slabs(i["ffn1_w_down"][0])]
    order = [w[:, 0:512], w[:, b0:b0 + 512], w[:, a_kv:a_kv + 128], w[:, b0 + 512:b0 + 1024], w[:, a_kv + 128:b0],
             w[:, b0 + 1024:]]
    out += [slabs_by_column(np.concatenate(order, axis=1)), slabs_by_column(i["w_out"][0])]
    out += [gate_up_slabs(i["ffn2_w_gu"][0]), down_slabs(i["ffn2_w_down"][0])]
    proj = i["w_ple_proj"][0].reshape(2, P, 2, 4, P).transpose(2, 1, 3, 0, 4).reshape(2, P, SLAB)
    out += [proj, slabs_by_column(i["w_ple_gate"][0])]
    ffn = lambda l: [gate_up_slabs(i["w_up_2"][l]), down_slabs(i["w_down_2"][l])]
    out += latent_slabs(i, 0, 1, True) + latent_slabs(i, 0, 0, True) + ffn(0) + ffn(0)
    out += latent_slabs(i, 1, 1, False) + latent_slabs(i, 1, 0, True) + ffn(1)
    out.append(np.zeros((HL, P, SLAB), np.float32))
    return np.concatenate(out)


def column_table(i):
    t = np.zeros((P, COLS.n), np.float32)

    def put(name, v):
        c = COLS.at[name]
        t[:, c:c + v.size // P] = v.reshape(-1, P).T
    for n in ("ffn1_pre_g", "ffn1_post_g", "attn_pre_g", "b_out", "attn_post_g", "ffn2_pre_g", "ffn2_post_g",
              "ple_pre_g", "ple_post_g"):
        put(n, i[n][0])
    put("g_final", i["g_final_2"])
    b = i["b_in"][0]
    put("b_in", np.concatenate([b[0:512], b[768:1280], b[512:640], b[1280:1792], b[640:768], b[1792:]]))
    for l in range(2):
        for n, v in (("b_ada", "b_ada_2"), ("g_mix", "g_mix_2"), ("b_f", "b_fourier_2"), ("g_q", "g_q_a_2"),
                     ("g_kv", "g_kv_a_2"), ("g_ffn", "g_ffn_2"), ("b_dw", "b_dw_2")):
            put(f"{n}{l}", i[v][l])
        for k in range(3):
            put(f"w_dw{k}{l}", i["w_dw_2"][l, k])
    return t


def feature_major(a):
    return a.T.reshape(-1, P, a.shape[0]).transpose(1, 0, 2)


def kernel(**inputs):
    import concourse.bacc as bacc
    from concourse.bass_utils import run_bass_kernel_spmd

    i = {k: np.asarray(v) for k, v in inputs.items()}
    arrays = {
        "ws": weight_stream(i),
        "wa": np.concatenate([slabs_by_column(i["w_ada_2"][l]) for l in range(2)]),
        "cols": column_table(i),
        "xT": feature_major(i["x"][0]),
        "ctxT": feature_major(i["ctx_2"][0]),
        "pT": feature_major(i["p"][0, 0]),
        "cT": np.stack([i["c_2"][0].reshape(KD, P).T, i["c_ctx_2"].reshape(KD, P).T], axis=2),
        "rel_bias": i["rel_bias"],
        "sinks": i["sinks"][0],
        "no_sinks": np.full(8, NEG, np.float32),
        "b_in": i["b_in"][0],
        "onehot": bucket_tables(),
        "ident": np.eye(P, dtype=np.float32),
        "flip": np.eye(P, dtype=np.float32)[::-1],
        "rope": rope_table(),
    }
    arrays = {f"in_{k}_dram": np.ascontiguousarray(v) for k, v in arrays.items()}
    nc = bacc.Bacc("TRN2", target_bir_lowering=False, num_devices=1)
    d = {k[3:-5]: nc.dram_tensor(k, v.shape, mybir.dt.from_np(v.dtype), kind="ExternalInput").ap()
         for k, v in arrays.items()}
    d["n_slabs"] = arrays["in_ws_dram"].shape[0]
    d["tables"] = nc.dram_tensor("tables", (2, 8, NTAB), F32).ap()
    d["out"] = nc.dram_tensor("out_0_dram", (P, KD, TL), F32, kind="ExternalOutput").ap()
    build(nc, d)
    res = run_bass_kernel_spmd(nc, [arrays], core_ids=[0])
    out = res.results[0]["out_0_dram"]
    return np.ascontiguousarray(out.transpose(1, 0, 2).reshape(D, TL).T)[None]
```

```python
from contextlib import ExitStack
import math

import numpy as np
import concourse.bass as bass
from concourse import mybir

F32 = mybir.dt.float32
F32R = mybir.dt.float32r
ALU = mybir.AluOpType
ACT = mybir.ActivationFunctionType
AX_X = mybir.AxisListType.X

P = 128
D = 1024
KD = D // P
TL, TC = 512, 256
DFF = 2816
KF = DFF // P
SLAB = 8 * P
RAW = 2
HL = 4
BODY = 4
HD = 64
N_BUCKETS = 32
NTAB = 640
NEG = -1e30
EPS = 1e-6
MLA_H, NOPE, ROPE = 12, 64, 32
MLA_SCALE = (NOPE + ROPE) ** -0.5
NMOD = 48


def bucket_tables():
    dist = 511 - np.arange(NTAB)
    n = np.maximum(dist, 0)
    nf = np.maximum(n, 1).astype(np.float32)
    half = N_BUCKETS // 2
    large = half + (np.log(nf / np.float32(half)) / np.float32(math.log(2048 / half))
                    * np.float32(N_BUCKETS - half)).astype(np.int32)
    bucket = np.where(n < half, n, np.minimum(large, N_BUCKETS - 1))
    t = np.zeros((N_BUCKETS + 1, 2, NTAB), np.float32)
    t[bucket, :, np.arange(NTAB)] = 1.0
    count = (dist <= 128).astype(int) + (dist % 4 == 0) + (dist % 16 == 0)
    t[N_BUCKETS, 0] = np.where((dist >= 0) & (dist <= 127), 0.0, NEG)
    t[N_BUCKETS, 1] = np.where((dist >= 0) & (count > 0), np.log(np.maximum(count, 1)), NEG)
    return t


def rope_table():
    t = np.arange(TL)
    freq = (10000.0 ** (-np.arange(8, dtype=np.float32) / 8)).astype(np.float32)
    ang = np.concatenate([(t // 64)[None, :] * freq[:, None], (t % 64)[None, :] * freq[:, None]]).astype(np.float32)
    out = np.zeros((P, TL), np.float32)
    out[64:96] = np.concatenate([np.cos(ang), np.cos(ang)])
    out[96:128] = np.concatenate([-np.sin(ang), np.sin(ang)])
    return out


def dft_slabs(n):
    ang = 2 * np.pi * (np.outer(np.arange(n), np.arange(n)) % n) / n
    mats = [m.astype(np.float32).reshape(n // P, P, n).transpose(1, 0, 2).reshape(P, -1) for m in (np.cos(ang), np.sin(ang))]
    return np.concatenate(mats, axis=1).reshape(P, -1, SLAB).transpose(1, 0, 2)


def channel_dft(n):
    ang = 2 * np.pi * (np.outer(np.arange(64), np.arange(64)) % 64) / 64
    s = 1.0 / math.sqrt(n * 64)
    out = np.zeros((2, P, P), np.float32)
    for g in (0, 64):
        out[0, g:g + 64, g:g + 64] = np.cos(ang) * s
        out[1, g:g + 64, g:g + 64] = -np.sin(ang) * s
    return out


class Cols:
    def __init__(self):
        self.at, self.n = {}, 0

    def add(self, name, tiles):
        self.at[name] = self.n
        self.n += tiles


COLS = Cols()
for _n in ("ffn1_pre_g", "ffn1_post_g", "attn_pre_g", "b_out", "attn_post_g", "ffn2_pre_g", "ffn2_post_g",
           "ple_pre_g", "ple_post_g", "zero", "g_final"):
    COLS.add(_n, KD)
COLS.add("b_in", 18)
for _l in range(2):
    for _n, _k in (("b_ada", NMOD), ("g_mix", KD), ("b_f", 2), ("g_q", 3), ("g_kv", 1), ("g_ffn", KD),
                   ("w_dw0", 2 * KF), ("w_dw1", 2 * KF), ("w_dw2", 2 * KF), ("b_dw", 2 * KF)):
        COLS.add(f"{_n}{_l}", _k)


class Role:
    def __init__(self, sem, primed=0):
        self.sem, self.n, self.primed = sem, primed, primed

    def span(self, units):
        s = Span(self.sem, self.n)
        self.n += units
        return s


class Span:
    def __init__(self, sem, base):
        self.sem, self.base = sem, base

    def wait(self, e, k):
        v = self.base + k + 1
        if not isinstance(v, int) or v > 0:
            e.wait_ge(self.sem, v)


def units(e, n, body, fn):
    full = n // body if n // body >= 2 else 0
    if full:
        with e.Fori(0, full) as i:
            for j in range(body):
                fn(j, i)
    for k in range(full * body, n):
        fn(k % body, k // body)


def skewed(e, bodies, size, stages):
    def step(b, j, lo, hi):
        for lag, fn in stages:
            back = 0
            jj = j - lag
            while jj < 0:
                jj += size
                back += 1
            if lo is not None and b - back < lo:
                continue
            if hi is not None and b - back >= hi:
                continue
            fn(b - back if back else b, jj)

    assert max(lag for lag, _ in stages) <= size
    for j in range(size):
        step(0, j, 0, bodies)
    if bodies > 1:
        with e.Fori(1, bodies) as i:
            for j in range(size):
                step(i, j, None, None)
    for j in range(max(lag for lag, _ in stages)):
        step(bodies, j, 0, bodies)


def build(nc, d):
    ctx = ExitStack()
    with ctx:
        base0 = 16512
        top = 229344
        place = {"next": base0}

        def sb(name, shape, dt=F32, at=None):
            size = int(np.prod(shape[1:])) * 4
            if at is None:
                at = place["next"]
                place["next"] += (size + 31) // 32 * 32
                assert place["next"] <= top, name
            return nc.alloc_sbuf_tensor_at(name, shape, dt, offset=at)

        KB = 1024
        cols = sb("cols", [P, COLS.n])
        rope = sb("rope", [P, TL])
        ident = sb("ident", [P, P])
        flip = sb("flip", [P, P])
        ones = sb("ones", [P, P])
        mod = sb("mod", [P, 2, NMOD, 2])
        gains = sb("gains", [P, 2, 2, 2, KD])
        silu_c = sb("silu_c", [P, KD, 2])
        c_raw = sb("c_raw", [P, KD, 2])
        sinks = sb("sinks", [P, 16])
        rel = sb("rel", [N_BUCKETS + 1, 16])
        small = sb("small", [P, 64])
        rinv = sb("rinv", [P, 8])
        eps = sb("eps", [P, 2])
        qb8 = sb("qb8", [P, 8])
        x = sb("x", [P, KD, TL])
        cx = sb("cx", [P, KD, TC])
        raw = sb("raw", [P, RAW, SLAB])
        whi = sb("whi", [P, HL, SLAB], F32R)
        wlo = sb("wlo", [P, HL, SLAB], F32R)
        AR = place["next"]
        ada_raw = sb("ada_raw", [P, 2, SLAB])
        XN = place["next"]
        xnh = sb("xnh", [P, KD, TL], F32R)
        xnl = sb("xnl", [P, KD, TL], F32R)
        HM = place["next"]
        hmh = sb("hmh", [P, KF, TL], F32R)
        hml = sb("hml", [P, KF, TL], F32R)
        SH = place["next"]
        sil = sb("sil", [P, TL])
        hbuf = sb("hbuf", [P, 2, TL])
        yg = sb("yg", [P, 2, TL], at=AR)
        yv = sb("yv", [P, 2, TL], at=AR + 4 * KB)
        rstd = sb("rstd", [P, TL], at=SH)
        tmp = sb("tmp", [P, 2, TL], at=SH + 2 * KB)
        nt = dict(sq=sb("nt_sq", [P, 4, TL], at=HM + 60 * KB), rstd=rstd, tmp=tmp)
        fsb = sb("fsb", [P, 4, TL], at=XN)
        pn_ffn = dict(sq=sb("pf_sq", [P, 4, TL], at=XN + 8 * KB), rstd=rstd, tmp=tmp)
        pn_hm = dict(sq=sb("ph_sq", [P, 4, TL], at=HM + 48 * KB), rstd=rstd, tmp=tmp)
        f_hm = sb("f_hm", [P, KD, TL], at=HM + 72 * KB)
        nt2 = {k: sb("nt2_" + k, s, at=HM + o * KB) for k, s, o in
               (("sq", [P, 1, TL], 68), ("rstd", [P, TL], 70), ("tmp", [P, 1, TL], 86))}
        onehot = sb("onehot", [N_BUCKETS + 1, 2, NTAB], at=HM)
        tab = sb("tab", [8, 4, NTAB // 2], at=HM + 8 * KB)
        q1 = sb("q1", [HD, 16, TL], at=HM)
        k1 = sb("k1", [HD, 12, TL], at=HM + 32 * KB)
        v1 = sb("v1", [P, 4, 12 * HD], at=HM + 56 * KB)
        qst1 = sb("qst1", [HD, 2, TL], at=HM + 68 * KB)
        strip = sb("strip", [P, 2, TL], at=HM + 72 * KB)
        p1 = sb("p1", [P, 2, TL], at=HM + 76 * KB)
        pt1 = sb("pt1", [P, 2, TL], at=HM + 80 * KB)
        vt1 = sb("vt1", [P, 2, TL], at=HM + 84 * KB)
        mix1 = sb("mix1", [P, 4, 2 * TL], at=XN)
        m1h = sb("m1h", [P, KD, TL], F32R, at=HM)
        m1l = sb("m1l", [P, KD, TL], F32R, at=HM + 16 * KB)
        sg = sb("sg", [P, KD, TL], at=HM)
        p_raw = sb("p_raw", [P, 2, TL], at=HM + 36 * KB)
        ph = sb("ph", [P, 2, TL], F32R, at=HM + 40 * KB)
        pl = sb("pl", [P, 2, TL], F32R, at=HM + 44 * KB)
        q2 = sb("q2", [96, MLA_H, TL], at=HM)
        k2 = sb("k2", [96, MLA_H, TL + TC], at=HM + 24 * KB)
        v2 = sb("v2", [P, 6, MLA_H * HD], at=HM + 60 * KB)
        qst2 = sb("qst2", [96, 2, TL], at=HM + 78 * KB)
        p2 = sb("p2", [P, 2, TL + TC], at=HM + 82 * KB)
        pt2 = sb("pt2", [P, 2, TL + TC], at=SH)
        mix2 = sb("mix2", [P, 4, MLA_H * HD], at=XN + 4 * KB)
        m2h = sb("m2h", [P, 6, TL], F32R, at=HM)
        m2l = sb("m2l", [P, 6, TL], F32R, at=HM + 12 * KB)
        rt2 = sb("rt2", [96, 2, TL], at=XN + 12 * KB)
        finh = sb("finh", [P, 4, 256], F32R, at=HM)
        finl = sb("finl", [P, 4, 256], F32R, at=HM + 4 * KB)
        fh = sb("fh", [P, 2, TL], F32R, at=HM)
        fl = sb("fl", [P, 2, TL], F32R, at=HM + 4 * KB)
        pqh = sb("pqh", [P, 4, TL], F32R, at=HM + 8 * KB)
        pql = sb("pql", [P, 4, TL], F32R, at=HM + 16 * KB)
        cq = sb("cq", [P, 4, TL], at=HM + 78 * KB)
        cnh = sb("cnh", [P, 4, TL], F32R, at=XN + 4 * KB)
        cnl = sb("cnl", [P, 4, TL], F32R, at=XN + 20 * KB)
        yout = sb("yout", [P, KD, TL], at=XN)

        ps = ctx.enter_context(nc.psum_tensor("ps", [P, 8, TL], F32))

        def sem(name):
            return ctx.enter_context(nc.semaphore(name))

        def role(name, primed=0):
            return Role(sem(name), primed)

        s_setup = sem("setup_loads")
        s_out = sem("output_stores")
        s_tab = sem("bias_table_stored")
        s_pload = sem("p_loaded")
        s_krope = sem("krope_spread")
        raw_full = [sem(f"raw_full{i}") for i in range(RAW)]
        ada_full = [sem(f"ada_full{i}") for i in range(2)]
        strip_full = [sem(f"strip_full{i}") for i in range(2)]
        count = {"slabs": 0, "ada": 0, "strips": 0, "krope": 0}
        r = {}
        for name, primed in (
                ("slab_hi", 0), ("slab_lo", 0), ("slab_used", 0), ("ada_used", 0), ("mod", 0), ("gain", 0),
                ("const", 0), ("silu_c", 0), ("tab_mm", 0), ("tab_sb", 0),
                ("sil", 0), ("h", 2), ("h_hi", 0), ("h_lo", 2), ("yg", 0), ("yv", 0), ("cg", 0), ("cv", 0),
                ("x", 0), ("xp", 0), ("cx", 4), ("fsb", 0), ("sq", 0), ("acc", 0), ("ss", 0), ("std", 0), ("rstd", 0),
                ("tmp", 0), ("xn_hi", 0), ("xn", 0), ("upd", 0), ("ev_a", 4), ("ev_d", 4),
                ("qst", 0), ("S", 0), ("mx", 0), ("negm", 0), ("exp", 0), ("es", 0), ("tot", 0), ("rinv", 0),
                ("PT", 0), ("cp_a", 0), ("cp_d", 0), ("pv", 0), ("o", 0),
                ("mt_mm", 0), ("mt_hi", 0), ("mt", 0), ("fin_hi", 0), ("fin", 0), ("pq_hi", 0), ("pq", 0),
                ("f_mm", 0), ("f_hi", 0), ("f", 0), ("four_hi", 0), ("four", 0), ("cq", 0), ("kr", 0),
                ("rot", 0), ("vt", 0), ("p_hi", 0), ("p_lo", 0), ("e", 0), ("sg", 4), ("y", 0), ("qb", 0), ("yout", 0)):
            r[name] = Role(sem(name), primed)

        def take(kind, n):
            b = count[kind]
            count[kind] += n
            return b

        def col(name, n=0):
            return cols[:, bass.ds(COLS.at[name] + n, 1)]

        hi_done, lo_done, used = r["slab_hi"].span(0), r["slab_lo"].span(0), r["slab_used"].span(0)

        def load(e, s0, i):
            lo_done.wait(e, s0 + BODY * i - RAW)
            e.dma_start(raw[:, s0 % RAW, :], d["ws"][bass.ds(s0 + BODY * i, 1)].rearrange("a p n -> (a p) n")) \
                .then_inc(raw_full[s0 % RAW], 16)

        def split_hi(e, s0, i=0):
            if isinstance(i, int) and s0 + BODY * i >= count["slabs"]:
                return
            e.wait_ge(raw_full[s0 % RAW], 16 * (s0 // RAW + 1) + 16 * (BODY // RAW) * i)
            used.wait(e, s0 + BODY * i - HL)
            e.activation(whi[:, s0 % HL, :], raw[:, s0 % RAW, :], ACT.Copy).then_inc(hi_done.sem, 1)

        def split_lo(e, s0, i=0):
            if isinstance(i, int) and s0 + BODY * i >= count["slabs"]:
                return
            hi_done.wait(e, s0 + BODY * i)
            e.tensor_tensor(wlo[:, s0 % HL, :], raw[:, s0 % RAW, :], whi[:, s0 % HL, :].bitcast(F32),
                            ALU.subtract).then_inc(lo_done.sem, 1)

        def slab(s0):
            return whi[:, s0 % HL, :], wlo[:, s0 % HL, :]

        def ring_act(e, base, n, evac=lambda j, i: None):
            def step(j, i):
                used.wait(e, base + BODY * i + j)
                evac(j, i)
                split_hi(e, base + j + HL, i)
            units(e, n, BODY, step)

        def ring_dve(e, base, n, evac=lambda j, i: None):
            def step(j, i):
                used.wait(e, base + BODY * i + j)
                evac(j, i)
                split_lo(e, base + j + HL, i)
            units(e, n, BODY, step)

        def ring_pe(e, base, n, mms):
            def step(j, i):
                lo_done.wait(e, base + BODY * i + j)
                mms(j, i, *slab(base + j)).then_inc(used.sem, 1)
            units(e, n, BODY, step)

        def mm3(e, out, a, b, start, stop):
            e.matmul(out, a[0], b[0], start=start, stop=False, skip_group_check=True)
            e.matmul(out, a[0], b[1], start=False, stop=False, skip_group_check=True)
            return e.matmul(out, a[1], b[0], start=False, stop=stop, skip_group_check=True)

        def blk(pair, b, n=P):
            return tuple(w[:, b * n:(b + 1) * n] for w in pair)

        def dense(e, out, w, acts, T, kb=KD, wait_k=None):
            for k in range(kb):
                if wait_k is not None:
                    wait_k(k)
                act = acts[k] if isinstance(acts, list) else tuple(a[:, k, 0:T] for a in acts)
                mm = mm3(e, out, blk(w, k), act, k == 0, k == kb - 1)
            return mm

        phases = []

        class Phase:
            def __init__(self):
                phases.append(self)

            def pe(self, e): pass
            def act(self, e): pass
            def dve(self, e): pass
            def pool(self, e): pass

        class Setup(Phase):
            LOADS = 11

            def __init__(self):
                super().__init__()
                self.const = r["const"].span(4)
                self.qb = r["qb"].span(1)
                self.silu = r["silu_c"].span(1)
                self.mm = r["tab_mm"].span(1)
                self.tsb = r["tab_sb"].span(1)

            def wait(self, e):
                e.wait_ge(s_setup, 16 * self.LOADS)

            def pool(self, e):
                for n, (dst, v) in enumerate(((ones[:], 1.0), (rel[N_BUCKETS:N_BUCKETS + 1, :], 1.0), (eps[:, 0:1], EPS),
                                              (eps[:, 1:2], 4 * EPS))):
                    self.const.wait(e, n - 1)
                    e.memset(dst, v).then_inc(self.const.sem, 1)
                self.const.wait(e, 3)
                for ro in r.values():
                    if ro.primed:
                        e.sem_inc(ro.sem, ro.primed)
                self.wait(e)

            def act(self, e):
                for dst, src in ((cols[:], d["cols"]), (x[:], d["xT"]), (c_raw[:], d["cT"]),
                                 (onehot[:], d["onehot"]), (rel[0:N_BUCKETS, :], d["rel_bias"]),
                                 (ident[:], d["ident"]), (flip[:], d["flip"]), (cx[:], d["ctxT"]),
                                 (rope[:], d["rope"]), (sinks[:, 0:8], d["sinks"].partition_broadcast(P)),
                                 (sinks[:, 8:16], d["no_sinks"].partition_broadcast(P))):
                    e.dma_start(dst, src).then_inc(s_setup, 16)
                self.wait(e)
                self.const.wait(e, 3)
                e.activation(silu_c[:], c_raw[:], ACT.Silu).then_inc(self.silu.sem, 1)
                self.mm.wait(e, 0)
                e.activation(tab[:], ps[0:8, 0:4, 0:NTAB // 2], ACT.Copy).then_inc(self.tsb.sem, 1)
                self.tsb.wait(e, 0)
                for m in range(2):
                    e.dma_start(d["tables"][m].rearrange("h (c x) -> h c x", c=2),
                                tab[:, 2 * m:2 * m + 2, :]).then_inc(s_tab, 16)
                for s in range(HL):
                    split_hi(e, s)
                e.wait_ge(s_tab, 32)

            def pe(self, e):
                self.wait(e)
                self.const.wait(e, 1)
                for m in range(2):
                    for c in range(2):
                        mm = e.matmul(ps[0:8, 2 * m + c, 0:320], rel[:, 8 * m:8 * m + 8],
                                      onehot[:, m, c * 320:(c + 1) * 320], start=True, stop=True)
                mm.then_inc(self.mm.sem, 1)
                self.tsb.wait(e, 0)
                self.silu.wait(e, 0)

            def dve(self, e):
                self.wait(e)
                b0 = COLS.at["b_in"]
                e.tensor_scalar(qb8[:], cols[:, b0:b0 + 8], 0.125, None, ALU.mult).then_inc(self.qb.sem, 1)
                for s in range(HL):
                    split_lo(e, s)

        class Norm:
            def __init__(self, srcs, ready, T, dim, t, gain=None, shift=None, outs=None, plain=None, bank=4):
                self.bank = bank
                self.srcs, self.ready, self.T, self.dim, self.t = srcs, ready, T, dim, t
                self.gain, self.shift, self.outs, self.plain = gain, shift, outs, plain
                n = self.n = len(srcs)
                self.pairs = (n + 1) // 2
                self.sq, self.acc, self.ss = r["sq"].span(n), r["acc"].span(n // 2), r["ss"].span(self.pairs)
                self.std, self.rs = r["std"].span(1), r["rstd"].span(1)
                if outs is not None:
                    self.tmp, self.hi, self.out = r["tmp"].span(n), r["xn_hi"].span(n), r["xn"].span(n)
                if plain is not None:
                    self.out = r["yout"].span(n)

            def act_squares(self, e, first=0, last=None):
                for n in range(first, self.n if last is None else last):
                    self.ready(e, n)
                    if n >= 4:
                        self.ss.wait(e, (n - 4) // 2)
                    e.activation(self.t["sq"][:, n % 4, 0:self.T], self.srcs[n], ACT.Square).then_inc(self.sq.sem, 1)

            def pool_add(self, e, p):
                self.sq.wait(e, 2 * p + 1)
                a, b_ = (self.t["sq"][:, (2 * p + q) % 4, 0:self.T] for q in range(2))
                e.tensor_tensor(a, a, b_, ALU.add).then_inc(self.acc.sem, 1)

            def pool_adds(self, e):
                for p in range(self.n // 2):
                    self.acc.wait(e, p - 1)
                    self.pool_add(e, p)

            def pe_stats(self, e, first=0, last=None):
                for p in range(first, self.pairs if last is None else last):
                    if 2 * p + 1 < self.n:
                        self.acc.wait(e, p)
                    else:
                        self.sq.wait(e, 2 * p)
                    e.matmul(ps[:, self.bank, 0:self.T], ones[:], self.t["sq"][:, 2 * p % 4, 0:self.T], start=p == 0,
                             stop=p == self.pairs - 1, skip_group_check=True).then_inc(self.ss.sem, 1)

            def act_std(self, e, half=False):
                self.ss.wait(e, self.pairs - 1)
                f = 4.0 if half else 1.0
                e.activation(self.t["rstd"][:, 0:self.T], ps[:, self.bank, 0:self.T], ACT.Sqrt,
                             scale=f / self.dim, bias=eps[:, int(half):int(half) + 1]).then_inc(self.std.sem, 1)

            def dve_rstd(self, e):
                self.std.wait(e, 0)
                e.reciprocal(self.t["rstd"][:, 0:self.T], self.t["rstd"][:, 0:self.T]).then_inc(self.rs.sem, 1)

            def act_hi(self, e):
                for n in range(self.n):
                    self.tmp.wait(e, n)
                    e.activation(self.outs[0][:, n, 0:self.T], self.t["tmp"][:, n % 2, 0:self.T], ACT.Identity,
                                 bias=self.shift(n)).then_inc(self.hi.sem, 1)

            def dve_tiles(self, e):
                self.rs.wait(e, 0)
                def lo(n):
                    self.hi.wait(e, n)
                    e.scalar_tensor_tensor(out=self.outs[1][:, n, 0:self.T], in0=self.t["tmp"][:, n % 2, 0:self.T],
                                           scalar=self.shift(n), in1=self.outs[0][:, n, 0:self.T].bitcast(F32),
                                           op0=ALU.add, op1=ALU.subtract).then_inc(self.out.sem, 1)
                for n in range(self.n):
                    if n >= 2:
                        self.out.wait(e, n - 2)
                    e.scalar_tensor_tensor(out=self.t["tmp"][:, n % 2, 0:self.T], in0=self.srcs[n],
                                           scalar=self.gain(n), in1=self.t["rstd"][:, 0:self.T],
                                           op0=ALU.mult, op1=ALU.mult).then_inc(self.tmp.sem, 1)
                    if n >= 1:
                        lo(n - 1)
                lo(self.n - 1)

            def dve_plain(self, e):
                self.rs.wait(e, 0)
                for n in range(self.n):
                    e.scalar_tensor_tensor(out=self.plain[:, n, 0:self.T], in0=self.srcs[n], scalar=self.gain(n),
                                           in1=self.t["rstd"][:, 0:self.T], op0=ALU.mult,
                                           op1=ALU.mult).then_inc(self.out.sem, 1)

        fills = []
        last_fill = [None]

        class Fill:
            def __init__(self, *parts):
                self.parts, n = parts, sum(parts)
                self.n, self.first = n, take("ada", n)
                self.layer, self.tile = divmod(self.first, NMOD)
                self.ends = n > 0 and self.tile + n == NMOD
                assert self.tile + n <= NMOD
                if n:
                    self.before, last_fill[0] = last_fill[0], self
                    fills.append((count["slabs"], count["ada"]))
                    self.mod, self.gain = r["mod"].span(1), r["gain"].span(4 if self.ends else 0)

            def pe(self, e, part):
                done, n = sum(self.parts[:part]), self.parts[part] if part < len(self.parts) else 0
                if n and done == 0 and self.before is not None:
                    self.before.mod.wait(e, 0)

                def tile(j, i):
                    a0 = self.first + done + j
                    e.wait_ge(ada_full[a0 % 2], 16 * (a0 // 2 + 1) + 16 * i)
                    for k in range(KD):
                        mm = e.matmul(ps[:, 7, bass.ds(2 * (done + j) + 4 * i, 2)], ada_raw[:, a0 % 2, k * P:(k + 1) * P],
                                      silu_c[:, k, :], start=(k == 0), stop=(k == KD - 1), skip_group_check=True)
                    mm.then_inc(r["ada_used"].sem, 1)
                units(e, n, 2, tile)

            def dve(self, e):
                if not self.n:
                    return
                e.wait_ge(r["ada_used"].sem, self.first + self.n)
                l, c = self.layer, COLS.at[f"b_ada{self.layer}"] + self.tile
                e.tensor_tensor(mod[:, l, self.tile:self.tile + self.n],
                                ps[:, 7, 0:2 * self.n].rearrange("p (n c) -> p n c", c=2),
                                cols[:, c:c + self.n].unsqueeze(2).broadcast_to([P, self.n, 2]), ALU.add) \
                    .then_inc(self.mod.sem, 1)
                if self.ends:
                    self.mod.wait(e, 0)
                    for st in range(2):
                        for w, (g0, g) in enumerate(((8, "g_mix"), (32, "g_ffn"))):
                            c = COLS.at[f"{g}{l}"]
                            e.scalar_tensor_tensor(out=gains[:, l, st, w, :], in0=mod[:, l, g0:g0 + KD, st],
                                                   scalar=1.0, in1=cols[:, c:c + KD], op0=ALU.add,
                                                   op1=ALU.mult).then_inc(self.gain.sem, 1)
                    self.gain.wait(e, 3)

        NO_FILL = Fill()

        def bank7_guard():
            f = last_fill[0]
            return (lambda e: None) if f is None else (lambda e: f.mod.wait(e, 0))

        class Tiles:
            def __init__(self, units_):
                self.units = units_

            def wait(self, e, n):
                sp, k = self.units[n]
                sp.wait(e, k)

        def stats_with_fill(e, norm, fill, part):
            fill.pe(e, part)
            norm.pe_stats(e, 0, 2)
            fill.pe(e, part + 1)
            norm.pe_stats(e, 2, 4)
            fill.pe(e, part + 2)

        class PreNorm(Phase):
            def __init__(self, stream, ready, gain, shift, fill=NO_FILL, part=0, post=None, std_free=lambda e: None):
                super().__init__()
                xs, T = stream
                self.norm = Norm([xs[:, n, 0:T] for n in range(KD)], ready, T, D, nt, gain, shift, (xnh, xnl))
                self.out, self.fill, self.part, self.pool_first = self.norm.out, fill, part, 0
                self.std_free = std_free
                if post is not None:
                    post.next, self.pool_first = self.norm, 2

            def act(self, e):
                self.norm.act_squares(e)
                self.std_free(e)
                self.norm.act_std(e)
                self.norm.act_hi(e)

            def pool(self, e):
                for p in range(self.pool_first, KD // 2):
                    self.norm.acc.wait(e, p - 1)
                    self.norm.pool_add(e, p)

            def pe(self, e):
                stats_with_fill(e, self.norm, self.fill, self.part)

            def dve(self, e):
                self.norm.dve_rstd(e)
                self.norm.dve_tiles(e)
                self.fill.dve(e)

        class PostNorm(Phase):
            POOL = (1, 3, 5)

            def __init__(self, srcs, ready, t, gain, half, early=0, fill=NO_FILL):
                super().__init__()
                self.norm = Norm(srcs, ready, TL, D, t, gain)
                self.half, self.early, self.gain, self.fill, self.next = half, early, gain, fill, None
                self.upd = r["upd"].span(KD)
                on_dve, on_pool = r["x"].span(KD - len(self.POOL)), r["xp"].span(len(self.POOL))
                dve_tiles = [n for n in range(KD) if n not in self.POOL]
                self.out = Tiles([(on_pool, self.POOL.index(n)) if n in self.POOL else (on_dve, dve_tiles.index(n))
                                  for n in range(KD)])

            def act(self, e):
                self.norm.act_squares(e, self.early)
                self.norm.act_std(e, self.half)

            def add(self, e, n):
                self.upd.wait(e, n)
                e.tensor_tensor(x[:, n, :], x[:, n, :], self.norm.t["tmp"][:, n % 2, :], ALU.add) \
                    .then_inc(self.out.units[n][0].sem, 1)

            def pe(self, e):
                stats_with_fill(e, self.norm, self.fill, 0)

            def pool(self, e):
                self.norm.pool_adds(e)
                for n in self.POOL:
                    if n > 1:
                        self.out.wait(e, n - 2)
                    self.add(e, n)
                    if n > 1 and self.next is not None:
                        self.next.acc.wait(e, (n - 3) // 2 - 1)
                        self.next.pool_add(e, (n - 3) // 2)

            def dve(self, e):
                m = self.norm
                m.dve_rstd(e)
                m.rs.wait(e, 0)
                for n in range(KD):
                    if n >= 2:
                        self.out.wait(e, n - 2)
                    e.scalar_tensor_tensor(out=m.t["tmp"][:, n % 2, :], in0=m.srcs[n], scalar=self.gain(n),
                                           in1=m.t["rstd"][:], op0=ALU.mult, op1=ALU.mult).then_inc(self.upd.sem, 1)
                    if n >= 1 and n - 1 not in self.POOL:
                        self.add(e, n - 1)
                self.add(e, KD - 1)

        class GateUp(Phase):
            def __init__(self, T, xn, conv=None):
                super().__init__()
                self.T, self.xn, self.conv = T, xn, conv
                self.base = take("slabs", 2 * KF)
                self.sil, self.h = r["sil"].span(KF), r["h"].span(KF)
                self.h_hi, self.h_lo = r["h_hi"].span(KF), r["h_lo"].span(KF)
                if conv is not None:
                    self.yg, self.yv = r["yg"].span(KF), r["yv"].span(KF)
                    self.cg, self.cv = r["cg"].span(2 * KF), r["cv"].span(2 * KF)

            def pe(self, e):
                T, acts = self.T, (xnh, xnl)

                def mms(j, i, hi, lo):
                    if j % 2 == 0:
                        self.h.wait(e, 2 * i + j // 2 - 2)
                    mm = dense(e, ps[:, j, 0:T], (hi, lo), acts, T,
                               wait_k=(lambda k: self.xn.wait(e, k)) if j == 0 else None)
                    return mm

                ring_pe(e, self.base, 2 * KF, mms)

            def act(self, e):
                T = self.T

                def hid(b, m, q):
                    self.h.wait(e, m)
                    e.activation(hmh[:, bass.ds(m, 1), 0:T].rearrange("p a t -> p (a t)"), hbuf[:, q, 0:T],
                                 ACT.Copy).then_inc(self.h_hi.sem, 1)

                def evac(j, i):
                    q, m = j // 2, 2 * i + j // 2
                    if self.conv is None:
                        if j % 2 == 0:
                            self.h.wait(e, m - 1)
                            e.activation(sil[:, 0:T], ps[:, j, 0:T], ACT.Silu).then_inc(self.sil.sem, 1)
                        else:
                            split_hi(e, self.base + j + HL, i)
                            hid(None, m, q)
                        return
                    l = self.conv
                    y, ro, off = (yg, self.yg, 0) if j % 2 == 0 else (yv, self.yv, KF)
                    self.h.wait(e, m - 2)
                    e.activation(y[:, q, 0:T], ps[:, j, 0:T], ACT.Identity, bias=col(f"b_dw{l}", m + off),
                                 scale=col(f"w_dw1{l}", m + off)).then_inc(ro.sem, 1)
                    if j % 2 == 1:
                        split_hi(e, self.base + j + HL, i)
                        self.cg.wait(e, 2 * m + 1)
                        self.h.wait(e, m - 1)
                        e.activation(sil[:, 0:T], yg[:, q, 0:T], ACT.Silu).then_inc(self.sil.sem, 1)
                        hid(None, m, q)

                def step(j, i):
                    used.wait(e, self.base + BODY * i + j)
                    evac(j, i)
                    if j % 2 == 0:
                        split_hi(e, self.base + j + HL, i)
                units(e, 2 * KF, BODY, step)

            def dve(self, e):
                T = self.T

                def make_h(m, q, up):
                    self.sil.wait(e, m)
                    self.h_lo.wait(e, m - 2)
                    e.tensor_tensor(hbuf[:, q, 0:T], sil[:, 0:T], up, ALU.mult).then_inc(self.h.sem, 1)

                def lo(m, q):
                    self.h_hi.wait(e, m)
                    dst = (slice(None), bass.ds(m, 1), slice(0, T))
                    e.tensor_tensor(hml[dst].rearrange("p a t -> p (a t)"), hbuf[:, q, 0:T],
                                    hmh[dst].rearrange("p a t -> p (a t)").bitcast(F32),
                                    ALU.subtract).then_inc(self.h_lo.sem, 1)

                def conv(j, m, q):
                    l = self.conv
                    y, ro, dn, off = (yg, self.yg, self.cg, 0) if j % 2 == 0 else (yv, self.yv, self.cv, KF)
                    ro.wait(e, m)
                    for k, (o, s, w) in enumerate(((slice(1, T), slice(0, T - 1), f"w_dw0{l}"),
                                                   (slice(0, T - 1), slice(1, T), f"w_dw2{l}"))):
                        if k:
                            dn.wait(e, 2 * m)
                        e.scalar_tensor_tensor(out=y[:, q, o], in0=ps[:, j, s], scalar=col(w, m + off), in1=y[:, q, o],
                                               op0=ALU.mult, op1=ALU.add).then_inc(dn.sem, 1)

                def step(j, i):
                    q, m = j // 2, 2 * i + j // 2
                    used.wait(e, self.base + BODY * i + j)
                    if self.conv is not None:
                        conv(j, m, q)
                    if j % 2 == 1:
                        if self.conv is None:
                            make_h(m, q, ps[:, j, 0:T])
                            split_lo(e, self.base + j + HL, i)
                        else:
                            split_lo(e, self.base + j + HL, i)
                            self.cv.wait(e, 2 * m + 1)
                            make_h(m, q, yv[:, q, 0:T])
                        lo(m, q)
                    else:
                        split_lo(e, self.base + j + HL, i)
                units(e, 2 * KF, BODY, step)

        class Down(Phase):
            SH = KF // 2

            def __init__(self, T, gu, stream=None, gate=None, x_role=None):
                super().__init__()
                self.T, self.gu, self.gate = T, gu, gate
                self.stream, self.bank7 = stream, bank7_guard()
                self.base = take("slabs", 2 * self.SH)
                if gate is None:
                    self.fsb = r["fsb"].span(4)
                else:
                    self.out = r[x_role].span(KD)

            def halves(self, e, step):
                for hf in range(2):
                    b = self.base + hf * self.SH
                    for j in range(3):
                        step(hf, b, j, 0, j)
                    with e.Fori(0, 2) as i:
                        for j in range(BODY):
                            step(hf, b + 3, j, i, 3 + j + BODY * i)

            def bank(self, n):
                return n + 4 if n < 4 else n - 4

            def pe(self, e):
                T = self.T
                self.bank7(e)

                def step(hf, b, j, i, k):
                    lo_done.wait(e, b + BODY * i + j)
                    if hf == 0:
                        self.gu.h_lo.wait(e, 2 * k + 1)
                    w = slab(b + j)
                    for kk in range(2):
                        act = tuple(h[:, bass.ds(2 * k + kk, 1), 0:T].rearrange("p a t -> p (a t)") for h in (hmh, hml))
                        for n in range(4):
                            mm = mm3(e, ps[:, self.bank(4 * hf + n), 0:T], blk(w, kk * 4 + n), act,
                                     isinstance(k, int) and k == 0 and kk == 0, True)
                    mm.then_inc(used.sem, 1)
                self.halves(e, step)

            def act(self, e):
                def step(hf, b, j, i, k):
                    used.wait(e, b + BODY * i + j)
                    split_hi(e, b + j + HL, i)
                    if self.gate is None and hf == 1 and isinstance(k, int) and k == 0:
                        for n in range(4):
                            e.activation(fsb[:, n, :], ps[:, self.bank(n), :], ACT.Copy).then_inc(self.fsb.sem, 1)
                        self.post.norm.act_squares(e, 0, 4)
                self.halves(e, step)

            def update(self, e, hf):
                xs, T = self.stream
                for n in range(4 * hf, 4 * hf + 4):
                    e.scalar_tensor_tensor(out=xs[:, n, 0:T], in0=ps[:, self.bank(n), 0:T], scalar=self.gate(n),
                                           in1=xs[:, n, 0:T], op0=ALU.mult, op1=ALU.add).then_inc(self.out.sem, 1)

            def dve(self, e):
                def step(hf, b, j, i, k):
                    used.wait(e, b + BODY * i + j)
                    split_lo(e, b + j + HL, i)
                    if self.gate is not None and hf == 1 and isinstance(k, int) and k == 0:
                        self.update(e, 0)
                self.halves(e, step)
                if self.gate is not None:
                    self.update(e, 1)

        def ffn_block1(pre_gain, post_gain, ready, pre_fill, part, post, post_fill):
            pre = PreNorm((x, TL), ready, lambda n: col(pre_gain, n), lambda n: col("zero", n), pre_fill, part, post)
            gu = GateUp(TL, pre.out)
            down = Down(TL, gu)

            def f_ready(e, n):
                if n < 4:
                    down.fsb.wait(e, n)
                else:
                    used.wait(e, down.base + 2 * Down.SH - 1)
            srcs = [fsb[:, n, :] if n < 4 else ps[:, n - 4, :] for n in range(KD)]
            fill = Fill(*post_fill)
            down.post = PostNorm(srcs, f_ready, pn_ffn, lambda n: col(post_gain, n), True, 4, fill)
            return down.post, fill

        class Attention(Phase):
            def __init__(self, heads, tt, tiles, q, k, v, qst, p, pt, mix, dk, scale, ready, q0=0, kslot=None,
                         key0=0, vt0=0, mix0=0, bias=False, head0=0, dsplit=0, free=None):
                super().__init__()
                self.heads, self.tt, self.tiles, self.q, self.k, self.v, self.qst_buf, self.p, self.pt, self.mix = heads, tt, tiles, q, k, v, qst, p, pt, mix
                self.dk, self.scale, self.ready, self.q0, self.kslot, self.key0, self.vt0, self.mix0, self.bias, self.head0, self.dsplit = dk, scale, ready, q0, kslot, key0, vt0, mix0, bias, head0, dsplit
                self.U, self.bank7 = 2 * tt, bank7_guard()
                n = heads * tt
                self.S, self.mx, self.negm, self.exp, self.rinv, self.PT, self.pv = (
                    r[name].span(n) for name in ("S", "mx", "negm", "exp", "rinv", "PT", "pv"))
                self.cp_a, self.cp_d = r["cp_a"].span(n), r["cp_d"].span(n if dsplit else 0)
                self.qst, self.o = r["qst"].span(heads), r["o"].span(heads)
                if bias:
                    self.es, self.tot = r["es"].span(n), r["tot"].span(n)
                    self.strips0 = take("strips", heads // 2)

            def unit(self, b, j):
                return self.U * b + j, 2 * b + j // self.tt, j // self.tt, j % self.tt

            def cols_of(self, qt):
                t = self.tiles(qt)
                return t[0] * P, len(t) * P

            def s_ap(self, j, lo, n):
                return ps[:, 2 * (j % 2):2 * (j % 2) + 2, :].rearrange("p a t -> p (a t)")[:, lo:lo + n]

            def pool(self, e):
                self.ready(e)
                T = self.tt * P

                def stage(b, j):
                    h = 2 * b + j
                    self.S.wait(e, self.tt * (h - 1) - 1)
                    self.qst.wait(e, h - 1)
                    src = self.q[0:self.dk, bass.ds(h + self.q0, 1), 0:T].rearrange("p a t -> p (a t)")
                    e.tensor_copy(self.qst_buf[0:self.dk, j, 0:T], src).then_inc(self.qst.sem, 1)
                    if self.bias:
                        e.dma_start(strip[:, j, :], strips_view[bass.ds(h + self.head0, 1)]
                                    .rearrange("a p n -> (a p) n")).then_inc(strip_full[j], 16)
                if self.bias:
                    e.wait_ge(s_tab, 32)
                skewed(e, self.heads // 2, 2, [(0, stage)])

            def pe(self, e):
                self.ready(e)
                self.bank7(e)

                def scores(b, j):
                    u, h, par, qt = self.unit(b, j)
                    self.exp.wait(e, u - 2)
                    if qt == 0:
                        self.qst.wait(e, h)
                        if self.bias:
                            e.wait_ge(strip_full[par], 16 * (self.strips0 + b + 1))
                    c0, n = self.cols_of(qt)
                    if self.bias:
                        g0 = (3 - qt) * P + c0
                        e.matmul(self.s_ap(j, 0, n), flip[:], strip[:, par, g0:g0 + n], start=True, stop=False,
                                 skip_group_check=True)
                    for lo in range(0, n, 512):
                        m = min(512, n - lo)
                        kk = self.k[0:self.dk, bass.ds(self.kslot(b, par), 1), self.key0 + c0 + lo:self.key0 + c0 + lo + m]
                        mm = e.matmul(self.s_ap(j, lo, m), self.qst_buf[0:self.dk, par, qt * P:(qt + 1) * P],
                                      kk.rearrange("p a t -> p (a t)"), start=not self.bias, stop=True,
                                      skip_group_check=True)
                    mm.then_inc(self.S.sem, 1)

                def turn(b, j):
                    u, h, par, qt = self.unit(b, j)
                    self.exp.wait(e, u)
                    self.cp_a.wait(e, u - 1)
                    if self.dsplit:
                        self.cp_d.wait(e, u - 1)
                    _, n = self.cols_of(qt)
                    for t in range(n // P):
                        mm = e.transpose(ps[:, 4 + t // 4, (t % 4) * P:(t % 4 + 1) * P],
                                         self.p[:, j % 2, t * P:(t + 1) * P], ident[:])
                    mm.then_inc(self.PT.sem, 1)

                def pv(b, j):
                    u, h, par, qt = self.unit(b, j)
                    self.cp_a.wait(e, u)
                    if self.dsplit:
                        self.cp_d.wait(e, u)
                    if qt == 0:
                        self.o.wait(e, h - 2)
                    ts = self.tiles(qt)
                    for i_, t in enumerate(ts):
                        vv = self.v[:, self.vt0 + t, bass.ds(self.kslot(b, par) * HD, HD)]
                        mm = e.matmul(ps[:, 6 + par, qt * HD:(qt + 1) * HD], self.pt[:, j % 2, i_ * P:(i_ + 1) * P], vv,
                                      start=(i_ == 0), stop=(i_ == len(ts) - 1), skip_group_check=True)
                    mm.then_inc(self.pv.sem, 1)
                skewed(e, self.heads // 2, self.U, [(0, scores), (2, turn), (3, pv)])

            def sm(self, what, j):
                return small[:, 24 + 8 * what + j:25 + 8 * what + j]

            def dve(self, e):
                def rowmax(b, j):
                    u, h, par, qt = self.unit(b, j)
                    self.S.wait(e, u)
                    _, n = self.cols_of(qt)
                    e.tensor_reduce(self.sm(0, j), self.s_ap(j, 0, n), AX_X, ALU.max).then_inc(self.mx.sem, 1)
                    self.mx.wait(e, u)
                    if self.bias:
                        e.tensor_scalar(self.sm(1, j), self.sm(0, j), sinks[:, bass.ds(h + self.head0, 1)], -1.0, ALU.max,
                                        ALU.mult).then_inc(self.negm.sem, 1)
                    else:
                        e.tensor_scalar(self.sm(1, j), self.sm(0, j), -self.scale, None, ALU.mult) \
                            .then_inc(self.negm.sem, 1)

                def copy_t(b, j):
                    u, h, par, qt = self.unit(b, j)
                    self.PT.wait(e, u)
                    e.tensor_copy(self.pt[:, j % 2, 0:self.dsplit], ps[:, 4, 0:self.dsplit]).then_inc(self.cp_d.sem, 1)

                def inverse(b, j):
                    u, h, par, qt = self.unit(b, j)
                    src = self.sm(2, j)
                    if qt == 0:
                        self.o.wait(e, h - 2)
                    if self.bias:
                        self.es.wait(e, u)
                        e.tensor_tensor(self.sm(4, j), self.sm(2, j), self.sm(3, j), ALU.add).then_inc(self.tot.sem, 1)
                        self.tot.wait(e, u)
                        src = self.sm(4, j)
                    else:
                        self.exp.wait(e, u)
                    e.reciprocal(rinv[:, j:j + 1], src).then_inc(self.rinv.sem, 1)

                def finish(b, j):
                    u, h, par, qt = self.unit(b, j)
                    if qt < self.tt - 1:
                        return
                    self.pv.wait(e, u)
                    self.rinv.wait(e, u)
                    j0 = j - self.tt + 1
                    e.tensor_tensor(self.mix[:, 0:self.tt, bass.ds(h * HD + self.mix0, HD)],
                                    ps[:, 6 + par, 0:self.tt * HD].rearrange("p (t c) -> p t c", c=HD),
                                    rinv[:, j0:j0 + self.tt].unsqueeze(2).broadcast_to([P, self.tt, HD]),
                                    ALU.mult).then_inc(self.o.sem, 1)
                st = [(0, rowmax)] + ([(2, copy_t)] if self.dsplit else []) + [(2, inverse), (4, finish)]
                skewed(e, self.heads // 2, self.U, st)

            def act(self, e):
                def copy_t(b, j):
                    u, h, par, qt = self.unit(b, j)
                    self.PT.wait(e, u)
                    _, n = self.cols_of(qt)
                    n -= self.dsplit
                    bank = 5 if self.dsplit else 4
                    if n == 0:
                        raise AssertionError
                    e.activation(self.pt[:, j % 2, self.dsplit:self.dsplit + n], ps[:, bank, 0:n],
                                 ACT.Copy).then_inc(self.cp_a.sem, 1)

                def exps(b, j):
                    u, h, par, qt = self.unit(b, j)
                    self.negm.wait(e, u)
                    self.PT.wait(e, u - 2)
                    _, n = self.cols_of(qt)
                    e.activation(self.p[:, j % 2, 0:n], self.s_ap(j, 0, n), ACT.Exp, bias=self.sm(1, j),
                                 scale=self.scale, accum_out=self.sm(2, j)).then_inc(self.exp.sem, 1)
                    if self.bias:
                        e.activation(self.sm(3, j), sinks[:, bass.ds(h + self.head0, 1)], ACT.Exp,
                                     bias=self.sm(1, j)).then_inc(self.es.sem, 1)
                skewed(e, self.heads // 2, self.U, [(2, copy_t), (0, exps)])

        class MixTurn(Phase):
            def __init__(self, mix, n, tt, outs, ready):
                super().__init__()
                self.mix, self.n, self.tt = mix, n, tt
                self.outs, self.ready = outs, ready
                self.mm, self.hi, self.out = r["mt_mm"].span(n), r["mt_hi"].span(n), r["mt"].span(n)

            def pe(self, e):
                self.ready(e)
                for c in range(self.n):
                    if c >= 4:
                        self.out.wait(e, c - 4)
                    for t in range(self.tt):
                        mm = e.transpose(ps[:, c % 4, t * P:(t + 1) * P], self.mix[:, t, c * P:(c + 1) * P], ident[:])
                    mm.then_inc(self.mm.sem, 1)

            def act(self, e):
                T = self.tt * P
                for c in range(self.n):
                    self.mm.wait(e, c)
                    e.activation(self.outs[0][:, c, 0:T], ps[:, c % 4, 0:T], ACT.Copy).then_inc(self.hi.sem, 1)

            def dve(self, e):
                T = self.tt * P
                for c in range(self.n):
                    self.hi.wait(e, c)
                    e.tensor_tensor(self.outs[1][:, c, 0:T], ps[:, c % 4, 0:T],
                                    self.outs[0][:, c, 0:T].bitcast(F32), ALU.subtract).then_inc(self.out.sem, 1)

        class InProj1(Phase):
            def __init__(self, xn):
                super().__init__()
                self.xn, self.qb = xn, setup.qb
                self.base = take("slabs", 18)
                self.a, self.v = r["ev_a"].span(18), r["ev_d"].span(18)
                self.vt = r["vt"].span(5)

            def pe(self, e):
                def tile(j, k):
                    self.a.wait(e, k - 4)
                    self.v.wait(e, k - 4)
                    return dense(e, ps[:, j, :], slab(self.base + j), (xnh, xnl), TL,
                                 wait_k=(lambda k_: self.xn.wait(e, k_)) if j == 0 else None)

                def turn(c):
                    self.a.wait(e, 13 + c)
                    self.v.wait(e, 13 + c - 2)
                    for t in range(4):
                        mm = e.transpose(ps[:, 4 + c % 2, t * P:(t + 1) * P], vt1[:, c % 2, t * P:(t + 1) * P], ident[:])
                    mm.then_inc(self.vt.sem, 1)

                ring_pe(e, self.base, 8, lambda j, i, hi, lo: tile(j, BODY * i + j))
                for k in range(8, 18):
                    lo_done.wait(e, self.base + k)
                    self.a.wait(e, k - 4)
                    if k < 17:
                        self.v.wait(e, k - 4)
                    dense(e, ps[:, k % 4, :], slab(self.base + k), (xnh, xnl), TL).then_inc(used.sem, 1)
                    if k > 13:
                        turn(k - 14)
                turn(4)

            def act(self, e):
                self.qb.wait(e, 0)
                def q(j, i):
                    c = BODY * i + j
                    e.activation(q1[:, bass.ds(2 * c, 1), :].rearrange("p a t -> p (a t)"), ps[0:HD, j, :], ACT.Identity,
                                 scale=0.125, bias=qb8[0:HD, bass.ds(c, 1)]).then_inc(self.a.sem, 1)
                ring_act(e, self.base, 8, q)
                for k in range(8, 18):
                    used.wait(e, self.base + k)
                    if k < 13:
                        for s in ((0, 1) if k == 8 else (4 + 2 * (k - 9),)):
                            op = e.activation(k1[:, s, :], ps[0:HD, k % 4, :], ACT.Identity, bias=col("b_in", k)[0:HD])
                    else:
                        self.vt.wait(e, k - 13 - 2)
                        op = e.activation(vt1[:, (k - 13) % 2, :], ps[:, k % 4, :], ACT.Identity, bias=col("b_in", k))
                    op.then_inc(self.a.sem, 1)
                    split_hi(e, self.base + k + HL)

            def dve(self, e):
                self.qb.wait(e, 0)
                def q(j, i):
                    c = BODY * i + j
                    e.tensor_scalar(q1[:, bass.ds(2 * c + 1, 1), :].rearrange("p a t -> p (a t)"), ps[HD:P, j, :], 0.125,
                                    qb8[HD:P, bass.ds(c, 1)], ALU.mult, ALU.add).then_inc(self.v.sem, 1)
                ring_dve(e, self.base, 8, q)

                def values(c):
                    self.vt.wait(e, c)
                    src = ps[:, 4 + c % 2, :].rearrange("p (t c) -> p t c", c=P)
                    if c == 0:
                        for kv in range(2):
                            for dup in range(2):
                                at = (2 * kv + dup) * HD
                                op = e.tensor_copy(v1[:, :, at:at + HD], src[:, :, kv * HD:(kv + 1) * HD])
                    else:
                        at = 4 * HD + (c - 1) * P
                        op = e.tensor_copy(v1[:, :, at:at + P], src)
                    op.then_inc(self.v.sem, 1)

                for k in range(8, 18):
                    used.wait(e, self.base + k)
                    if k < 13:
                        for s in ((2, 3) if k == 8 else (5 + 2 * (k - 9),)):
                            op = e.tensor_scalar(k1[:, s, :], ps[HD:P, k % 4, :], col("b_in", k)[HD:P], None, ALU.add)
                        op.then_inc(self.v.sem, 1)
                    split_lo(e, self.base + k + HL)
                    if k > 13:
                        values(k - 14)
                values(4)

        class OutProj(Phase):
            def __init__(self, T, acts, ready, stream=None, gate=None, x_role=None):
                super().__init__()
                self.T, self.acts, self.ready, self.stream, self.gate = T, acts, ready, stream, gate
                self.base = take("slabs", KD)
                self.out = r["ev_a"].span(KD) if gate is None else r[x_role].span(KD)

            def pe(self, e):
                self.ready(e)

                def mms(j, i, hi, lo):
                    k = BODY * i + j
                    self.out.wait(e, k - 4)
                    return dense(e, ps[:, j, 0:self.T], (hi, lo), self.acts, self.T)
                ring_pe(e, self.base, KD, mms)

            def act(self, e):
                if self.gate is not None:
                    return ring_act(e, self.base, KD)
                def evac(j, i):
                    n = BODY * i + j
                    e.activation(f_hm[:, bass.ds(n, 1), :].rearrange("p a t -> p (a t)"), ps[:, j, :],
                                 ACT.Identity, bias=col("b_out", n)).then_inc(self.out.sem, 1)
                ring_act(e, self.base, KD, evac)

            def dve(self, e):
                if self.gate is None:
                    return ring_dve(e, self.base, KD)
                xs, T = self.stream

                def evac(j, i):
                    n = BODY * i + j
                    xa = xs[:, bass.ds(n, 1), 0:T].rearrange("p a t -> p (a t)")
                    e.scalar_tensor_tensor(out=xa, in0=ps[:, j, 0:T], scalar=self.gate(n), in1=xa, op0=ALU.mult,
                                           op1=ALU.add).then_inc(self.out.sem, 1)
                ring_dve(e, self.base, KD, evac)

        class Embed(Phase):
            def __init__(self, xn):
                super().__init__()
                self.xn = xn
                self.base = take("slabs", 10)
                self.e = r["e"].span(6)
                self.sg, self.y = r["sg"].span(KD), r["y"].span(KD)
                self.p_hi, self.p_lo = r["p_hi"].span(1), r["p_lo"].span(1)

            def pe(self, e):
                def mms(j, i, hi, lo):
                    self.sg.wait(e, BODY * i + j - 4)
                    return dense(e, ps[:, j, :], (hi, lo), (xnh, xnl), TL,
                                 wait_k=(lambda k: self.xn.wait(e, k)) if j == 0 else None)
                ring_pe(e, self.base, KD, mms)
                self.p_lo.wait(e, 0)
                for s in range(2):
                    lo_done.wait(e, self.base + KD + s)
                    for n in range(4):
                        self.sg.wait(e, 4 + n)
                        if s:
                            self.y.wait(e, n)
                        for k in range(2):
                            mm = mm3(e, ps[:, n, :], blk(slab(self.base + KD + s), 2 * n + k), (ph[:, k, :], pl[:, k, :]),
                                     k == 0, k == 1)
                        mm.then_inc(self.e.sem if n < 3 else used.sem, 1)

            def pool(self, e):
                e.dma_start(p_raw[:], d["pT"]).then_inc(s_pload, 16)

            def act(self, e):
                def gate(j, i):
                    n = BODY * i + j
                    e.activation(sg[:, n, :], ps[:, j, :], ACT.Sigmoid).then_inc(self.sg.sem, 1)
                for h in range(2):
                    ring_act(e, self.base + 4 * h, 4, lambda j, i: gate(j, h))
                    if h == 0:
                        e.wait_ge(s_pload, 16)
                        e.activation(ph[:], p_raw[:], ACT.Copy).then_inc(self.p_hi.sem, 1)
                ring_act(e, self.base + KD, 2)

            def dve(self, e):
                ring_dve(e, self.base, 4)
                self.p_hi.wait(e, 0)
                e.tensor_tensor(pl[:], p_raw[:], ph[:].bitcast(F32), ALU.subtract).then_inc(self.p_lo.sem, 1)
                ring_dve(e, self.base + 4, 4)
                for s in range(2):
                    for n in range(4):
                        if n < 3:
                            self.e.wait(e, 3 * s + n)
                        else:
                            used.wait(e, self.base + KD + s)
                        e.tensor_tensor(f_hm[:, 4 * s + n, :], sg[:, 4 * s + n, :], ps[:, n, :], ALU.mult) \
                            .then_inc(self.y.sem, 1)
                    split_lo(e, self.base + KD + s + HL)

        class LatentIn(Phase):
            def __init__(self, T, xn, key0, rotate, full):
                super().__init__()
                self.T, self.tt, self.xn, self.key0, self.rotate, self.full = T, T // P, xn, key0, rotate, full
                self.base = take("slabs", 7 if full else 2)
                self.first = 0 if full else 5
                self.fin_hi, self.fin = r["fin_hi"].span(self.tt if full else 0), r["fin"].span(self.tt if full else 0)
                self.cq = r["cq"].span(4 if full else 1)
                self.rot, self.kr = r["rot"].span(2 if rotate else 0), r["kr"].span(1)
                self.spread, self.bank7 = take("krope", 1), bank7_guard()

            def cq_ready(self, e, c):
                self.cq.wait(e, c if self.full else 0)

            def pe(self, e):
                T, acts = self.T, (xnh, xnl)
                by_k = lambda kb: self.xn.wait(e, kb)
                for k in range(self.first, 7):
                    s = self.base + k - self.first
                    lo_done.wait(e, s)
                    w = slab(s)
                    if k < 2:
                        for kb in range(4):
                            by_k(4 * k + kb)
                            for t in range(self.tt):
                                mm = mm3(e, ps[:, t, 0:256], tuple(a[:, 4 * k + kb, t * P:(t + 1) * P] for a in acts),
                                         blk(w, kb, 256), k == 0 and kb == 0, k == 1 and kb == 3)
                    elif k < 6:
                        if k == 4:
                            self.bank7(e)
                        mm = dense(e, ps[:, (5, 6, 7, 4)[k - 2], 0:T], w, acts, T, wait_k=by_k if k == 5 else None)
                    else:
                        if self.full:
                            self.fin.wait(e, 0)
                        mm = dense(e, ps[:, 0, 0:T], w, acts, T)
                    mm.then_inc(used.sem, 1)

            def act(self, e):
                T = self.T
                for k in range(self.first, 7):
                    s = self.base + k - self.first
                    used.wait(e, s)
                    if k == 1:
                        for t in range(self.tt):
                            e.activation(finh[:, t, :], ps[:, t, 0:256], ACT.Copy).then_inc(self.fin_hi.sem, 1)
                    if 2 <= k < 6:
                        e.activation(cq[:, k - 2, 0:T], ps[:, (5, 6, 7, 4)[k - 2], 0:T], ACT.Copy).then_inc(self.cq.sem, 1)
                    split_hi(e, s + HL)

            def dve(self, e):
                T = self.T
                for k in range(self.first, 7):
                    s = self.base + k - self.first
                    used.wait(e, s)
                    if k == 1:
                        for t in range(self.tt):
                            self.fin_hi.wait(e, t)
                            e.tensor_tensor(finl[:, t, :], ps[:, t, 0:256], finh[:, t, :].bitcast(F32),
                                            ALU.subtract).then_inc(self.fin.sem, 1)
                    split_lo(e, s + HL)
                out = k2[64:96, 0, self.key0:self.key0 + T]
                if self.rotate:
                    rotary(e, out, 0, 0, T, self.rot, 0, self.kr)
                else:
                    e.tensor_copy(out, ps[64:96, 0, 0:T]).then_inc(self.kr.sem, 1)

            def pool(self, e):
                self.kr.wait(e, 0)
                src = k2[64:96, 0:1, self.key0:self.key0 + self.T].broadcast_to([32, MLA_H - 1, self.T])
                e.dma_start(k2[64:96, 1:MLA_H, self.key0:self.key0 + self.T], src).then_inc(s_krope, 16)

        def rotary(e, out, bank, slot, T, rot, n, done):
            e.tensor_tensor(rt2[64:96, slot, 0:T], ps[96:128, bank, 0:T], rope[96:128, 0:T], ALU.mult).then_inc(rot.sem, 1)
            e.tensor_tensor(out, ps[64:96, bank, 0:T], rope[64:96, 0:T], ALU.mult).then_inc(rot.sem, 1)
            rot.wait(e, n + 1)
            e.tensor_tensor(out, out, rt2[64:96, slot, 0:T], ALU.add).then_inc(done.sem, 1)

        class Fourier(Phase):
            def __init__(self, l, T, inp, nq, nkv):
                super().__init__()
                self.l, self.T, self.tt, self.inp, self.nq, self.nkv = l, T, T // P, inp, nq, nkv
                self.nd = 2 * self.tt * T // SLAB
                self.base = take("slabs", self.nd + 1)
                self.pq_hi, self.pq = r["pq_hi"].span(4), r["pq"].span(4)
                self.f_mm, self.f_hi, self.f = r["f_mm"].span(1), r["f_hi"].span(2), r["f"].span(2)
                self.four_hi, self.four = r["four_hi"].span(2), r["four"].span(2)

            def pe(self, e):
                T, tt = self.T, self.tt
                self.inp.fin.wait(e, tt - 1)
                self.inp.kr.wait(e, 0)
                for s in range(self.nd):
                    lo_done.wait(e, self.base + s)
                    w = slab(self.base + s)
                    for g in range(SLAB // T):
                        m, tb = divmod(s * (SLAB // T) + g, tt)
                        for c in range(2):
                            mm = mm3(e, ps[:, 2 * m + c, 0:T], tuple(f[:, tb, c * P:(c + 1) * P] for f in (finh, finl)),
                                     blk(w, g, T), tb == 0, tb == tt - 1)
                    mm.then_inc(used.sem, 1)
                self.inp.cq_ready(e, 3)
                self.nq.pe_stats(e)
                self.nkv.pe_stats(e)
                s = self.base + self.nd
                lo_done.wait(e, s)
                w = slab(s)
                self.pq.wait(e, 3)
                for c in range(2):
                    for m in range(2):
                        mm = mm3(e, ps[:, 5 + c, 0:T], blk(w, m), tuple(a[:, 2 * m + c, 0:T] for a in (pqh, pql)),
                                 m == 0, m == 1)
                mm.then_inc(self.f_mm.sem, 1)
                self.f.wait(e, 1)
                for n in range(2):
                    for k in range(2):
                        mm = mm3(e, ps[:, n, 0:T], blk(w, 2 + 2 * k + n), tuple(a[:, k, 0:T] for a in (fh, fl)),
                                 k == 0, k == 1)
                mm.then_inc(used.sem, 1)

            def act(self, e):
                T = self.T
                self.nq.act_squares(e)
                self.nkv.act_squares(e)
                for s in range(self.nd):
                    used.wait(e, self.base + s)
                    split_hi(e, self.base + s + HL)
                for c in range(4):
                    e.activation(pqh[:, c, 0:T], ps[:, c, 0:T], ACT.Copy).then_inc(self.pq_hi.sem, 1)
                self.nq.act_std(e)
                self.nkv.act_std(e)
                self.f_mm.wait(e, 0)
                for c in range(2):
                    e.activation(fh[:, c, 0:T], ps[:, 5 + c, 0:T], ACT.Copy).then_inc(self.f_hi.sem, 1)
                self.nq.act_hi(e)
                self.nkv.act_hi(e)
                used.wait(e, self.base + self.nd)
                for n in range(2):
                    e.activation(xnh[:, n, 0:T], ps[:, n, 0:T], ACT.Identity, bias=col(f"b_f{self.l}", n)) \
                        .then_inc(self.four_hi.sem, 1)
                split_hi(e, self.base + self.nd + HL)

            def pool(self, e):
                self.nq.pool_adds(e)
                self.nkv.pool_adds(e)

            def dve(self, e):
                T = self.T
                for s in range(self.nd):
                    used.wait(e, self.base + s)
                    split_lo(e, self.base + s + HL)
                for c in range(4):
                    self.pq_hi.wait(e, c)
                    e.tensor_tensor(pql[:, c, 0:T], ps[:, c, 0:T], pqh[:, c, 0:T].bitcast(F32),
                                    ALU.subtract).then_inc(self.pq.sem, 1)
                self.nq.dve_rstd(e)
                self.nkv.dve_rstd(e)
                for c in range(2):
                    self.f_hi.wait(e, c)
                    e.tensor_tensor(fl[:, c, 0:T], ps[:, 5 + c, 0:T], fh[:, c, 0:T].bitcast(F32),
                                    ALU.subtract).then_inc(self.f.sem, 1)
                self.nq.dve_tiles(e)
                self.nkv.dve_tiles(e)
                for n in range(2):
                    self.four_hi.wait(e, n)
                    e.scalar_tensor_tensor(out=xnl[:, n, 0:T], in0=ps[:, n, 0:T], scalar=col(f"b_f{self.l}", n),
                                           in1=xnh[:, n, 0:T].bitcast(F32), op0=ALU.add,
                                           op1=ALU.subtract).then_inc(self.four.sem, 1)
                split_lo(e, self.base + self.nd + HL)

        class NormOnly(Phase):
            def __init__(self, norm):
                super().__init__()
                self.norm = norm

            def act(self, e):
                self.norm.act_squares(e)
                self.norm.act_std(e)
                self.norm.act_hi(e)

            def pe(self, e):
                self.norm.pe_stats(e)

            def dve(self, e):
                self.norm.dve_rstd(e)
                self.norm.dve_tiles(e)

        class QProj(Phase):
            def __init__(self, T, norm, rotate, four):
                super().__init__()
                self.T, self.norm, self.rotate, self.four = T, norm, rotate, four
                self.base = take("slabs", MLA_H // 2)
                self.a = r["ev_a"].span(MLA_H)
                self.v = r["ev_d"].span(MLA_H if rotate else 0)
                self.rot = r["rot"].span(2 * MLA_H if rotate else 0)

            def pe(self, e):
                T = self.T
                self.norm.out.wait(e, 2)
                self.four.four.wait(e, 1)
                for s in range(MLA_H // 2):
                    lo_done.wait(e, self.base + s)
                    for hh in range(2):
                        h = 2 * s + hh
                        if h >= 4:
                            self.a.wait(e, h - 4)
                            if self.rotate:
                                self.v.wait(e, h - 4)
                        for k in range(3):
                            mm = mm3(e, ps[:, h % 4, 0:T], blk(slab(self.base + s), 3 * hh + k),
                                     (cnh[:, k, 0:T], cnl[:, k, 0:T]), k == 0, k == 2)
                    mm.then_inc(used.sem, 1)

            def act(self, e):
                T = self.T
                n = NOPE if self.rotate else NOPE + ROPE
                for s in range(MLA_H // 2):
                    used.wait(e, self.base + s)
                    for h in (2 * s, 2 * s + 1):
                        e.activation(q2[0:n, h, 0:T], ps[0:n, h % 4, 0:T], ACT.Copy).then_inc(self.a.sem, 1)
                    split_hi(e, self.base + s + HL)

            def dve(self, e):
                T = self.T
                for s in range(MLA_H // 2):
                    used.wait(e, self.base + s)
                    if self.rotate:
                        for h in (2 * s, 2 * s + 1):
                            if h >= 2:
                                self.v.wait(e, h - 2)
                            rotary(e, q2[64:96, h, 0:T], h % 4, h % 2, T, self.rot, 2 * h, self.v)
                    split_lo(e, self.base + s + HL)

        class KVProj(Phase):
            def __init__(self, T, norm, key0, after=None):
                super().__init__()
                self.T, self.tt, self.norm, self.key0, self.after = T, T // P, norm, key0, after
                self.base = take("slabs", 2)
                n = MLA_H // 2 + self.tt
                self.vt = r["vt"].span(self.tt)
                self.a, self.v = r["ev_a"].span(n), r["ev_d"].span(n)

            def pe(self, e):
                T = self.T
                self.norm.out.wait(e, 0)
                if self.after is not None:
                    self.after.a.wait(e, MLA_H - 1)
                    if self.after.rotate:
                        self.after.v.wait(e, MLA_H - 1)
                lo_done.wait(e, self.base)
                for p_ in range(MLA_H // 2):
                    if p_ >= 4:
                        self.a.wait(e, p_ - 4)
                        self.v.wait(e, p_ - 4)
                    mm = mm3(e, ps[:, p_ % 4, 0:T], blk(slab(self.base), p_), (cnh[:, 3, 0:T], cnl[:, 3, 0:T]), True, True)
                    if p_ == 3:
                        mm.then_inc(self.vt.sem, 1)
                mm.then_inc(used.sem, 1)
                lo_done.wait(e, self.base + 1)
                w = slab(self.base + 1)
                for t in range(self.tt):
                    last = MLA_H // 2 + t - 2 if t >= 2 else (5 if t == 0 else 3)
                    self.a.wait(e, last)
                    self.v.wait(e, last)
                    act = tuple(c[:, 3, t * P:(t + 1) * P] for c in (cnh, cnl))
                    mm3(e, ps[:, 2 * (t % 2), :], act, tuple(a[:, 0:512] for a in w), True, True)
                    mm = mm3(e, ps[:, 2 * (t % 2) + 1, 0:256], act, tuple(a[:, 512:768] for a in w), True, True)
                    mm.then_inc(self.vt.sem if t < self.tt - 1 else used.sem, 1)

            def act(self, e):
                T, k0 = self.T, self.key0
                for p_ in range(MLA_H // 2):
                    if p_ == 0:
                        self.vt.wait(e, 0)
                    if p_ == 4:
                        used.wait(e, self.base)
                    e.activation(k2[0:HD, 2 * p_, k0:k0 + T], ps[0:HD, p_ % 4, 0:T], ACT.Copy).then_inc(self.a.sem, 1)
                split_hi(e, self.base + HL)
                for t in range(self.tt):
                    self.tile_ready(e, t)
                    e.activation(v2[:, k0 // P + t, 0:512], ps[:, 2 * (t % 2), :], ACT.Copy).then_inc(self.a.sem, 1)
                split_hi(e, self.base + 1 + HL)

            def tile_ready(self, e, t):
                if t < self.tt - 1:
                    self.vt.wait(e, t + 1)
                else:
                    used.wait(e, self.base + 1)

            def dve(self, e):
                T, k0 = self.T, self.key0
                for p_ in range(MLA_H // 2):
                    if p_ == 0:
                        self.vt.wait(e, 0)
                    if p_ == 4:
                        used.wait(e, self.base)
                    e.tensor_copy(k2[0:HD, 2 * p_ + 1, k0:k0 + T], ps[HD:P, p_ % 4, 0:T]).then_inc(self.v.sem, 1)
                split_lo(e, self.base + HL)
                for t in range(self.tt):
                    self.tile_ready(e, t)
                    e.tensor_copy(v2[:, k0 // P + t, 512:768], ps[:, 2 * (t % 2) + 1, 0:256]).then_inc(self.v.sem, 1)
                split_lo(e, self.base + 1 + HL)

        class Final(Phase):
            def __init__(self, ready):
                super().__init__()
                self.norm = Norm([x[:, n, :] for n in range(KD)], ready, TL, D, nt, lambda n: col("g_final", n),
                                 plain=yout)

            def act(self, e):
                self.norm.act_squares(e)
                self.norm.act_std(e)
                for n in range(KD):
                    self.norm.out.wait(e, n)
                    e.dma_start(d["out"][:, n, :], yout[:, n, :]).then_inc(s_out, 16)
                e.wait_ge(s_out, 16 * KD)

            def pool(self, e):
                self.norm.pool_adds(e)

            def pe(self, e):
                self.norm.pe_stats(e)

            def dve(self, e):
                self.norm.dve_rstd(e)
                self.norm.dve_plain(e)

        def latent_mixer(l, st, x_ready, fill=NO_FILL, part=0, std_free=lambda e: None):
            T, xs, key0 = ((TL, x, 0), (TC, cx, TL))[st]
            full = st == 0 or l == 0
            pre = PreNorm((xs, T), x_ready, lambda n: gains[:, l, st, 0, n:n + 1], lambda n: mod[:, l, n, st:st + 1],
                          fill, part, None, std_free)
            inp = LatentIn(T, pre.out, key0, st == 0, full)
            zero = lambda n: col("zero", n)
            nkv = lambda: Norm([cq[:, 3, 0:T]], lambda e, n: inp.cq_ready(e, 3), T, P, nt2, lambda n: col(f"g_kv{l}", n),
                               zero, (cnh[:, 3:4, :], cnl[:, 3:4, :]), bank=7)
            if full:
                nq = Norm([cq[:, c, 0:T] for c in range(3)], lambda e, n: inp.cq_ready(e, n), T, 3 * P, nt,
                          lambda n: col(f"g_q{l}", n), zero, (cnh, cnl))
                nk = nkv()
                four = Fourier(l, T, inp, nq, nk)
                qp = QProj(T, nq, st == 0, four)
            else:
                nk = nkv()
                NormOnly(nk)
                qp = None
            kv = KVProj(T, nk, key0, qp)
            if not full:
                return None
            spread = inp.spread + 1

            def ready(e):
                kv.a.wait(e, MLA_H // 2 + kv.tt - 1)
                kv.v.wait(e, MLA_H // 2 + kv.tt - 1)
                e.wait_ge(s_krope, 16 * spread)
            keys = (lambda qt: list(range(6))) if st == 0 else (lambda qt: [0, 1])
            att = Attention(MLA_H, T // P, keys, q2, k2, v2, qst2, p2, pt2, mix2, 96, MLA_SCALE, ready,
                            kslot=lambda b, par: 2 * b + par, key0=0 if st == 0 else TL, vt0=0 if st == 0 else 4,
                            dsplit=512 if st == 0 else 0)
            turn = MixTurn(mix2, 6, T // P, (m2h, m2l), lambda e: att.o.wait(e, MLA_H - 1))

            def mixed(e):
                four.four.wait(e, 1)
                turn.out.wait(e, 5)
            role_x = ("x", "cx")[st]
            acts = [(xnh[:, k, 0:T], xnl[:, k, 0:T]) for k in range(2)] + \
                [(m2h[:, k, 0:T], m2l[:, k, 0:T]) for k in range(6)]
            out = OutProj(T, acts, mixed, (xs, T), lambda n: mod[:, l, bass.ds(16 + n, 1), st],
                          role_x)
            return out.out

        def latent_ffn(l, st, x_done, fill=NO_FILL):
            T, xs = ((TL, x), (TC, cx))[st]
            pre = PreNorm((xs, T), lambda e, n: x_done.wait(e, n), lambda n: gains[:, l, st, 1, n:n + 1],
                          lambda n: mod[:, l, 24 + n, st:st + 1], fill)
            gu = GateUp(T, pre.out, conv=l)
            down = Down(T, gu, (xs, T), lambda n: mod[:, l, 40 + n, st:st + 1], ("x", "cx")[st])
            return down.out

        setup = Setup()
        tables_view = d["tables"]
        strips_view = bass.AP(tables_view.tensor, 0, [[NTAB, 16], [1, P], [1, TL]])
        after = lambda sp: (lambda e, n: sp.wait(e, n))

        post, fill = ffn_block1("ffn1_pre_g", "ffn1_post_g", lambda e, n: e.wait_ge(s_setup, 16 * Setup.LOADS),
                                Fill(2, 4, 3), 0, None, (0, 3, 0, 3, 4, 3))
        pre = PreNorm((x, TL), after(post.out), lambda n: col("attn_pre_g", n), lambda n: col("zero", n), fill, 3, post)
        proj = InProj1(pre.out)

        def qkv_ready(e):
            proj.a.wait(e, 12)
            proj.v.wait(e, 17)
        att_a = Attention(8, 4, lambda qt: [qt - 1, qt] if qt else [0], q1, k1, v1, qst1, p1, pt1, mix1, HD, 1.0,
                          qkv_ready, kslot=lambda b, par: b, bias=True)
        att_b = Attention(8, 4, lambda qt: list(range(qt + 1)), q1, k1, v1, qst1, p1, pt1, mix1, HD, 1.0,
                          qkv_ready, q0=8, kslot=lambda b, par: 4 + 2 * b + par, mix0=512, bias=True, head0=8)
        turn1 = MixTurn(mix1, 8, 4, (m1h, m1l), lambda e: att_b.o.wait(e, 7))
        outp = OutProj(TL, (m1h, m1l), lambda e: turn1.out.wait(e, 7))
        f_tiles = [f_hm[:, n, :] for n in range(KD)]
        fill = Fill(2, 3, 2, 3, 4, 3)
        post = PostNorm(f_tiles, after(outp.out), pn_hm, lambda n: col("attn_post_g", n), False, 0, fill)

        post, fill = ffn_block1("ffn2_pre_g", "ffn2_post_g", after(post.out), fill, 3, post, (0, 3, 0, 2, 3, 1))
        pre = PreNorm((x, TL), after(post.out), lambda n: col("ple_pre_g", n), lambda n: col("zero", n), fill, 3, post)
        emb = Embed(pre.out)
        fill = Fill(1, 4, 2, 2, 4, 4)
        post = PostNorm(f_tiles, after(emb.y), pn_hm, lambda n: col("ple_post_g", n), False, 0, fill)

        x_now = post.out
        c1 = latent_mixer(0, 1, lambda e, n: None, fill, 3, lambda e: post.out.wait(e, KD - 1))
        x_mix = latent_mixer(0, 0, after(x_now), Fill(3, 7, 4))
        x_now = latent_ffn(0, 0, x_mix, Fill(5, 7, 5))
        c2 = latent_ffn(0, 1, c1)
        latent_mixer(1, 1, after(c2))
        x_mix = latent_mixer(1, 0, after(x_now))
        x_now = latent_ffn(1, 0, x_mix)
        Final(after(x_now))
        assert count["ada"] == 2 * NMOD, count
        take("slabs", HL)
        assert count["slabs"] == d["n_slabs"], count

        block = ctx.enter_context(nc.Block())

        @block.sync
        def _(e):
            at, at_ada = 0, 0

            def main(n):
                nonlocal at
                b = at
                units(e, n, BODY, lambda j, i: load(e, b + j, i))
                at += n

            def ada_loads(n):
                nonlocal at_ada
                a0 = at_ada

                def one(j, i):
                    v = a0 + j + 2 * i - 1
                    if not isinstance(v, int) or v > 0:
                        e.wait_ge(r["ada_used"].sem, v)
                    e.dma_start(ada_raw[:, (a0 + j) % 2, :],
                                d["wa"][bass.ds(a0 + j + 2 * i, 1)].rearrange("a p n -> (a p) n")) \
                        .then_inc(ada_full[(a0 + j) % 2], 16)
                units(e, n, 2, one)
                at_ada += n

            main(RAW)
            ada_loads(2)
            for slabs, ada in fills:
                main(slabs + RAW + HL - at)
                ada_loads(min(ada + 2, 2 * NMOD) - at_ada)
            main(count["slabs"] - at)

        @block.tensor
        def _(e):
            for ph_ in phases:
                ph_.pe(e)

        @block.scalar
        def _(e):
            for ph_ in phases:
                ph_.act(e)

        @block.vector
        def _(e):
            for ph_ in phases:
                ph_.dve(e)

        @block.gpsimd
        def _(e):
            for ph_ in phases:
                ph_.pool(e)


def slabs_by_column(w):
    k, n = w.shape
    return w.reshape(k // P, P, n // P, P).transpose(2, 1, 0, 3).reshape(n // P, P, -1)


def gate_up_slabs(w):
    s = slabs_by_column(w)
    return np.stack([s[:KF], s[KF:]], axis=1).reshape(2 * KF, P, SLAB)


def down_slabs(w):
    a = w.reshape(KF // 2, 2, P, 2, 4 * P)
    return a.transpose(3, 0, 2, 1, 4).reshape(KF, P, SLAB)


def pad(a):
    return np.concatenate([a, np.zeros((P, SLAB - a.shape[1]), a.dtype)], axis=1)[None]


def latent_slabs(i, l, st, full):
    T = (TL, TC)[st]
    w = i["w_in_2"][l]
    out = []
    kr = w[:, 768:800]
    swapped = np.concatenate([kr[:, 16:], kr[:, :16]], axis=1)
    kr = slabs_by_column(np.concatenate([kr, swapped, kr, swapped], axis=1))
    if full:
        out.append(w[:, :256].reshape(2, 4, P, 256).transpose(0, 2, 1, 3).reshape(2, P, SLAB))
        out.append(slabs_by_column(w[:, 256:640]))
    out += [slabs_by_column(w[:, 640:768]), kr]
    if full:
        out.append(dft_slabs(T))
        wf = i["w_fourier_2"][l].reshape(2, P, 2, P).transpose(1, 0, 2, 3).reshape(P, 512)
        out.append(pad(np.concatenate([*channel_dft(T), wf], axis=1)))
        q = i["w_q_b_2"][l].reshape(3, P, MLA_H, 96)
        q = np.concatenate([q, q[..., 80:], q[..., 64:80]], axis=3)
        for s in range(MLA_H // 2):
            out.append(pad(q[:, :, 2 * s:2 * s + 2].transpose(1, 2, 0, 3).reshape(P, 768)))
    kv = i["w_kv_b_2"][l].reshape(P, MLA_H, 2, HD)
    out += [pad(kv[:, :, 0].reshape(P, 768)), pad(kv[:, :, 1].reshape(P, 768))]
    if full:
        out.append(slabs_by_column(i["w_out_2"][l]))
    return out


def weight_stream(i):
    a_kv, b0 = 512, 768
    w = i["w_in"][0]
    out = [gate_up_slabs(i["ffn1_w_gu"][0]), down_slabs(i["ffn1_w_down"][0])]
    order = [w[:, 0:512], w[:, b0:b0 + 512], w[:, a_kv:a_kv + 128], w[:, b0 + 512:b0 + 1024], w[:, a_kv + 128:b0],
             w[:, b0 + 1024:]]
    out += [slabs_by_column(np.concatenate(order, axis=1)), slabs_by_column(i["w_out"][0])]
    out += [gate_up_slabs(i["ffn2_w_gu"][0]), down_slabs(i["ffn2_w_down"][0])]
    proj = i["w_ple_proj"][0].reshape(2, P, 2, 4, P).transpose(2, 1, 3, 0, 4).reshape(2, P, SLAB)
    out += [slabs_by_column(i["w_ple_gate"][0]), proj]
    ffn = lambda l: [gate_up_slabs(i["w_up_2"][l]), down_slabs(i["w_down_2"][l])]
    out += latent_slabs(i, 0, 1, True) + latent_slabs(i, 0, 0, True) + ffn(0) + ffn(0)
    out += latent_slabs(i, 1, 1, False) + latent_slabs(i, 1, 0, True) + ffn(1)
    out.append(np.zeros((HL, P, SLAB), np.float32))
    return np.concatenate(out)


def column_table(i):
    t = np.zeros((P, COLS.n), np.float32)

    def put(name, v):
        c = COLS.at[name]
        t[:, c:c + v.size // P] = v.reshape(-1, P).T
    for n in ("ffn1_pre_g", "ffn1_post_g", "attn_pre_g", "b_out", "attn_post_g", "ffn2_pre_g", "ffn2_post_g",
              "ple_pre_g", "ple_post_g"):
        put(n, i[n][0])
    put("g_final", i["g_final_2"])
    b = i["b_in"][0]
    put("b_in", np.concatenate([b[0:512], b[768:1280], b[512:640], b[1280:1792], b[640:768], b[1792:]]))
    for l in range(2):
        for n, v in (("b_ada", "b_ada_2"), ("g_mix", "g_mix_2"), ("b_f", "b_fourier_2"), ("g_q", "g_q_a_2"),
                     ("g_kv", "g_kv_a_2"), ("g_ffn", "g_ffn_2"), ("b_dw", "b_dw_2")):
            put(f"{n}{l}", i[v][l])
        for k in range(3):
            put(f"w_dw{k}{l}", i["w_dw_2"][l, k])
    return t


def feature_major(a):
    return a.T.reshape(-1, P, a.shape[0]).transpose(1, 0, 2)


def kernel(**inputs):
    import concourse.bacc as bacc
    from concourse.bass_utils import run_bass_kernel_spmd

    i = {k: np.asarray(v) for k, v in inputs.items()}
    arrays = {
        "ws": weight_stream(i),
        "wa": np.concatenate([slabs_by_column(i["w_ada_2"][l]) for l in range(2)]),
        "cols": column_table(i),
        "xT": feature_major(i["x"][0]),
        "ctxT": feature_major(i["ctx_2"][0]),
        "pT": feature_major(i["p"][0, 0]),
        "cT": np.stack([i["c_2"][0].reshape(KD, P).T, i["c_ctx_2"].reshape(KD, P).T], axis=2),
        "rel_bias": i["rel_bias"],
        "sinks": i["sinks"][0],
        "no_sinks": np.full(8, NEG, np.float32),
        "onehot": bucket_tables(),
        "ident": np.eye(P, dtype=np.float32),
        "flip": np.eye(P, dtype=np.float32)[::-1],
        "rope": rope_table(),
    }
    arrays = {f"in_{k}_dram": np.ascontiguousarray(v) for k, v in arrays.items()}
    nc = bacc.Bacc("TRN2", target_bir_lowering=False, num_devices=1)
    d = {k[3:-5]: nc.dram_tensor(k, v.shape, mybir.dt.from_np(v.dtype), kind="ExternalInput").ap()
         for k, v in arrays.items()}
    d["n_slabs"] = arrays["in_ws_dram"].shape[0]
    d["tables"] = nc.dram_tensor("tables", (2, 8, NTAB), F32).ap()
    d["out"] = nc.dram_tensor("out_0_dram", (P, KD, TL), F32, kind="ExternalOutput").ap()
    build(nc, d)
    res = run_bass_kernel_spmd(nc, [arrays], core_ids=[0])
    out = res.results[0]["out_0_dram"]
    return np.ascontiguousarray(out.transpose(1, 0, 2).reshape(D, TL).T)[None]
```

```python
from contextlib import ExitStack
import math

import numpy as np
import concourse.bass as bass
from concourse import mybir

F32 = mybir.dt.float32
F32R = mybir.dt.float32r
ALU = mybir.AluOpType
ACT = mybir.ActivationFunctionType
AX_X = mybir.AxisListType.X

P = 128
D = 1024
KD = D // P
TL, TC = 512, 256
DFF = 2816
KF = DFF // P
SLAB = 8 * P
RAW = 2
HL = 4
BODY = 4
HD = 64
N_BUCKETS = 32
NTAB = 640
NEG = -1e30
EPS = 1e-6
MLA_H, NOPE, ROPE = 12, 64, 32
MLA_SCALE = (NOPE + ROPE) ** -0.5
NMOD = 48


def bucket_tables():
    dist = 511 - np.arange(NTAB)
    n = np.maximum(dist, 0)
    nf = np.maximum(n, 1).astype(np.float32)
    half = N_BUCKETS // 2
    large = half + (np.log(nf / np.float32(half)) / np.float32(math.log(2048 / half))
                    * np.float32(N_BUCKETS - half)).astype(np.int32)
    bucket = np.where(n < half, n, np.minimum(large, N_BUCKETS - 1))
    t = np.zeros((N_BUCKETS + 1, 2, NTAB), np.float32)
    t[bucket, :, np.arange(NTAB)] = 1.0
    count = (dist <= 128).astype(int) + (dist % 4 == 0) + (dist % 16 == 0)
    t[N_BUCKETS, 0] = np.where((dist >= 0) & (dist <= 127), 0.0, NEG)
    t[N_BUCKETS, 1] = np.where((dist >= 0) & (count > 0), np.log(np.maximum(count, 1)), NEG)
    return t


def rope_table():
    t = np.arange(TL)
    freq = (10000.0 ** (-np.arange(8, dtype=np.float32) / 8)).astype(np.float32)
    ang = np.concatenate([(t // 64)[None, :] * freq[:, None], (t % 64)[None, :] * freq[:, None]]).astype(np.float32)
    out = np.zeros((P, TL), np.float32)
    out[64:96] = np.concatenate([np.cos(ang), np.cos(ang)])
    out[96:128] = np.concatenate([-np.sin(ang), np.sin(ang)])
    return out


def dft_slabs(n):
    ang = 2 * np.pi * (np.outer(np.arange(n), np.arange(n)) % n) / n
    mats = [m.astype(np.float32).reshape(n // P, P, n).transpose(1, 0, 2).reshape(P, -1) for m in (np.cos(ang), np.sin(ang))]
    return np.concatenate(mats, axis=1).reshape(P, -1, SLAB).transpose(1, 0, 2)


def channel_dft(n):
    ang = 2 * np.pi * (np.outer(np.arange(64), np.arange(64)) % 64) / 64
    s = 1.0 / math.sqrt(n * 64)
    out = np.zeros((2, P, P), np.float32)
    for g in (0, 64):
        out[0, g:g + 64, g:g + 64] = np.cos(ang) * s
        out[1, g:g + 64, g:g + 64] = -np.sin(ang) * s
    return out


class Cols:
    def __init__(self):
        self.at, self.n = {}, 0

    def add(self, name, tiles):
        self.at[name] = self.n
        self.n += tiles


COLS = Cols()
for _n in ("ffn1_pre_g", "ffn1_post_g", "attn_pre_g", "b_out", "attn_post_g", "ffn2_pre_g", "ffn2_post_g",
           "ple_pre_g", "ple_post_g", "zero", "g_final"):
    COLS.add(_n, KD)
COLS.add("b_in", 18)
for _l in range(2):
    for _n, _k in (("b_ada", NMOD), ("g_mix", KD), ("b_f", 2), ("g_q", 3), ("g_kv", 1), ("g_ffn", KD),
                   ("w_dw0", 2 * KF), ("w_dw1", 2 * KF), ("w_dw2", 2 * KF), ("b_dw", 2 * KF)):
        COLS.add(f"{_n}{_l}", _k)


class Role:
    def __init__(self, sem, primed=0):
        self.sem, self.n, self.primed = sem, primed, primed

    def span(self, units):
        s = Span(self.sem, self.n)
        self.n += units
        return s


class Span:
    def __init__(self, sem, base):
        self.sem, self.base = sem, base

    def wait(self, e, k):
        v = self.base + k + 1
        if not isinstance(v, int) or v > 0:
            e.wait_ge(self.sem, v)


def units(e, n, body, fn):
    full = n // body if n // body >= 2 else 0
    if full:
        with e.Fori(0, full) as i:
            for j in range(body):
                fn(j, i)
    for k in range(full * body, n):
        fn(k % body, k // body)


def skewed(e, bodies, size, stages):
    def step(b, j, lo, hi):
        for lag, fn in stages:
            back = 0
            jj = j - lag
            while jj < 0:
                jj += size
                back += 1
            if lo is not None and b - back < lo:
                continue
            if hi is not None and b - back >= hi:
                continue
            fn(b - back if back else b, jj)

    assert max(lag for lag, _ in stages) <= size
    for j in range(size):
        step(0, j, 0, bodies)
    if bodies > 1:
        with e.Fori(1, bodies) as i:
            for j in range(size):
                step(i, j, None, None)
    for j in range(max(lag for lag, _ in stages)):
        step(bodies, j, 0, bodies)


def build(nc, d):
    ctx = ExitStack()
    with ctx:
        base0 = 16512
        top = 229344
        place = {"next": base0}

        def sb(name, shape, dt=F32, at=None):
            size = int(np.prod(shape[1:])) * 4
            if at is None:
                at = place["next"]
                place["next"] += (size + 31) // 32 * 32
                assert place["next"] <= top, name
            return nc.alloc_sbuf_tensor_at(name, shape, dt, offset=at)

        KB = 1024
        cols = sb("cols", [P, COLS.n])
        ident = sb("ident", [P, P])
        flip = sb("flip", [P, P])
        ones = sb("ones", [P, P])
        mod = sb("mod", [P, 2, NMOD, 2])
        gains = sb("gains", [P, 2, 2, 2, KD])
        sinks = sb("sinks", [P, 16])
        rel = sb("rel", [N_BUCKETS + 1, 16])
        small = sb("small", [P, 64])
        rinv = sb("rinv", [P, 8])
        eps = sb("eps", [P, 2])
        qb8 = sb("qb8", [P, 8])
        x = sb("x", [P, KD, TL])
        CX = place["next"]
        cx = sb("cx", [P, KD, TC])
        raw = sb("raw", [P, RAW, SLAB])
        whi = sb("whi", [P, HL, SLAB], F32R)
        wlo = sb("wlo", [P, HL, SLAB], F32R)
        AR = place["next"]
        ada = sb("ada", [P, 2, SLAB])
        XN = place["next"]
        xnh = sb("xnh", [P, KD, TL], F32R)
        xnl = sb("xnl", [P, KD, TL], F32R)
        HM = place["next"]
        hmh = sb("hmh", [P, KF, TL], F32R)
        hml = sb("hml", [P, KF, TL], F32R)
        SH = place["next"]
        sil = sb("sil", [P, TL])
        hbuf = sb("hbuf", [P, 2, TL])
        RP = place["next"]
        rope = sb("rope", [P, TL])
        yg = sb("yg", [P, 2, TL], at=AR)
        yv = sb("yv", [P, 2, TL], at=AR + 4 * KB)
        rstd = sb("rstd", [P, TL], at=SH)
        tmp = sb("tmp", [P, 2, TL], at=SH + 2 * KB)
        nt = dict(sq=sb("nt_sq", [P, 4, TL], at=HM + 60 * KB), rstd=rstd, tmp=tmp)
        fsb = sb("fsb", [P, 4, TL], at=XN)
        pn_ffn = dict(sq=sb("pf_sq", [P, 4, TL], at=XN + 8 * KB), rstd=rstd, tmp=tmp)
        pn_hm = dict(sq=sb("ph_sq", [P, 4, TL], at=HM + 48 * KB), rstd=rstd, tmp=tmp)
        f_hm = sb("f_hm", [P, KD, TL], at=HM + 72 * KB)
        nt2 = {k: sb("nt2_" + k, s, at=HM + o * KB) for k, s, o in
               (("sq", [P, 1, TL], 68), ("rstd", [P, TL], 70), ("tmp", [P, 1, TL], 86))}
        silu_c = sb("silu_c", [P, 2, D], at=CX)
        prod = sb("prod", [P, D], at=RP)
        assert RP + 4 * D <= top
        onehot = sb("onehot", [N_BUCKETS + 1, 2, NTAB], at=HM)
        tab = sb("tab", [8, 4, NTAB // 2], at=HM + 8 * KB)
        q1 = sb("q1", [HD, 16, TL], at=HM)
        k1 = sb("k1", [HD, 12, TL], at=HM + 32 * KB)
        v1 = sb("v1", [P, 4, 12 * HD], at=HM + 56 * KB)
        qst1 = sb("qst1", [HD, 2, TL], at=HM + 68 * KB)
        strip = sb("strip", [P, 2, TL], at=HM + 72 * KB)
        p1 = sb("p1", [P, 2, TL], at=HM + 76 * KB)
        pt1 = sb("pt1", [P, 2, TL], at=HM + 80 * KB)
        vt1 = sb("vt1", [P, 2, TL], at=HM + 84 * KB)
        mix1 = sb("mix1", [P, 4, 2 * TL], at=XN)
        m1h = sb("m1h", [P, KD, TL], F32R, at=HM)
        m1l = sb("m1l", [P, KD, TL], F32R, at=HM + 16 * KB)
        sg = sb("sg", [P, KD, TL], at=HM)
        p_raw = sb("p_raw", [P, 2, TL], at=HM + 36 * KB)
        ph = sb("ph", [P, 2, TL], F32R, at=HM + 40 * KB)
        pl = sb("pl", [P, 2, TL], F32R, at=HM + 44 * KB)
        q2 = sb("q2", [96, MLA_H, TL], at=HM)
        k2 = sb("k2", [96, MLA_H, TL + TC], at=HM + 24 * KB)
        v2 = sb("v2", [P, 6, MLA_H * HD], at=HM + 60 * KB)
        qst2 = sb("qst2", [96, 2, TL], at=HM + 78 * KB)
        p2 = sb("p2", [P, 2, TL + TC], at=HM + 82 * KB)
        pt2 = sb("pt2", [P, 2, TL + TC], at=SH)
        mix2 = sb("mix2", [P, 4, MLA_H * HD], at=XN + 4 * KB)
        m2h = sb("m2h", [P, 6, TL], F32R, at=HM)
        m2l = sb("m2l", [P, 6, TL], F32R, at=HM + 12 * KB)
        rt2 = sb("rt2", [96, 2, TL], at=XN + 12 * KB)
        finh = sb("finh", [P, 4, 256], F32R, at=HM)
        finl = sb("finl", [P, 4, 256], F32R, at=HM + 4 * KB)
        fh = sb("fh", [P, 2, TL], F32R, at=HM)
        fl = sb("fl", [P, 2, TL], F32R, at=HM + 4 * KB)
        pqh = sb("pqh", [P, 4, TL], F32R, at=HM + 8 * KB)
        pql = sb("pql", [P, 4, TL], F32R, at=HM + 16 * KB)
        cq = sb("cq", [P, 4, TL], at=HM + 78 * KB)
        cnh = sb("cnh", [P, 4, TL], F32R, at=XN + 4 * KB)
        cnl = sb("cnl", [P, 4, TL], F32R, at=XN + 20 * KB)
        yout = sb("yout", [P, KD, TL], at=XN)

        ps = ctx.enter_context(nc.psum_tensor("ps", [P, 8, TL], F32))

        def sem(name):
            return ctx.enter_context(nc.semaphore(name))

        s_setup = sem("setup_loads")
        x_full = [sem(f"x_full{c}") for c in range(KD // 2)]
        s_out = sem("output_stores")
        s_tab = sem("bias_table_stored")
        s_pload = sem("p_loaded")
        s_krope = sem("krope_spread")
        s_cload = sem("conditioning_loaded")
        s_block2 = sem("block2_loads")
        raw_full = [sem(f"raw_full{i}") for i in range(RAW)]
        ada_full = [sem(f"ada_full{i}") for i in range(2)]
        strip_full = [sem(f"strip_full{i}") for i in range(2)]
        count = {"slabs": 0, "ada": 0, "strips": 0, "krope": 0}
        r = {}
        for name, primed in (
                ("slab_hi", 0), ("slab_lo", 0), ("slab_used", 0), ("prod", 0), ("prod_d", 0), ("mod_acc", 2), ("mod", 0), ("gain", 0),
                ("const", 0), ("silu_c", 0), ("tab_mm", 0), ("tab_sb", 0),
                ("sil", 0), ("h", 2), ("h_hi", 0), ("h_lo", 2), ("yg", 0), ("yv", 0), ("cg", 0), ("cv", 0),
                ("x", 0), ("xp", 0), ("cx", 4), ("fsb", 0), ("sq", 0), ("acc", 0), ("ss", 0), ("std", 0), ("rstd", 0),
                ("tmp", 0), ("xn_hi", 0), ("xn", 0), ("upd", 0), ("ev_a", 4), ("ev_d", 4),
                ("qst", 0), ("S", 0), ("mx", 0), ("negm", 0), ("exp", 0), ("es", 0), ("tot", 0), ("rinv", 0),
                ("PT", 0), ("cp_a", 0), ("cp_d", 0), ("pv", 0), ("o", 0),
                ("mt_mm", 0), ("mt_hi", 0), ("mt", 0), ("fin_hi", 0), ("fin", 0), ("pq_hi", 0), ("pq", 0),
                ("f_mm", 0), ("f_hi", 0), ("f", 0), ("four_hi", 0), ("four", 0), ("cq", 0), ("kr", 0),
                ("rot", 0), ("q_add", 0), ("vt", 0), ("p_hi", 0), ("p_lo", 0), ("e", 0), ("sg", 4), ("y", 0), ("qb", 0), ("yout", 0)):
            r[name] = Role(sem(name), primed)

        def take(kind, n):
            b = count[kind]
            count[kind] += n
            return b

        def col(name, n=0):
            return cols[:, bass.ds(COLS.at[name] + n, 1)]

        hi_done, lo_done, used = r["slab_hi"].span(0), r["slab_lo"].span(0), r["slab_used"].span(0)

        def load(e, s0, i):
            lo_done.wait(e, s0 + BODY * i - RAW)
            e.dma_start(raw[:, s0 % RAW, :], d["ws"][bass.ds(s0 + BODY * i, 1)].rearrange("a p n -> (a p) n")) \
                .then_inc(raw_full[s0 % RAW], 16)

        def split_hi(e, s0, i=0):
            if isinstance(i, int) and s0 + BODY * i >= count["slabs"]:
                return
            e.wait_ge(raw_full[s0 % RAW], 16 * (s0 // RAW + 1) + 16 * (BODY // RAW) * i)
            used.wait(e, s0 + BODY * i - HL)
            e.activation(whi[:, s0 % HL, :], raw[:, s0 % RAW, :], ACT.Copy).then_inc(hi_done.sem, 1)

        def split_lo(e, s0, i=0):
            if isinstance(i, int) and s0 + BODY * i >= count["slabs"]:
                return
            hi_done.wait(e, s0 + BODY * i)
            e.tensor_tensor(wlo[:, s0 % HL, :], raw[:, s0 % RAW, :], whi[:, s0 % HL, :].bitcast(F32),
                            ALU.subtract).then_inc(lo_done.sem, 1)

        def slab(s0):
            return whi[:, s0 % HL, :], wlo[:, s0 % HL, :]

        def ring_act(e, base, n, evac=lambda j, i: None):
            def step(j, i):
                used.wait(e, base + BODY * i + j)
                evac(j, i)
                split_hi(e, base + j + HL, i)
            units(e, n, BODY, step)

        def ring_dve(e, base, n, evac=lambda j, i: None):
            def step(j, i):
                used.wait(e, base + BODY * i + j)
                evac(j, i)
                split_lo(e, base + j + HL, i)
            units(e, n, BODY, step)

        def ring_pe(e, base, n, mms):
            def step(j, i):
                lo_done.wait(e, base + BODY * i + j)
                mms(j, i, *slab(base + j)).then_inc(used.sem, 1)
            units(e, n, BODY, step)

        def mm3(e, out, a, b, start, stop):
            e.matmul(out, a[0], b[0], start=start, stop=False, skip_group_check=True)
            e.matmul(out, a[0], b[1], start=False, stop=False, skip_group_check=True)
            return e.matmul(out, a[1], b[0], start=False, stop=stop, skip_group_check=True)

        def blk(pair, b, n=P):
            return tuple(w[:, b * n:(b + 1) * n] for w in pair)

        def dense(e, out, w, acts, T, kb=KD, wait_k=None):
            for k in range(kb):
                if wait_k is not None:
                    wait_k(k)
                act = acts[k] if isinstance(acts, list) else tuple(a[:, k, 0:T] for a in acts)
                mm = mm3(e, out, blk(w, k), act, k == 0, k == kb - 1)
            return mm

        phases = []

        class Phase:
            guest = None

            def __init__(self):
                phases.append(self)

            def pe(self, e): pass
            def act(self, e): pass
            def dve(self, e): pass
            def pool(self, e): pass

        def load_x(e, c):
            e.dma_start(x[:, 2 * c:2 * c + 2, :], d["xT"][:, 2 * c:2 * c + 2, :]).then_inc(x_full[c], 16)

        class Setup(Phase):
            LOADS = 7

            def __init__(self):
                super().__init__()
                self.const = r["const"].span(4)
                self.qb = r["qb"].span(1)
                self.silu = r["silu_c"].span(1)
                self.first = None
                self.mm = r["tab_mm"].span(1)
                self.tsb = r["tab_sb"].span(1)

            def wait(self, e):
                e.wait_ge(s_setup, 16 * self.LOADS)

            def pool(self, e):
                for n, (dst, v) in enumerate(((ones[:], 1.0), (rel[N_BUCKETS:N_BUCKETS + 1, :], 1.0), (eps[:, 0:1], EPS),
                                              (eps[:, 1:2], 4 * EPS))):
                    self.const.wait(e, n - 1)
                    e.memset(dst, v).then_inc(self.const.sem, 1)
                self.const.wait(e, 3)
                for ro in r.values():
                    if ro.primed:
                        e.sem_inc(ro.sem, ro.primed)

            def act(self, e):
                for c in range(2):
                    load_x(e, c)
                for dst, src in ((cols[:], d["cols"]), (onehot[:], d["onehot"]), (rel[0:N_BUCKETS, :], d["rel_bias"]),
                                 (ident[:], d["ident"]), (flip[:], d["flip"]), (sinks[:, 0:8], d["sinks"].partition_broadcast(P)),
                                 (sinks[:, 8:16], d["no_sinks"].partition_broadcast(P))):
                    e.dma_start(dst, src).then_inc(s_setup, 16)
                e.dma_start(silu_c[:], d["c"].partition_broadcast(P)).then_inc(s_cload, 16)
                self.const.wait(e, 3)
                self.first.act_squares(e)
                for s in range(RAW):
                    split_hi(e, s)

            def act_rest(self, e):
                self.wait(e)
                self.mm.wait(e, 0)
                e.activation(tab[:], ps[0:8, 0:4, 0:NTAB // 2], ACT.Copy).then_inc(self.tsb.sem, 1)
                self.tsb.wait(e, 0)
                for m in range(2):
                    e.dma_start(d["tables"][m].rearrange("h (c x) -> h c x", c=2),
                                tab[:, 2 * m:2 * m + 2, :]).then_inc(s_tab, 16)
                self.first.act_hi(e)
                for s in range(RAW, HL):
                    split_hi(e, s)
                e.wait_ge(s_cload, 16)
                e.activation(silu_c[:], silu_c[:], ACT.Silu).then_inc(self.silu.sem, 1)
                e.wait_ge(s_tab, 32)

            def pe(self, e):
                self.const.wait(e, 3)

            def pe_rest(self, e):
                self.wait(e)
                for m in range(2):
                    for c in range(2):
                        mm = e.matmul(ps[0:8, 2 * m + c, 0:320], rel[:, 8 * m:8 * m + 8],
                                      onehot[:, m, c * 320:(c + 1) * 320], start=True, stop=True)
                mm.then_inc(self.mm.sem, 1)
                self.tsb.wait(e, 0)

            def dve(self, e):
                for s in range(RAW):
                    split_lo(e, s)

            def dve_rest(self, e):
                for s in range(RAW, HL):
                    split_lo(e, s)
                b0 = COLS.at["b_in"]
                e.tensor_scalar(qb8[:], cols[:, b0:b0 + 8], 0.125, None, ALU.mult).then_inc(self.qb.sem, 1)

        class Norm:
            def __init__(self, srcs, ready, T, dim, t, gain=None, shift=None, outs=None, plain=None, bank=4):
                self.bank = bank
                self.srcs, self.ready, self.T, self.dim, self.t = srcs, ready, T, dim, t
                self.gain, self.shift, self.outs, self.plain = gain, shift, outs, plain
                n = self.n = len(srcs)
                self.pairs = (n + 1) // 2
                self.sq, self.acc, self.ss = r["sq"].span(n), r["acc"].span(n // 2), r["ss"].span(self.pairs)
                self.std, self.rs = r["std"].span(1), r["rstd"].span(1)
                if outs is not None:
                    self.tmp, self.hi, self.out = r["tmp"].span(n), r["xn_hi"].span(n), r["xn"].span(n)
                if plain is not None:
                    self.out = r["yout"].span(n)

            def act_squares(self, e, first=0, last=None):
                for n in range(first, self.n if last is None else last):
                    self.ready(e, n)
                    if n >= 4:
                        self.ss.wait(e, (n - 4) // 2)
                    e.activation(self.t["sq"][:, n % 4, 0:self.T], self.srcs[n], ACT.Square).then_inc(self.sq.sem, 1)

            def pool_add(self, e, p):
                self.sq.wait(e, 2 * p + 1)
                a, b_ = (self.t["sq"][:, (2 * p + q) % 4, 0:self.T] for q in range(2))
                e.tensor_tensor(a, a, b_, ALU.add).then_inc(self.acc.sem, 1)

            def pool_adds(self, e):
                for p in range(self.n // 2):
                    self.acc.wait(e, p - 1)
                    self.pool_add(e, p)

            def pe_stats(self, e, first=0, last=None):
                for p in range(first, self.pairs if last is None else last):
                    if 2 * p + 1 < self.n:
                        self.acc.wait(e, p)
                    else:
                        self.sq.wait(e, 2 * p)
                    e.matmul(ps[:, self.bank, 0:self.T], ones[:], self.t["sq"][:, 2 * p % 4, 0:self.T], start=p == 0,
                             stop=p == self.pairs - 1, skip_group_check=True).then_inc(self.ss.sem, 1)

            def act_std(self, e, half=False):
                self.ss.wait(e, self.pairs - 1)
                f = 4.0 if half else 1.0
                e.activation(self.t["rstd"][:, 0:self.T], ps[:, self.bank, 0:self.T], ACT.Sqrt,
                             scale=f / self.dim, bias=eps[:, int(half):int(half) + 1]).then_inc(self.std.sem, 1)

            def dve_rstd(self, e):
                self.std.wait(e, 0)
                e.reciprocal(self.t["rstd"][:, 0:self.T], self.t["rstd"][:, 0:self.T]).then_inc(self.rs.sem, 1)

            def act_hi(self, e):
                for n in range(self.n):
                    self.tmp.wait(e, n)
                    e.activation(self.outs[0][:, n, 0:self.T], self.t["tmp"][:, n % 2, 0:self.T], ACT.Identity,
                                 bias=self.shift(n)).then_inc(self.hi.sem, 1)

            def dve_tiles(self, e):
                self.rs.wait(e, 0)
                def lo(n):
                    self.hi.wait(e, n)
                    e.scalar_tensor_tensor(out=self.outs[1][:, n, 0:self.T], in0=self.t["tmp"][:, n % 2, 0:self.T],
                                           scalar=self.shift(n), in1=self.outs[0][:, n, 0:self.T].bitcast(F32),
                                           op0=ALU.add, op1=ALU.subtract).then_inc(self.out.sem, 1)
                for n in range(self.n):
                    if n >= 2:
                        self.out.wait(e, n - 2)
                    e.scalar_tensor_tensor(out=self.t["tmp"][:, n % 2, 0:self.T], in0=self.srcs[n],
                                           scalar=self.gain(n), in1=self.t["rstd"][:, 0:self.T],
                                           op0=ALU.mult, op1=ALU.mult).then_inc(self.tmp.sem, 1)
                    if n >= 1:
                        lo(n - 1)
                lo(self.n - 1)

            def dve_plain(self, e):
                self.rs.wait(e, 0)
                for n in range(self.n):
                    e.scalar_tensor_tensor(out=self.plain[:, n, 0:self.T], in0=self.srcs[n], scalar=self.gain(n),
                                           in1=self.t["rstd"][:, 0:self.T], op0=ALU.mult,
                                           op1=ALU.mult).then_inc(self.out.sem, 1)

        class Modulation:
            def __init__(self, l):
                self.l, self.first = l, take("ada", NMOD)
                self.prod, self.prod_d = r["prod"].span(NMOD), r["prod_d"].span(NMOD)
                self.acc = r["mod_acc"].span(2 * NMOD)
                self.mod, self.gain = r["mod"].span(1), r["gain"].span(4)

            def pool(self, e):
                setup.silu.wait(e, 0)

                def tile(j, i):
                    a = 2 * i + j
                    e.wait_ge(ada_full[j], 16 * (self.first // 2 + 1) + 16 * i)
                    self.acc.wait(e, 2 * a - 2)
                    e.tensor_tensor(prod[:], ada[:, j, :], silu_c[:, 0, :], ALU.mult).then_inc(self.prod.sem, 1)
                units(e, NMOD, 2, tile)

            def dve(self, e, a, slot):
                self.prod.wait(e, a)
                e.tensor_tensor(ada[:, slot, :], ada[:, slot, :], silu_c[:, 1, :], ALU.mult).then_inc(self.prod_d.sem, 1)

            def act(self, e, a, slot):
                for v, (done, p_) in enumerate(((self.prod, prod[:]), (self.prod_d, ada[:, slot, :]))):
                    done.wait(e, a)
                    e.activation(p_, p_, ACT.Copy, accum_out=mod[:, self.l, bass.ds(a, 1), v]).then_inc(self.acc.sem, 1)

            def finish(self, e):
                self.acc.wait(e, 2 * NMOD - 1)
                l, c = self.l, COLS.at[f"b_ada{self.l}"]
                e.tensor_tensor(mod[:, l], mod[:, l], cols[:, c:c + NMOD].unsqueeze(2).broadcast_to([P, NMOD, 2]),
                                ALU.add).then_inc(self.mod.sem, 1)
                self.mod.wait(e, 0)
                for st in range(2):
                    for w, (g0, g) in enumerate(((8, "g_mix"), (32, "g_ffn"))):
                        c = COLS.at[f"{g}{l}"]
                        e.scalar_tensor_tensor(out=gains[:, l, st, w, :], in0=mod[:, l, g0:g0 + KD, st], scalar=1.0,
                                               in1=cols[:, c:c + KD], op0=ALU.add, op1=ALU.mult) \
                            .then_inc(self.gain.sem, 1)

        class Tiles:
            def __init__(self, units_):
                self.units = units_

            def wait(self, e, n):
                sp, k = self.units[n]
                sp.wait(e, k)

        class PreNorm(Phase):
            def __init__(self, stream, ready, gain, shift, post=None, std_free=lambda e: None, host=None, whole=False):
                super().__init__()
                xs, T = stream
                self.norm = Norm([xs[:, n, 0:T] for n in range(KD)], ready, T, D, pn_ffn if whole else nt, gain, shift,
                                 (xnh, xnl))
                self.out, self.pool_first, self.std_free = self.norm.out, 0, std_free
                self.stats, self.tiles = host is None, not whole
                if post is not None:
                    post.next, self.pool_first = self.norm, 2
                if host is not None:
                    self.host, host.guest = host, self.norm

            def act(self, e):
                if self is first_pre:
                    self.norm.act_std(e)
                elif self.stats:
                    self.norm.act_squares(e)
                    self.std_free(e)
                    self.norm.act_std(e)
                if self is first_pre:
                    setup.act_rest(e)
                elif self.tiles:
                    self.norm.act_hi(e)

            def pool(self, e):
                for p in range(self.pool_first, KD // 2):
                    self.norm.acc.wait(e, p - 1)
                    self.norm.pool_add(e, p)

            def pe(self, e):
                if self.stats:
                    self.norm.pe_stats(e)
                if self is first_pre:
                    setup.pe_rest(e)
                if not self.tiles:
                    self.host.out.wait(e, KD - 1)

            def dve(self, e):
                if self.stats:
                    self.norm.dve_rstd(e)
                if self is first_pre:
                    setup.wait(e)
                if self.tiles:
                    self.norm.dve_tiles(e)
                if self is first_pre:
                    setup.dve_rest(e)

        class PostNorm(Phase):
            POOL = (1, 3, 5)

            def __init__(self, srcs, ready, t, gain, half, early=0):
                super().__init__()
                self.norm = Norm(srcs, ready, TL, D, t, gain)
                self.half, self.early, self.gain, self.next = half, early, gain, None
                self.upd = r["upd"].span(KD)
                on_dve, on_pool = r["x"].span(KD - len(self.POOL)), r["xp"].span(len(self.POOL))
                dve_tiles = [n for n in range(KD) if n not in self.POOL]
                self.out = Tiles([(on_pool, self.POOL.index(n)) if n in self.POOL else (on_dve, dve_tiles.index(n))
                                  for n in range(KD)])

            def act(self, e):
                self.norm.act_squares(e, self.early)
                self.norm.act_std(e, self.half)

            def add(self, e, n):
                self.upd.wait(e, n)
                e.tensor_tensor(x[:, n, :], x[:, n, :], self.norm.t["tmp"][:, n % 2, :], ALU.add) \
                    .then_inc(self.out.units[n][0].sem, 1)

            def pe(self, e):
                self.norm.pe_stats(e)

            def pool(self, e):
                self.norm.pool_adds(e)
                for n in self.POOL:
                    if n > 1:
                        self.out.wait(e, n - 2)
                    self.add(e, n)
                    if n > 1 and self.next is not None:
                        self.next.acc.wait(e, (n - 3) // 2 - 1)
                        self.next.pool_add(e, (n - 3) // 2)

            def dve(self, e):
                m = self.norm
                m.dve_rstd(e)
                m.rs.wait(e, 0)
                for n in range(KD):
                    if n >= 2:
                        self.out.wait(e, n - 2)
                    e.scalar_tensor_tensor(out=m.t["tmp"][:, n % 2, :], in0=m.srcs[n], scalar=self.gain(n),
                                           in1=m.t["rstd"][:], op0=ALU.mult, op1=ALU.mult).then_inc(self.upd.sem, 1)
                    if n >= 1 and n - 1 not in self.POOL:
                        self.add(e, n - 1)
                self.add(e, KD - 1)

        class GateUp(Phase):
            def __init__(self, T, xn, conv=None, mods=None):
                super().__init__()
                self.T, self.xn, self.conv, self.mods = T, xn, conv, mods
                self.base = take("slabs", 2 * KF)
                self.sil, self.h = r["sil"].span(KF), r["h"].span(KF)
                self.h_hi, self.h_lo = r["h_hi"].span(KF), r["h_lo"].span(KF)
                if conv is not None:
                    self.yg, self.yv = r["yg"].span(KF), r["yv"].span(KF)
                    self.cg, self.cv = r["cg"].span(2 * KF), r["cv"].span(2 * KF)

            def pe(self, e):
                T, acts = self.T, (xnh, xnl)

                def mms(j, i, hi, lo):
                    if j % 2 == 0:
                        self.h.wait(e, 2 * i + j // 2 - 2)
                    mm = dense(e, ps[:, j, 0:T], (hi, lo), acts, T,
                               wait_k=(lambda k: self.xn.wait(e, k)) if j == 0 else None)
                    return mm

                ring_pe(e, self.base, 2 * KF, mms)

            def act(self, e):
                T = self.T

                def hid(m, q):
                    self.h.wait(e, m)
                    e.activation(hmh[:, bass.ds(m, 1), 0:T].rearrange("p a t -> p (a t)"), hbuf[:, q, 0:T],
                                 ACT.Copy).then_inc(self.h_hi.sem, 1)

                def evac(j, i):
                    q, m = j // 2, 2 * i + j // 2
                    if self.conv is None:
                        if j % 2 == 0:
                            self.h.wait(e, m - 1)
                            e.activation(sil[:, 0:T], ps[:, j, 0:T], ACT.Silu).then_inc(self.sil.sem, 1)
                        else:
                            split_hi(e, self.base + j + HL, i)
                            hid(m, q)
                        return
                    l = self.conv
                    y, ro, off = (yg, self.yg, 0) if j % 2 == 0 else (yv, self.yv, KF)
                    self.h.wait(e, m - 2)
                    e.activation(y[:, q, 0:T], ps[:, j, 0:T], ACT.Copy, scale=col(f"w_dw1{l}", m + off)) \
                        .then_inc(ro.sem, 1)
                    if j % 2 == 1:
                        self.cg.wait(e, 2 * m + 1)
                        self.h.wait(e, m - 1)
                        e.activation(sil[:, 0:T], yg[:, q, 0:T], ACT.Silu, bias=col(f"b_dw{l}", m)) \
                            .then_inc(self.sil.sem, 1)
                        split_hi(e, self.base + j + HL, i)
                        hid(m, q)

                def step(j, i):
                    used.wait(e, self.base + BODY * i + j)
                    evac(j, i)
                    if j % 2 == 0:
                        split_hi(e, self.base + j + HL, i)
                    if self.mods is not None:
                        self.mods.act(e, BODY * i + j, j % 2)
                units(e, 2 * KF, BODY, step)

            def pool(self, e):
                if self.mods is not None:
                    self.mods.pool(e)

            def dve(self, e):
                T = self.T

                def make_h(m, q, up):
                    self.sil.wait(e, m)
                    self.h_lo.wait(e, m - 2)
                    if self.conv is None:
                        e.tensor_tensor(hbuf[:, q, 0:T], sil[:, 0:T], up, ALU.mult).then_inc(self.h.sem, 1)
                    else:
                        e.scalar_tensor_tensor(out=hbuf[:, q, 0:T], in0=up, scalar=col(f"b_dw{self.conv}", m + KF),
                                               in1=sil[:, 0:T], op0=ALU.add, op1=ALU.mult).then_inc(self.h.sem, 1)

                def lo(m, q):
                    self.h_hi.wait(e, m)
                    dst = (slice(None), bass.ds(m, 1), slice(0, T))
                    e.tensor_tensor(hml[dst].rearrange("p a t -> p (a t)"), hbuf[:, q, 0:T],
                                    hmh[dst].rearrange("p a t -> p (a t)").bitcast(F32),
                                    ALU.subtract).then_inc(self.h_lo.sem, 1)

                def conv(j, m, q):
                    l = self.conv
                    y, ro, dn, off = (yg, self.yg, self.cg, 0) if j % 2 == 0 else (yv, self.yv, self.cv, KF)
                    ro.wait(e, m)
                    for k, (o, s, w) in enumerate(((slice(1, T), slice(0, T - 1), f"w_dw0{l}"),
                                                   (slice(0, T - 1), slice(1, T), f"w_dw2{l}"))):
                        if k:
                            dn.wait(e, 2 * m)
                        e.scalar_tensor_tensor(out=y[:, q, o], in0=ps[:, j, s], scalar=col(w, m + off), in1=y[:, q, o],
                                               op0=ALU.mult, op1=ALU.add).then_inc(dn.sem, 1)

                def step(j, i):
                    q, m = j // 2, 2 * i + j // 2
                    used.wait(e, self.base + BODY * i + j)
                    if self.conv is not None:
                        conv(j, m, q)
                    if j % 2 == 1:
                        if self.conv is None:
                            make_h(m, q, ps[:, j, 0:T])
                            if self.mods is not None:
                                self.mods.dve(e, BODY * i + j, j % 2)
                            split_lo(e, self.base + j + HL, i)
                        else:
                            self.cv.wait(e, 2 * m + 1)
                            make_h(m, q, yv[:, q, 0:T])
                            split_lo(e, self.base + j + HL, i)
                        lo(m, q)
                    else:
                        if self.mods is not None:
                            self.mods.dve(e, BODY * i + j, j % 2)
                        split_lo(e, self.base + j + HL, i)
                units(e, 2 * KF, BODY, step)

        class Down(Phase):
            SH = KF // 2

            def __init__(self, T, gu, stream=None, gate=None, x_role=None):
                super().__init__()
                self.T, self.gu, self.gate = T, gu, gate
                self.stream = stream
                self.base = take("slabs", 2 * self.SH)
                if gate is None:
                    self.fsb = r["fsb"].span(4)
                else:
                    self.out = r[x_role].span(KD)

            def halves(self, e, step):
                for hf in range(2):
                    b = self.base + hf * self.SH
                    for j in range(3):
                        step(hf, b, j, 0, j)
                    with e.Fori(0, 2) as i:
                        for j in range(BODY):
                            step(hf, b + 3, j, i, 3 + j + BODY * i)

            def bank(self, n):
                return n + 4 if n < 4 else n - 4

            def mod_tile(self, hf, k):
                if self.gu.mods is None or not isinstance(k, int):
                    return None
                return {(0, 0): 44, (0, 1): 45, (0, 2): 46, (1, 1): 47}.get((hf, k))

            def pe(self, e):
                T = self.T

                def step(hf, b, j, i, k):
                    lo_done.wait(e, b + BODY * i + j)
                    if hf == 0:
                        self.gu.h_lo.wait(e, 2 * k + 1)
                    w = slab(b + j)
                    for kk in range(2):
                        act = tuple(h[:, bass.ds(2 * k + kk, 1), 0:T].rearrange("p a t -> p (a t)") for h in (hmh, hml))
                        for n in range(4):
                            mm = mm3(e, ps[:, self.bank(4 * hf + n), 0:T], blk(w, kk * 4 + n), act,
                                     isinstance(k, int) and k == 0 and kk == 0, True)
                    mm.then_inc(used.sem, 1)
                    if self.guest is not None and hf == 1 and isinstance(k, int):
                        if k == 1:
                            self.out.wait(e, 0)
                            self.guest.pe_stats(e, 0, 2)
                        elif k == 2:
                            self.guest.pe_stats(e, 2)
                self.halves(e, step)

            def act(self, e):
                def step(hf, b, j, i, k):
                    used.wait(e, b + BODY * i + j)
                    split_hi(e, b + j + HL, i)
                    if self.gate is None and hf == 1 and isinstance(k, int) and k == 0:
                        for n in range(4):
                            e.activation(fsb[:, n, :], ps[:, self.bank(n), :], ACT.Copy).then_inc(self.fsb.sem, 1)
                        self.post.norm.act_squares(e, 0, 4)
                    a = self.mod_tile(hf, k)
                    if a is not None:
                        self.gu.mods.act(e, a, a % 2)
                    if self.guest is not None and hf == 1 and isinstance(k, int):
                        if k < 2:
                            self.guest.act_squares(e, 4 * k, 4 * k + 4)
                        else:
                            self.guest.act_std(e)
                            self.guest.act_hi(e)
                self.halves(e, step)

            def update(self, e, hf):
                xs, T = self.stream
                for n in range(4 * hf, 4 * hf + 4):
                    e.scalar_tensor_tensor(out=xs[:, n, 0:T], in0=ps[:, self.bank(n), 0:T], scalar=self.gate(n),
                                           in1=xs[:, n, 0:T], op0=ALU.mult, op1=ALU.add).then_inc(self.out.sem, 1)

            def dve(self, e):
                def step(hf, b, j, i, k):
                    used.wait(e, b + BODY * i + j)
                    a = self.mod_tile(hf, k)
                    if a is not None:
                        self.gu.mods.dve(e, a, a % 2)
                    split_lo(e, b + j + HL, i)
                    if self.gu.mods is not None and hf == 1 and isinstance(k, int) and k == 2:
                        self.gu.mods.finish(e)
                    if self.gate is not None and hf == 1 and isinstance(k, int) and k == 0:
                        self.update(e, 0)
                    if self.guest is not None and hf == 1 and isinstance(k, int) and k == 2:
                        self.guest.dve_rstd(e)
                        self.guest.dve_tiles(e)
                self.halves(e, step)
                if self.gate is not None:
                    self.update(e, 1)

        def ffn_block1(l, pre_gain, post_gain, ready, post):
            pre = PreNorm((x, TL), ready, lambda n: col(pre_gain, n), lambda n: col("zero", n), post)
            gu = GateUp(TL, pre.out, mods=Modulation(l))
            gu.pre = pre
            down = Down(TL, gu)

            def f_ready(e, n):
                if n < 4:
                    down.fsb.wait(e, n)
                else:
                    used.wait(e, down.base + 2 * Down.SH - 1)
            srcs = [fsb[:, n, :] if n < 4 else ps[:, n - 4, :] for n in range(KD)]
            down.post = PostNorm(srcs, f_ready, pn_ffn, lambda n: col(post_gain, n), True, 4)
            return down.post, gu

        class Attention(Phase):
            def __init__(self, heads, tt, tiles, q, k, v, qst, p, pt, mix, dk, scale, ready, q0=0, kslot=None,
                         key0=0, vt0=0, mix0=0, bias=False, head0=0, dsplit=0, q_ready=None):
                super().__init__()
                self.heads, self.tt, self.tiles, self.q, self.k, self.v, self.qst_buf, self.p, self.pt, self.mix = heads, tt, tiles, q, k, v, qst, p, pt, mix
                self.dk, self.scale, self.ready, self.q0, self.kslot, self.key0, self.vt0, self.mix0, self.bias, self.head0, self.dsplit = dk, scale, ready, q0, kslot, key0, vt0, mix0, bias, head0, dsplit
                self.U, self.q_ready = 2 * tt, q_ready
                n = heads * tt
                self.S, self.mx, self.negm, self.exp, self.rinv, self.PT, self.pv = (
                    r[name].span(n) for name in ("S", "mx", "negm", "exp", "rinv", "PT", "pv"))
                self.cp_a, self.cp_d = r["cp_a"].span(n), r["cp_d"].span(n if dsplit else 0)
                self.qst, self.o = r["qst"].span(heads), r["o"].span(heads)
                if bias:
                    self.es, self.tot = r["es"].span(n), r["tot"].span(n)
                    self.strips0 = take("strips", heads // 2)

            def unit(self, b, j):
                return self.U * b + j, 2 * b + j // self.tt, j // self.tt, j % self.tt

            def cols_of(self, qt):
                t = self.tiles(qt)
                return t[0] * P, len(t) * P

            def s_ap(self, j, lo, n):
                return ps[:, 2 * (j % 2):2 * (j % 2) + 2, :].rearrange("p a t -> p (a t)")[:, lo:lo + n]

            def pool(self, e):
                self.q_ready(e)
                T = self.tt * P

                def stage(b, j):
                    h = 2 * b + j
                    self.S.wait(e, self.tt * (h - 1) - 1)
                    self.qst.wait(e, h - 1)
                    src = self.q[0:self.dk, bass.ds(h + self.q0, 1), 0:T].rearrange("p a t -> p (a t)")
                    e.tensor_copy(self.qst_buf[0:self.dk, j, 0:T], src).then_inc(self.qst.sem, 1)
                    if self.bias:
                        e.dma_start(strip[:, j, :], strips_view[bass.ds(h + self.head0, 1)]
                                    .rearrange("a p n -> (a p) n")).then_inc(strip_full[j], 16)
                if self.bias:
                    e.wait_ge(s_tab, 32)
                skewed(e, self.heads // 2, 2, [(0, stage)])

            def pe(self, e):
                self.ready(e)

                def scores(b, j):
                    u, h, par, qt = self.unit(b, j)
                    self.exp.wait(e, u - 2)
                    if qt == 0:
                        self.qst.wait(e, h)
                        if self.bias:
                            e.wait_ge(strip_full[par], 16 * (self.strips0 + b + 1))
                    c0, n = self.cols_of(qt)
                    if self.bias:
                        g0 = (3 - qt) * P + c0
                        e.matmul(self.s_ap(j, 0, n), flip[:], strip[:, par, g0:g0 + n], start=True, stop=False,
                                 skip_group_check=True)
                    for lo in range(0, n, 512):
                        m = min(512, n - lo)
                        kk = self.k[0:self.dk, bass.ds(self.kslot(b, par), 1), self.key0 + c0 + lo:self.key0 + c0 + lo + m]
                        mm = e.matmul(self.s_ap(j, lo, m), self.qst_buf[0:self.dk, par, qt * P:(qt + 1) * P],
                                      kk.rearrange("p a t -> p (a t)"), start=not self.bias, stop=True,
                                      skip_group_check=True)
                    mm.then_inc(self.S.sem, 1)

                def turn(b, j):
                    u, h, par, qt = self.unit(b, j)
                    self.exp.wait(e, u)
                    self.cp_a.wait(e, u - 1)
                    if self.dsplit:
                        self.cp_d.wait(e, u - 1)
                    _, n = self.cols_of(qt)
                    for t in range(n // P):
                        mm = e.transpose(ps[:, 4 + t // 4, (t % 4) * P:(t % 4 + 1) * P],
                                         self.p[:, j % 2, t * P:(t + 1) * P], ident[:])
                    mm.then_inc(self.PT.sem, 1)

                def pv(b, j):
                    u, h, par, qt = self.unit(b, j)
                    self.cp_a.wait(e, u)
                    if self.dsplit:
                        self.cp_d.wait(e, u)
                    if qt == 0:
                        self.o.wait(e, h - 2)
                    ts = self.tiles(qt)
                    for i_, t in enumerate(ts):
                        vv = self.v[:, self.vt0 + t, bass.ds(self.kslot(b, par) * HD, HD)]
                        mm = e.matmul(ps[:, 6 + par, qt * HD:(qt + 1) * HD], self.pt[:, j % 2, i_ * P:(i_ + 1) * P], vv,
                                      start=(i_ == 0), stop=(i_ == len(ts) - 1), skip_group_check=True)
                    mm.then_inc(self.pv.sem, 1)
                skewed(e, self.heads // 2, self.U, [(0, scores), (2, turn), (3, pv)])

            def sm(self, what, j):
                return small[:, 24 + 8 * what + j:25 + 8 * what + j]

            def dve(self, e):
                def rowmax(b, j):
                    u, h, par, qt = self.unit(b, j)
                    self.S.wait(e, u)
                    _, n = self.cols_of(qt)
                    e.tensor_reduce(self.sm(0, j), self.s_ap(j, 0, n), AX_X, ALU.max).then_inc(self.mx.sem, 1)
                    self.mx.wait(e, u)
                    if self.bias:
                        e.tensor_scalar(self.sm(1, j), self.sm(0, j), sinks[:, bass.ds(h + self.head0, 1)], -1.0, ALU.max,
                                        ALU.mult).then_inc(self.negm.sem, 1)
                    else:
                        e.tensor_scalar(self.sm(1, j), self.sm(0, j), -self.scale, None, ALU.mult) \
                            .then_inc(self.negm.sem, 1)

                def copy_t(b, j):
                    u, h, par, qt = self.unit(b, j)
                    self.PT.wait(e, u)
                    e.tensor_copy(self.pt[:, j % 2, 0:self.dsplit], ps[:, 4, 0:self.dsplit]).then_inc(self.cp_d.sem, 1)

                def inverse(b, j):
                    u, h, par, qt = self.unit(b, j)
                    src = self.sm(2, j)
                    if qt == 0:
                        self.o.wait(e, h - 2)
                    if self.bias:
                        self.es.wait(e, u)
                        e.tensor_tensor(self.sm(4, j), self.sm(2, j), self.sm(3, j), ALU.add).then_inc(self.tot.sem, 1)
                        self.tot.wait(e, u)
                        src = self.sm(4, j)
                    else:
                        self.exp.wait(e, u)
                    e.reciprocal(rinv[:, j:j + 1], src).then_inc(self.rinv.sem, 1)

                def finish(b, j):
                    u, h, par, qt = self.unit(b, j)
                    if qt < self.tt - 1:
                        return
                    self.pv.wait(e, u)
                    self.rinv.wait(e, u)
                    j0 = j - self.tt + 1
                    e.tensor_tensor(self.mix[:, 0:self.tt, bass.ds(h * HD + self.mix0, HD)],
                                    ps[:, 6 + par, 0:self.tt * HD].rearrange("p (t c) -> p t c", c=HD),
                                    rinv[:, j0:j0 + self.tt].unsqueeze(2).broadcast_to([P, self.tt, HD]),
                                    ALU.mult).then_inc(self.o.sem, 1)
                st = [(0, rowmax)] + ([(2, copy_t)] if self.dsplit else []) + [(2, inverse), (4, finish)]
                skewed(e, self.heads // 2, self.U, st)

            def act(self, e):
                def copy_t(b, j):
                    u, h, par, qt = self.unit(b, j)
                    self.PT.wait(e, u)
                    _, n = self.cols_of(qt)
                    n -= self.dsplit
                    bank = 5 if self.dsplit else 4
                    if n == 0:
                        raise AssertionError
                    e.activation(self.pt[:, j % 2, self.dsplit:self.dsplit + n], ps[:, bank, 0:n],
                                 ACT.Copy).then_inc(self.cp_a.sem, 1)

                def exps(b, j):
                    u, h, par, qt = self.unit(b, j)
                    self.negm.wait(e, u)
                    self.PT.wait(e, u - 2)
                    _, n = self.cols_of(qt)
                    e.activation(self.p[:, j % 2, 0:n], self.s_ap(j, 0, n), ACT.Exp, bias=self.sm(1, j),
                                 scale=self.scale, accum_out=self.sm(2, j)).then_inc(self.exp.sem, 1)
                    if self.bias:
                        e.activation(self.sm(3, j), sinks[:, bass.ds(h + self.head0, 1)], ACT.Exp,
                                     bias=self.sm(1, j)).then_inc(self.es.sem, 1)
                skewed(e, self.heads // 2, self.U, [(2, copy_t), (0, exps)])

        class MixTurn(Phase):
            def __init__(self, mix, n, tt, outs, ready):
                super().__init__()
                self.mix, self.n, self.tt = mix, n, tt
                self.outs, self.ready = outs, ready
                self.mm, self.hi, self.out = r["mt_mm"].span(n), r["mt_hi"].span(n), r["mt"].span(n)

            def pe(self, e):
                self.ready(e)
                for c in range(self.n):
                    if c >= 4:
                        self.out.wait(e, c - 4)
                    for t in range(self.tt):
                        mm = e.transpose(ps[:, c % 4, t * P:(t + 1) * P], self.mix[:, t, c * P:(c + 1) * P], ident[:])
                    mm.then_inc(self.mm.sem, 1)

            def act(self, e):
                T = self.tt * P
                for c in range(self.n):
                    self.mm.wait(e, c)
                    e.activation(self.outs[0][:, c, 0:T], ps[:, c % 4, 0:T], ACT.Copy).then_inc(self.hi.sem, 1)

            def dve(self, e):
                T = self.tt * P
                for c in range(self.n):
                    self.hi.wait(e, c)
                    e.tensor_tensor(self.outs[1][:, c, 0:T], ps[:, c % 4, 0:T],
                                    self.outs[0][:, c, 0:T].bitcast(F32), ALU.subtract).then_inc(self.out.sem, 1)

        class InProj1(Phase):
            def __init__(self, xn):
                super().__init__()
                self.xn, self.qb = xn, setup.qb
                self.base = take("slabs", 18)
                self.a, self.v = r["ev_a"].span(18), r["ev_d"].span(18)
                self.vt = r["vt"].span(5)

            def pe(self, e):
                def tile(j, k):
                    self.a.wait(e, k - 4)
                    self.v.wait(e, k - 4)
                    return dense(e, ps[:, j, :], slab(self.base + j), (xnh, xnl), TL,
                                 wait_k=(lambda k_: self.xn.wait(e, k_)) if j == 0 else None)

                def turn(c):
                    self.a.wait(e, 13 + c)
                    self.v.wait(e, 13 + c - 2)
                    for t in range(4):
                        mm = e.transpose(ps[:, 4 + c % 2, t * P:(t + 1) * P], vt1[:, c % 2, t * P:(t + 1) * P], ident[:])
                    mm.then_inc(self.vt.sem, 1)

                ring_pe(e, self.base, 8, lambda j, i, hi, lo: tile(j, BODY * i + j))
                for k in range(8, 18):
                    lo_done.wait(e, self.base + k)
                    self.a.wait(e, k - 4)
                    if k < 17:
                        self.v.wait(e, k - 4)
                    dense(e, ps[:, k % 4, :], slab(self.base + k), (xnh, xnl), TL).then_inc(used.sem, 1)
                    if k > 13:
                        turn(k - 14)
                turn(4)

            def act(self, e):
                self.qb.wait(e, 0)
                def q(j, i):
                    c = BODY * i + j
                    e.activation(q1[:, bass.ds(2 * c, 1), :].rearrange("p a t -> p (a t)"), ps[0:HD, j, :], ACT.Identity,
                                 scale=0.125, bias=qb8[0:HD, bass.ds(c, 1)]).then_inc(self.a.sem, 1)
                ring_act(e, self.base, 8, q)
                for k in range(8, 18):
                    used.wait(e, self.base + k)
                    if k < 13:
                        for s in ((0, 1) if k == 8 else (4 + 2 * (k - 9),)):
                            op = e.activation(k1[:, s, :], ps[0:HD, k % 4, :], ACT.Identity, bias=col("b_in", k)[0:HD])
                    else:
                        self.vt.wait(e, k - 13 - 2)
                        op = e.activation(vt1[:, (k - 13) % 2, :], ps[:, k % 4, :], ACT.Identity, bias=col("b_in", k))
                    op.then_inc(self.a.sem, 1)
                    split_hi(e, self.base + k + HL)

            def dve(self, e):
                self.qb.wait(e, 0)
                def q(j, i):
                    c = BODY * i + j
                    e.tensor_scalar(q1[:, bass.ds(2 * c + 1, 1), :].rearrange("p a t -> p (a t)"), ps[HD:P, j, :], 0.125,
                                    qb8[HD:P, bass.ds(c, 1)], ALU.mult, ALU.add).then_inc(self.v.sem, 1)
                ring_dve(e, self.base, 8, q)

                def values(c):
                    self.vt.wait(e, c)
                    src = ps[:, 4 + c % 2, :].rearrange("p (t c) -> p t c", c=P)
                    if c == 0:
                        for kv in range(2):
                            for dup in range(2):
                                at = (2 * kv + dup) * HD
                                op = e.tensor_copy(v1[:, :, at:at + HD], src[:, :, kv * HD:(kv + 1) * HD])
                    else:
                        at = 4 * HD + (c - 1) * P
                        op = e.tensor_copy(v1[:, :, at:at + P], src)
                    op.then_inc(self.v.sem, 1)

                for k in range(8, 18):
                    used.wait(e, self.base + k)
                    if k < 13:
                        for s in ((2, 3) if k == 8 else (5 + 2 * (k - 9),)):
                            op = e.tensor_scalar(k1[:, s, :], ps[HD:P, k % 4, :], col("b_in", k)[HD:P], None, ALU.add)
                        op.then_inc(self.v.sem, 1)
                    split_lo(e, self.base + k + HL)
                    if k > 13:
                        values(k - 14)
                values(4)

        class OutProj(Phase):
            def __init__(self, T, acts, ready, stream=None, gate=None, x_role=None):
                super().__init__()
                self.T, self.acts, self.ready, self.stream, self.gate = T, acts, ready, stream, gate
                self.base = take("slabs", KD)
                self.out = r["ev_a"].span(KD) if gate is None else r[x_role].span(KD)

            def pe(self, e):
                self.ready(e)

                def mms(j, i, hi, lo):
                    k = BODY * i + j
                    self.out.wait(e, k - 4)
                    return dense(e, ps[:, j, 0:self.T], (hi, lo), self.acts, self.T)
                if self.guest is None:
                    return ring_pe(e, self.base, KD, mms)
                for h in range(2):
                    ring_pe(e, self.base + 4 * h, 4, lambda j, i, hi, lo: mms(j, h, hi, lo))
                    self.guest.pe_stats(e, 2 * h, 2 * h + 2)

            def act(self, e):
                if self.guest is not None:
                    for h in range(2):
                        self.guest.act_squares(e, 4 * h, 4 * h + 4)
                        ring_act(e, self.base + 4 * h, 4)
                    return self.guest.act_std(e)
                if self.gate is not None:
                    return ring_act(e, self.base, KD)
                def evac(j, i):
                    n = BODY * i + j
                    e.activation(f_hm[:, bass.ds(n, 1), :].rearrange("p a t -> p (a t)"), ps[:, j, :],
                                 ACT.Identity, bias=col("b_out", n)).then_inc(self.out.sem, 1)
                ring_act(e, self.base, KD, evac)

            def dve(self, e):
                if self.gate is None:
                    return ring_dve(e, self.base, KD)
                xs, T = self.stream

                def evac(j, i):
                    n = BODY * i + j
                    xa = xs[:, bass.ds(n, 1), 0:T].rearrange("p a t -> p (a t)")
                    e.scalar_tensor_tensor(out=xa, in0=ps[:, j, 0:T], scalar=self.gate(n), in1=xa, op0=ALU.mult,
                                           op1=ALU.add).then_inc(self.out.sem, 1)
                ring_dve(e, self.base, KD, evac)
                if self.guest is not None:
                    self.guest.dve_rstd(e)

        class Embed(Phase):
            def __init__(self, xn, mods):
                super().__init__()
                self.xn, self.mods = xn, mods
                self.base = take("slabs", 10)
                self.e = r["e"].span(6)
                self.sg, self.y = r["sg"].span(KD), r["y"].span(KD)
                self.p_hi, self.p_lo = r["p_hi"].span(1), r["p_lo"].span(1)

            def pe(self, e):
                def mms(j, i, hi, lo):
                    self.sg.wait(e, BODY * i + j - 4)
                    return dense(e, ps[:, j, :], (hi, lo), (xnh, xnl), TL,
                                 wait_k=(lambda k: self.xn.wait(e, k)) if j == 0 else None)
                ring_pe(e, self.base, KD, mms)
                self.p_lo.wait(e, 0)
                for s in range(2):
                    lo_done.wait(e, self.base + KD + s)
                    for n in range(4):
                        self.sg.wait(e, 4 + n)
                        if s:
                            self.y.wait(e, n)
                        for k in range(2):
                            mm = mm3(e, ps[:, n, :], blk(slab(self.base + KD + s), 2 * n + k), (ph[:, k, :], pl[:, k, :]),
                                     k == 0, k == 1)
                        mm.then_inc(self.e.sem if n < 3 else used.sem, 1)

            def pool(self, e):
                self.mods.gain.wait(e, 3)
                for dst, src in ((cx, d["ctxT"]), (rope, d["rope"])):
                    e.dma_start(dst[:], src).then_inc(s_block2, 16)
                e.dma_start(p_raw[:], d["pT"]).then_inc(s_pload, 16)

            def act(self, e):
                def gate(j, i):
                    n = BODY * i + j
                    e.activation(sg[:, n, :], ps[:, j, :], ACT.Sigmoid).then_inc(self.sg.sem, 1)
                for h in range(2):
                    ring_act(e, self.base + 4 * h, 4, lambda j, i: gate(j, h))
                    if h == 0:
                        e.wait_ge(s_pload, 16)
                        e.activation(ph[:], p_raw[:], ACT.Copy).then_inc(self.p_hi.sem, 1)
                ring_act(e, self.base + KD, 2)

            def dve(self, e):
                ring_dve(e, self.base, 4)
                self.p_hi.wait(e, 0)
                e.tensor_tensor(pl[:], p_raw[:], ph[:].bitcast(F32), ALU.subtract).then_inc(self.p_lo.sem, 1)
                ring_dve(e, self.base + 4, 4)
                for s in range(2):
                    for n in range(4):
                        if n < 3:
                            self.e.wait(e, 3 * s + n)
                        else:
                            used.wait(e, self.base + KD + s)
                        e.tensor_tensor(f_hm[:, 4 * s + n, :], sg[:, 4 * s + n, :], ps[:, n, :], ALU.mult) \
                            .then_inc(self.y.sem, 1)
                    split_lo(e, self.base + KD + s + HL)

        class LatentIn(Phase):
            def __init__(self, T, xn, key0, rotate, full):
                super().__init__()
                self.T, self.tt, self.xn, self.key0, self.rotate, self.full = T, T // P, xn, key0, rotate, full
                self.base = take("slabs", 7 if full else 2)
                self.first = 0 if full else 5
                self.fin_hi, self.fin = r["fin_hi"].span(self.tt if full else 0), r["fin"].span(self.tt if full else 0)
                self.cq = r["cq"].span(4 if full else 1)
                self.rot, self.kr = r["rot"].span(2 if rotate else 0), r["kr"].span(1)
                self.spread = take("krope", 1)

            def cq_ready(self, e, c):
                self.cq.wait(e, c if self.full else 0)

            def pe(self, e):
                T, acts = self.T, (xnh, xnl)
                by_k = lambda kb: self.xn.wait(e, kb)
                for k in range(self.first, 7):
                    s = self.base + k - self.first
                    lo_done.wait(e, s)
                    w = slab(s)
                    if k < 2:
                        for kb in range(4):
                            by_k(4 * k + kb)
                            for t in range(self.tt):
                                mm = mm3(e, ps[:, t, 0:256], tuple(a[:, 4 * k + kb, t * P:(t + 1) * P] for a in acts),
                                         blk(w, kb, 256), k == 0 and kb == 0, k == 1 and kb == 3)
                    elif k < 6:
                        mm = dense(e, ps[:, (5, 6, 7, 4)[k - 2], 0:T], w, acts, T, wait_k=by_k if k == 5 else None)
                    else:
                        if self.full:
                            self.fin.wait(e, 0)
                        mm = dense(e, ps[:, 0, 0:T], w, acts, T)
                    mm.then_inc(used.sem, 1)

            def act(self, e):
                T = self.T
                for k in range(self.first, 7):
                    s = self.base + k - self.first
                    used.wait(e, s)
                    if k == 1:
                        for t in range(self.tt):
                            e.activation(finh[:, t, :], ps[:, t, 0:256], ACT.Copy).then_inc(self.fin_hi.sem, 1)
                    if 2 <= k < 6:
                        e.activation(cq[:, k - 2, 0:T], ps[:, (5, 6, 7, 4)[k - 2], 0:T], ACT.Copy).then_inc(self.cq.sem, 1)
                    split_hi(e, s + HL)

            def dve(self, e):
                T = self.T
                for k in range(self.first, 7):
                    s = self.base + k - self.first
                    used.wait(e, s)
                    if k == 1:
                        for t in range(self.tt):
                            self.fin_hi.wait(e, t)
                            e.tensor_tensor(finl[:, t, :], ps[:, t, 0:256], finh[:, t, :].bitcast(F32),
                                            ALU.subtract).then_inc(self.fin.sem, 1)
                    split_lo(e, s + HL)
                out = k2[64:96, 0, self.key0:self.key0 + T]
                if self.rotate:
                    rotary(e, out, 0, 0, T, self.rot)
                    rotary_add(e, out, 0, T, self.rot, 0, self.kr)
                else:
                    e.tensor_copy(out, ps[64:96, 0, 0:T]).then_inc(self.kr.sem, 1)

            def pool(self, e):
                self.kr.wait(e, 0)
                src = k2[64:96, 0:1, self.key0:self.key0 + self.T].broadcast_to([32, MLA_H - 1, self.T])
                e.dma_start(k2[64:96, 1:MLA_H, self.key0:self.key0 + self.T], src).then_inc(s_krope, 16)

        def rotary(e, out, bank, slot, T, rot):
            e.tensor_tensor(rt2[64:96, slot, 0:T], ps[96:128, bank, 0:T], rope[96:128, 0:T], ALU.mult).then_inc(rot.sem, 1)
            e.tensor_tensor(out, ps[64:96, bank, 0:T], rope[64:96, 0:T], ALU.mult).then_inc(rot.sem, 1)

        def rotary_add(e, out, slot, T, rot, n, done):
            rot.wait(e, n + 1)
            e.tensor_tensor(out, out, rt2[64:96, slot, 0:T], ALU.add).then_inc(done.sem, 1)

        class Fourier(Phase):
            def __init__(self, l, T, inp, nq, nkv):
                super().__init__()
                self.l, self.T, self.tt, self.inp, self.nq, self.nkv = l, T, T // P, inp, nq, nkv
                self.nd = 2 * self.tt * T // SLAB
                self.base = take("slabs", self.nd + 1)
                self.pq_hi, self.pq = r["pq_hi"].span(4), r["pq"].span(4)
                self.f_mm, self.f_hi, self.f = r["f_mm"].span(1), r["f_hi"].span(2), r["f"].span(2)
                self.four_hi, self.four = r["four_hi"].span(2), r["four"].span(2)

            def pe(self, e):
                T, tt = self.T, self.tt
                self.inp.fin.wait(e, tt - 1)
                self.inp.kr.wait(e, 0)
                for s in range(self.nd):
                    lo_done.wait(e, self.base + s)
                    w = slab(self.base + s)
                    for g in range(SLAB // T):
                        m, tb = divmod(s * (SLAB // T) + g, tt)
                        for c in range(2):
                            mm = mm3(e, ps[:, 2 * m + c, 0:T], tuple(f[:, tb, c * P:(c + 1) * P] for f in (finh, finl)),
                                     blk(w, g, T), tb == 0, tb == tt - 1)
                    mm.then_inc(used.sem, 1)
                self.inp.cq_ready(e, 3)
                self.nq.pe_stats(e)
                self.nkv.pe_stats(e)
                s = self.base + self.nd
                lo_done.wait(e, s)
                w = slab(s)
                self.pq.wait(e, 3)
                for c in range(2):
                    for m in range(2):
                        mm = mm3(e, ps[:, 5 + c, 0:T], blk(w, m), tuple(a[:, 2 * m + c, 0:T] for a in (pqh, pql)),
                                 m == 0, m == 1)
                mm.then_inc(self.f_mm.sem, 1)
                self.f.wait(e, 1)
                for n in range(2):
                    for k in range(2):
                        mm = mm3(e, ps[:, n, 0:T], blk(w, 2 + 2 * k + n), tuple(a[:, k, 0:T] for a in (fh, fl)),
                                 k == 0, k == 1)
                mm.then_inc(used.sem, 1)

            def act(self, e):
                T = self.T
                self.nq.act_squares(e)
                self.nkv.act_squares(e)
                for s in range(self.nd):
                    used.wait(e, self.base + s)
                    split_hi(e, self.base + s + HL)
                for c in range(4):
                    e.activation(pqh[:, c, 0:T], ps[:, c, 0:T], ACT.Copy).then_inc(self.pq_hi.sem, 1)
                self.nq.act_std(e)
                self.nkv.act_std(e)
                self.f_mm.wait(e, 0)
                for c in range(2):
                    e.activation(fh[:, c, 0:T], ps[:, 5 + c, 0:T], ACT.Copy).then_inc(self.f_hi.sem, 1)
                self.nq.act_hi(e)
                self.nkv.act_hi(e)
                used.wait(e, self.base + self.nd)
                for n in range(2):
                    e.activation(xnh[:, n, 0:T], ps[:, n, 0:T], ACT.Identity, bias=col(f"b_f{self.l}", n)) \
                        .then_inc(self.four_hi.sem, 1)
                split_hi(e, self.base + self.nd + HL)

            def pool(self, e):
                self.nq.pool_adds(e)
                self.nkv.pool_adds(e)

            def dve(self, e):
                T = self.T
                for s in range(self.nd):
                    used.wait(e, self.base + s)
                    split_lo(e, self.base + s + HL)
                for c in range(4):
                    self.pq_hi.wait(e, c)
                    e.tensor_tensor(pql[:, c, 0:T], ps[:, c, 0:T], pqh[:, c, 0:T].bitcast(F32),
                                    ALU.subtract).then_inc(self.pq.sem, 1)
                self.nq.dve_rstd(e)
                self.nkv.dve_rstd(e)
                for c in range(2):
                    self.f_hi.wait(e, c)
                    e.tensor_tensor(fl[:, c, 0:T], ps[:, 5 + c, 0:T], fh[:, c, 0:T].bitcast(F32),
                                    ALU.subtract).then_inc(self.f.sem, 1)
                self.nq.dve_tiles(e)
                self.nkv.dve_tiles(e)
                for n in range(2):
                    self.four_hi.wait(e, n)
                    e.scalar_tensor_tensor(out=xnl[:, n, 0:T], in0=ps[:, n, 0:T], scalar=col(f"b_f{self.l}", n),
                                           in1=xnh[:, n, 0:T].bitcast(F32), op0=ALU.add,
                                           op1=ALU.subtract).then_inc(self.four.sem, 1)
                split_lo(e, self.base + self.nd + HL)

        class NormOnly(Phase):
            def __init__(self, norm):
                super().__init__()
                self.norm = norm

            def act(self, e):
                self.norm.act_squares(e)
                self.norm.act_std(e)
                self.norm.act_hi(e)

            def pe(self, e):
                self.norm.pe_stats(e)

            def dve(self, e):
                self.norm.dve_rstd(e)
                self.norm.dve_tiles(e)

        class QProj(Phase):
            def __init__(self, T, norm, rotate, four):
                super().__init__()
                self.T, self.norm, self.rotate, self.four = T, norm, rotate, four
                self.base = take("slabs", MLA_H // 2)
                self.a = r["ev_a"].span(MLA_H)
                self.v = r["q_add"].span(MLA_H if rotate else 0)
                self.rot = r["rot"].span(2 * MLA_H if rotate else 0)

            def pe(self, e):
                T = self.T
                self.norm.out.wait(e, 2)
                self.four.four.wait(e, 1)
                for s in range(MLA_H // 2):
                    lo_done.wait(e, self.base + s)
                    for hh in range(2):
                        h = 2 * s + hh
                        if h >= 4:
                            self.a.wait(e, h - 4)
                            if self.rotate:
                                self.rot.wait(e, 2 * (h - 4) + 1)
                        for k in range(3):
                            mm = mm3(e, ps[:, h % 4, 0:T], blk(slab(self.base + s), 3 * hh + k),
                                     (cnh[:, k, 0:T], cnl[:, k, 0:T]), k == 0, k == 2)
                    mm.then_inc(used.sem, 1)

            def act(self, e):
                T = self.T
                n = NOPE if self.rotate else NOPE + ROPE
                for s in range(MLA_H // 2):
                    used.wait(e, self.base + s)
                    for h in (2 * s, 2 * s + 1):
                        e.activation(q2[0:n, h, 0:T], ps[0:n, h % 4, 0:T], ACT.Copy).then_inc(self.a.sem, 1)
                    split_hi(e, self.base + s + HL)

            def dve(self, e):
                T = self.T
                for s in range(MLA_H // 2):
                    used.wait(e, self.base + s)
                    if self.rotate:
                        for h in (2 * s, 2 * s + 1):
                            if h >= 2:
                                self.v.wait(e, h - 2)
                            rotary(e, q2[64:96, h, 0:T], h % 4, h % 2, T, self.rot)
                    split_lo(e, self.base + s + HL)

            def pool(self, e):
                for h in range(MLA_H if self.rotate else 0):
                    rotary_add(e, q2[64:96, h, 0:self.T], h % 2, self.T, self.rot, 2 * h, self.v)

        class KVProj(Phase):
            def __init__(self, T, norm, key0, after=None):
                super().__init__()
                self.T, self.tt, self.norm, self.key0, self.after = T, T // P, norm, key0, after
                self.base = take("slabs", 2)
                n = MLA_H // 2 + self.tt
                self.vt = r["vt"].span(self.tt)
                self.a, self.v = r["ev_a"].span(n), r["ev_d"].span(n)

            def pe(self, e):
                T = self.T
                self.norm.out.wait(e, 0)
                if self.after is not None:
                    self.after.a.wait(e, MLA_H - 1)
                    if self.after.rotate:
                        self.after.rot.wait(e, 2 * MLA_H - 1)
                lo_done.wait(e, self.base)
                for p_ in range(MLA_H // 2):
                    if p_ >= 4:
                        self.a.wait(e, p_ - 4)
                        self.v.wait(e, p_ - 4)
                    mm = mm3(e, ps[:, p_ % 4, 0:T], blk(slab(self.base), p_), (cnh[:, 3, 0:T], cnl[:, 3, 0:T]), True, True)
                    if p_ == 3:
                        mm.then_inc(self.vt.sem, 1)
                mm.then_inc(used.sem, 1)
                if self.guest is not None:
                    self.guest.pe_stats(e, 0, 2)
                lo_done.wait(e, self.base + 1)
                w = slab(self.base + 1)
                for t in range(self.tt):
                    last = MLA_H // 2 + t - 2 if t >= 2 else (5 if t == 0 else 3)
                    self.a.wait(e, last)
                    self.v.wait(e, last)
                    act = tuple(c[:, 3, t * P:(t + 1) * P] for c in (cnh, cnl))
                    mm3(e, ps[:, 2 * (t % 2), :], act, tuple(a[:, 0:512] for a in w), True, True)
                    mm = mm3(e, ps[:, 2 * (t % 2) + 1, 0:256], act, tuple(a[:, 512:768] for a in w), True, True)
                    mm.then_inc(self.vt.sem if t < self.tt - 1 else used.sem, 1)
                if self.guest is not None:
                    self.guest.pe_stats(e, 2)

            def act(self, e):
                T, k0 = self.T, self.key0
                if self.guest is not None:
                    self.guest.act_squares(e, 0, 4)
                for p_ in range(MLA_H // 2):
                    if p_ == 0:
                        self.vt.wait(e, 0)
                    if p_ == 4:
                        used.wait(e, self.base)
                    e.activation(k2[0:HD, 2 * p_, k0:k0 + T], ps[0:HD, p_ % 4, 0:T], ACT.Copy).then_inc(self.a.sem, 1)
                split_hi(e, self.base + HL)
                for t in range(self.tt):
                    self.tile_ready(e, t)
                    e.activation(v2[:, k0 // P + t, 0:512], ps[:, 2 * (t % 2), :], ACT.Copy).then_inc(self.a.sem, 1)
                split_hi(e, self.base + 1 + HL)
                if self.guest is not None:
                    self.guest.act_squares(e, 4)
                    self.guest.act_std(e)

            def tile_ready(self, e, t):
                if t < self.tt - 1:
                    self.vt.wait(e, t + 1)
                else:
                    used.wait(e, self.base + 1)

            def dve(self, e):
                T, k0 = self.T, self.key0
                for p_ in range(MLA_H // 2):
                    if p_ == 0:
                        self.vt.wait(e, 0)
                    if p_ == 4:
                        used.wait(e, self.base)
                    e.tensor_copy(k2[0:HD, 2 * p_ + 1, k0:k0 + T], ps[HD:P, p_ % 4, 0:T]).then_inc(self.v.sem, 1)
                split_lo(e, self.base + HL)
                for t in range(self.tt):
                    self.tile_ready(e, t)
                    e.tensor_copy(v2[:, k0 // P + t, 512:768], ps[:, 2 * (t % 2) + 1, 0:256]).then_inc(self.v.sem, 1)
                split_lo(e, self.base + 1 + HL)
                if self.guest is not None:
                    self.guest.dve_rstd(e)

        class Final(Phase):
            def __init__(self, ready):
                super().__init__()
                self.norm = Norm([x[:, n, :] for n in range(KD)], ready, TL, D, nt, lambda n: col("g_final", n),
                                 plain=yout)

            def act(self, e):
                self.norm.act_squares(e)
                self.norm.act_std(e)
                for n in range(KD):
                    self.norm.out.wait(e, n)
                    e.dma_start(d["out"][:, n, :], yout[:, n, :]).then_inc(s_out, 16)
                e.wait_ge(s_out, 16 * KD)

            def pool(self, e):
                self.norm.pool_adds(e)

            def pe(self, e):
                self.norm.pe_stats(e)

            def dve(self, e):
                self.norm.dve_rstd(e)
                self.norm.dve_plain(e)

        def latent_mixer(l, st, x_ready, std_free=lambda e: None, host=None, whole=False):
            T, xs, key0 = ((TL, x, 0), (TC, cx, TL))[st]
            full = st == 0 or l == 0
            pre = PreNorm((xs, T), x_ready, lambda n: gains[:, l, st, 0, n:n + 1], lambda n: mod[:, l, n, st:st + 1],
                          None, std_free, host, whole)
            inp = LatentIn(T, pre.out, key0, st == 0, full)
            zero = lambda n: col("zero", n)
            nkv = lambda: Norm([cq[:, 3, 0:T]], lambda e, n: inp.cq_ready(e, 3), T, P, nt2, lambda n: col(f"g_kv{l}", n),
                               zero, (cnh[:, 3:4, :], cnl[:, 3:4, :]), bank=7)
            if full:
                nq = Norm([cq[:, c, 0:T] for c in range(3)], lambda e, n: inp.cq_ready(e, n), T, 3 * P, nt,
                          lambda n: col(f"g_q{l}", n), zero, (cnh, cnl))
                nk = nkv()
                four = Fourier(l, T, inp, nq, nk)
                qp = QProj(T, nq, st == 0, four)
            else:
                nk = nkv()
                NormOnly(nk)
                qp = None
            kv = KVProj(T, nk, key0, qp)
            if not full:
                return kv
            spread = inp.spread + 1

            def q_ready(e):
                qp.a.wait(e, MLA_H - 1)
                if qp.rotate:
                    qp.v.wait(e, MLA_H - 1)

            def ready(e):
                q_ready(e)
                kv.a.wait(e, MLA_H // 2 + kv.tt - 1)
                kv.v.wait(e, MLA_H // 2 + kv.tt - 1)
                e.wait_ge(s_krope, 16 * spread)
            keys = (lambda qt: list(range(6))) if st == 0 else (lambda qt: [0, 1])
            att = Attention(MLA_H, T // P, keys, q2, k2, v2, qst2, p2, pt2, mix2, 96, MLA_SCALE, ready,
                            kslot=lambda b, par: 2 * b + par, key0=0 if st == 0 else TL, vt0=0 if st == 0 else 4,
                            dsplit=512 if st == 0 else 0, q_ready=q_ready)
            turn = MixTurn(mix2, 6, T // P, (m2h, m2l), lambda e: att.o.wait(e, MLA_H - 1))

            def mixed(e):
                four.four.wait(e, 1)
                turn.out.wait(e, 5)
            role_x = ("x", "cx")[st]
            acts = [(xnh[:, k, 0:T], xnl[:, k, 0:T]) for k in range(2)] + \
                [(m2h[:, k, 0:T], m2l[:, k, 0:T]) for k in range(6)]
            out = OutProj(T, acts, mixed, (xs, T), lambda n: mod[:, l, bass.ds(16 + n, 1), st],
                          role_x)
            return out

        def latent_ffn(l, st, x_done, host=None, whole=False):
            T, xs = ((TL, x), (TC, cx))[st]
            pre = PreNorm((xs, T), lambda e, n: x_done.wait(e, n), lambda n: gains[:, l, st, 1, n:n + 1],
                          lambda n: mod[:, l, 24 + n, st:st + 1],
                          None, lambda e: None, host, whole)
            gu = GateUp(T, pre.out, conv=l)
            down = Down(T, gu, (xs, T), lambda n: mod[:, l, 40 + n, st:st + 1], ("x", "cx")[st])
            return down

        setup = Setup()
        tables_view = d["tables"]
        strips_view = bass.AP(tables_view.tensor, 0, [[NTAB, 16], [1, P], [1, TL]])
        after = lambda sp: (lambda e, n: sp.wait(e, n))

        post, gu1 = ffn_block1(0, "ffn1_pre_g", "ffn1_post_g", lambda e, n: e.wait_ge(x_full[n // 2], 16), None)
        first_pre = gu1.pre
        setup.first = first_pre.norm
        pre = PreNorm((x, TL), after(post.out), lambda n: col("attn_pre_g", n), lambda n: col("zero", n), post)
        proj = InProj1(pre.out)

        def q_ready(e):
            proj.a.wait(e, 7)
            proj.v.wait(e, 7)

        def qkv_ready(e):
            proj.a.wait(e, 12)
            proj.v.wait(e, 17)
        att_a = Attention(8, 4, lambda qt: [qt - 1, qt] if qt else [0], q1, k1, v1, qst1, p1, pt1, mix1, HD, 1.0,
                          qkv_ready, kslot=lambda b, par: b, bias=True, q_ready=q_ready)
        att_b = Attention(8, 4, lambda qt: list(range(qt + 1)), q1, k1, v1, qst1, p1, pt1, mix1, HD, 1.0,
                          qkv_ready, q0=8, kslot=lambda b, par: 4 + 2 * b + par, mix0=512, bias=True, head0=8,
                          q_ready=q_ready)
        turn1 = MixTurn(mix1, 8, 4, (m1h, m1l), lambda e: att_b.o.wait(e, 7))
        outp = OutProj(TL, (m1h, m1l), lambda e: turn1.out.wait(e, 7))
        f_tiles = [f_hm[:, n, :] for n in range(KD)]
        post = PostNorm(f_tiles, after(outp.out), pn_hm, lambda n: col("attn_post_g", n), False)

        post, gu2 = ffn_block1(1, "ffn2_pre_g", "ffn2_post_g", after(post.out), post)
        pre = PreNorm((x, TL), after(post.out), lambda n: col("ple_pre_g", n), lambda n: col("zero", n), post)
        emb = Embed(pre.out, gu2.mods)
        post = PostNorm(f_tiles, after(emb.y), pn_hm, lambda n: col("ple_post_g", n), False)

        c_mix = latent_mixer(0, 1, lambda e, n: e.wait_ge(s_block2, 32), lambda e: post.out.wait(e, KD - 1))
        x_mix = latent_mixer(0, 0, after(post.out), host=c_mix)
        c_ffn = latent_ffn(0, 1, c_mix.out, host=x_mix)
        x_ffn = latent_ffn(0, 0, x_mix.out, host=c_ffn, whole=True)
        c_kv = latent_mixer(1, 1, after(c_ffn.out), host=x_ffn, whole=True)
        x_mix = latent_mixer(1, 0, after(x_ffn.out), host=c_kv)
        x_last = latent_ffn(1, 0, x_mix.out)
        Final(after(x_last.out))
        assert count["ada"] == 2 * NMOD, count
        take("slabs", HL)
        assert count["slabs"] == d["n_slabs"], count

        block = ctx.enter_context(nc.Block())

        @block.sync
        def _(e):
            at = 0

            def main(n):
                nonlocal at
                b = at
                units(e, n, BODY, lambda j, i: load(e, b + j, i))
                at += n

            def ada_load(m, a, slot):
                m.acc.wait(e, 2 * a - 3)
                e.dma_start(ada[:, slot, :], d["wa"][bass.ds(m.first + a, 1)].rearrange("a p n -> (a p) n")) \
                    .then_inc(ada_full[slot], 16)

            for c in range(2, 4):
                load_x(e, c)
            for g in (gu1, gu2):
                main(g.base + RAW - at)
                ada_load(g.mods, 0, 0)
                ada_load(g.mods, 1, 1)
                main(HL)

                def both(j, i):
                    load(e, g.base + RAW + HL + j, i)
                    ada_load(g.mods, BODY * i + j + 2, j % 2)
                units(e, NMOD - 2, BODY, both)
                at += NMOD - 2
            main(count["slabs"] - at)

        @block.tensor
        def _(e):
            for ph_ in phases:
                ph_.pe(e)

        @block.scalar
        def _(e):
            for ph_ in phases:
                ph_.act(e)

        @block.vector
        def _(e):
            for ph_ in phases:
                ph_.dve(e)

        @block.gpsimd
        def _(e):
            for ph_ in phases:
                ph_.pool(e)


def slabs_by_column(w):
    k, n = w.shape
    return w.reshape(k // P, P, n // P, P).transpose(2, 1, 0, 3).reshape(n // P, P, -1)


def gate_up_slabs(w):
    s = slabs_by_column(w)
    return np.stack([s[:KF], s[KF:]], axis=1).reshape(2 * KF, P, SLAB)


def down_slabs(w):
    a = w.reshape(KF // 2, 2, P, 2, 4 * P)
    return a.transpose(3, 0, 2, 1, 4).reshape(KF, P, SLAB)


def pad(a):
    return np.concatenate([a, np.zeros((P, SLAB - a.shape[1]), a.dtype)], axis=1)[None]


def latent_slabs(i, l, st, full):
    T = (TL, TC)[st]
    w = i["w_in_2"][l]
    out = []
    kr = w[:, 768:800]
    swapped = np.concatenate([kr[:, 16:], kr[:, :16]], axis=1)
    kr = slabs_by_column(np.concatenate([kr, swapped, kr, swapped], axis=1))
    if full:
        out.append(w[:, :256].reshape(2, 4, P, 256).transpose(0, 2, 1, 3).reshape(2, P, SLAB))
        out.append(slabs_by_column(w[:, 256:640]))
    out += [slabs_by_column(w[:, 640:768]), kr]
    if full:
        out.append(dft_slabs(T))
        wf = i["w_fourier_2"][l].reshape(2, P, 2, P).transpose(1, 0, 2, 3).reshape(P, 512)
        out.append(pad(np.concatenate([*channel_dft(T), wf], axis=1)))
        q = i["w_q_b_2"][l].reshape(3, P, MLA_H, 96)
        q = np.concatenate([q, q[..., 80:], q[..., 64:80]], axis=3)
        for s in range(MLA_H // 2):
            out.append(pad(q[:, :, 2 * s:2 * s + 2].transpose(1, 2, 0, 3).reshape(P, 768)))
    kv = i["w_kv_b_2"][l].reshape(P, MLA_H, 2, HD)
    out += [pad(kv[:, :, 0].reshape(P, 768)), pad(kv[:, :, 1].reshape(P, 768))]
    if full:
        out.append(slabs_by_column(i["w_out_2"][l]))
    return out


def weight_stream(i):
    a_kv, b0 = 512, 768
    w = i["w_in"][0]
    out = [gate_up_slabs(i["ffn1_w_gu"][0]), down_slabs(i["ffn1_w_down"][0])]
    order = [w[:, 0:512], w[:, b0:b0 + 512], w[:, a_kv:a_kv + 128], w[:, b0 + 512:b0 + 1024], w[:, a_kv + 128:b0],
             w[:, b0 + 1024:]]
    out += [slabs_by_column(np.concatenate(order, axis=1)), slabs_by_column(i["w_out"][0])]
    out += [gate_up_slabs(i["ffn2_w_gu"][0]), down_slabs(i["ffn2_w_down"][0])]
    proj = i["w_ple_proj"][0].reshape(2, P, 2, 4, P).transpose(2, 1, 3, 0, 4).reshape(2, P, SLAB)
    out += [slabs_by_column(i["w_ple_gate"][0]), proj]
    ffn = lambda l: [gate_up_slabs(i["w_up_2"][l]), down_slabs(i["w_down_2"][l])]
    out += latent_slabs(i, 0, 1, True) + latent_slabs(i, 0, 0, True) + ffn(0) + ffn(0)
    out += latent_slabs(i, 1, 1, False) + latent_slabs(i, 1, 0, True) + ffn(1)
    out.append(np.zeros((HL, P, SLAB), np.float32))
    return np.concatenate(out)


def column_table(i):
    t = np.zeros((P, COLS.n), np.float32)

    def put(name, v):
        c = COLS.at[name]
        t[:, c:c + v.size // P] = v.reshape(-1, P).T
    for n in ("ffn1_pre_g", "ffn1_post_g", "attn_pre_g", "b_out", "attn_post_g", "ffn2_pre_g", "ffn2_post_g",
              "ple_pre_g", "ple_post_g"):
        put(n, i[n][0])
    put("g_final", i["g_final_2"])
    b = i["b_in"][0]
    put("b_in", np.concatenate([b[0:512], b[768:1280], b[512:640], b[1280:1792], b[640:768], b[1792:]]))
    for l in range(2):
        for n, v in (("b_ada", "b_ada_2"), ("g_mix", "g_mix_2"), ("b_f", "b_fourier_2"), ("g_q", "g_q_a_2"),
                     ("g_kv", "g_kv_a_2"), ("g_ffn", "g_ffn_2"), ("b_dw", "b_dw_2")):
            put(f"{n}{l}", i[v][l])
        for k in range(3):
            put(f"w_dw{k}{l}", i["w_dw_2"][l, k])
    return t


def feature_major(a):
    return a.T.reshape(-1, P, a.shape[0]).transpose(1, 0, 2)


def kernel(**inputs):
    import concourse.bacc as bacc
    from concourse.bass_utils import run_bass_kernel_spmd

    i = {k: np.asarray(v) for k, v in inputs.items()}
    arrays = {
        "ws": weight_stream(i),
        "wa": i["w_ada_2"].transpose(0, 2, 1).reshape(2 * NMOD, P, D),
        "cols": column_table(i),
        "xT": feature_major(i["x"][0]),
        "ctxT": feature_major(i["ctx_2"][0]),
        "pT": feature_major(i["p"][0, 0]),
        "c": np.stack([i["c_2"][0], i["c_ctx_2"]]),
        "rel_bias": i["rel_bias"],
        "sinks": i["sinks"][0],
        "no_sinks": np.full(8, NEG, np.float32),
        "onehot": bucket_tables(),
        "ident": np.eye(P, dtype=np.float32),
        "flip": np.eye(P, dtype=np.float32)[::-1],
        "rope": rope_table(),
    }
    arrays = {f"in_{k}_dram": np.ascontiguousarray(v) for k, v in arrays.items()}
    nc = bacc.Bacc("TRN2", target_bir_lowering=False, num_devices=1)
    d = {k[3:-5]: nc.dram_tensor(k, v.shape, mybir.dt.from_np(v.dtype), kind="ExternalInput").ap()
         for k, v in arrays.items()}
    d["n_slabs"] = arrays["in_ws_dram"].shape[0]
    d["tables"] = nc.dram_tensor("tables", (2, 8, NTAB), F32).ap()
    d["out"] = nc.dram_tensor("out_0_dram", (P, KD, TL), F32, kind="ExternalOutput").ap()
    build(nc, d)
    res = run_bass_kernel_spmd(nc, [arrays], core_ids=[0])
    out = res.results[0]["out_0_dram"]
    return np.ascontiguousarray(out.transpose(1, 0, 2).reshape(D, TL).T)[None]
```
